# Optimizing a Trainium2 kernel written in Bass

```python
import math
import jax, jax.numpy as jnp
from jax import lax
import numpy as np

D_MODEL = 1024
BATCH = 1
SEQ = 256
DEPTH = 2

GLA_HEADS = 4
GLA_DK = 64
GLA_DV = 128
GLA_KEY = GLA_HEADS * GLA_DK
GLA_VAL = GLA_HEADS * GLA_DV
GATE_RANK = 16
GATE_NORMALIZER = 16.0
CHUNK = 64
CONV_CH = 512
CONV_WIDTH = 31
MIX_WIDTH = GLA_VAL + CONV_CH
IN_COLS = 2 * GLA_KEY + 2 * GLA_VAL + GATE_RANK + 2 * CONV_CH
D_FF = 2816
N_EXPERTS = 8
TOP_K = 2
N_DENSE = (DEPTH + 1) // 2
N_MOE = DEPTH // 2
EPS = 1e-6

kernel_name = "hybrid_gla_conformer_moe_trunk"

def rmsnorm(x, w):
    xf = x.astype(jnp.float32)
    y = xf * lax.rsqrt(jnp.mean(xf * xf, axis=-1, keepdims=True) + EPS)
    return (y * w.astype(jnp.float32)).astype(x.dtype)

def layernorm(x, w, b):
    xf = x.astype(jnp.float32)
    mu = jnp.mean(xf, axis=-1, keepdims=True)
    var = jnp.mean(jnp.square(xf - mu), axis=-1, keepdims=True)
    y = (xf - mu) * lax.rsqrt(var + EPS)
    return (y * w.astype(jnp.float32) + b.astype(jnp.float32)).astype(x.dtype)

def gla_chunked(q, k, v, log_a):
    B, H, T, DK = q.shape
    DV = v.shape[-1]
    N = T // CHUNK

    def to_chunks(a):
        return a.astype(jnp.float32).reshape(B, H, N, CHUNK, a.shape[-1]).transpose(2, 0, 1, 3, 4)

    qc, kc, vc, ac = to_chunks(q), to_chunks(k), to_chunks(v), to_chunks(log_a)
    bc = jnp.cumsum(ac, axis=3)
    mask = jnp.tril(jnp.ones((CHUNK, CHUNK), dtype=bool))

    def step(S, inp):
        qi, ki, vi, bi = inp
        diff = bi[:, :, :, None, :] - bi[:, :, None, :, :]
        decay = jnp.exp(jnp.where(mask[:, :, None], diff, -jnp.inf))
        attn = jnp.einsum('bhid,bhjd,bhijd->bhij', qi, ki, decay)
        o_intra = jnp.einsum('bhij,bhjv->bhiv', attn, vi)
        o_inter = jnp.einsum('bhid,bhdv->bhiv', qi * jnp.exp(bi), S)
        b_last = bi[:, :, -1:, :]
        S_new = jnp.exp(b_last[:, :, 0, :])[..., None] * S + jnp.einsum(
            'bhjd,bhjv->bhdv', ki * jnp.exp(b_last - bi), vi)
        return S_new, o_intra + o_inter

    S0 = jnp.zeros((B, H, DK, DV), jnp.float32)
    _, ys = lax.scan(step, S0, (qc, kc, vc, bc))
    return ys.transpose(1, 2, 0, 3, 4).reshape(B, H, T, DV)

def causal_dwconv(u, w, b):
    kern = w[:, None, :].astype(u.dtype)
    y = lax.conv_general_dilated(u, kern, window_strides=(1,), padding=[(CONV_WIDTH - 1, 0)],
                                 dimension_numbers=('NWC', 'WIO', 'NWC'), feature_group_count=CONV_CH)
    return y + b.astype(u.dtype)

def swiglu(h, wg, wu, wd):
    return (jax.nn.silu(h @ wg) * (h @ wu)) @ wd

def token_mixer(h, w_in, w_gate_up, b_gate, gla_norm_w, conv_w, conv_b, cn_w, cn_b, w_out):
    B, T, _ = h.shape
    z = h @ w_in
    sizes = [GLA_KEY, GLA_KEY, GLA_VAL, GLA_VAL, GATE_RANK, CONV_CH, CONV_CH]
    offs = np.cumsum([0] + sizes)
    q, k, v, g, gr, ca, cb = [z[..., offs[i]:offs[i + 1]] for i in range(len(sizes))]

    gate_logit = (gr @ w_gate_up + b_gate).astype(jnp.float32)
    log_a = jax.nn.log_sigmoid(gate_logit) / GATE_NORMALIZER

    def heads(a, d):
        return a.reshape(B, T, GLA_HEADS, d).transpose(0, 2, 1, 3)

    o = gla_chunked(heads(q, GLA_DK) * (GLA_DK ** -0.5), heads(k, GLA_DK), heads(v, GLA_DV),
                    heads(log_a, GLA_DK))
    o = o.transpose(0, 2, 1, 3).astype(h.dtype)
    o = rmsnorm(o, gla_norm_w)
    o = (o * jax.nn.silu(g.reshape(B, T, GLA_HEADS, GLA_DV))).reshape(B, T, GLA_VAL)

    u = ca * jax.nn.sigmoid(cb)
    u = causal_dwconv(u, conv_w, conv_b)
    u = jax.nn.silu(layernorm(u, cn_w, cn_b))

    return jnp.concatenate([o, u], axis=-1) @ w_out

def moe_swiglu(h, w_router, we_gate, we_up, we_down):
    B, T, D = h.shape
    hf = h.reshape(B * T, D)
    logits = (hf @ w_router).astype(jnp.float32)
    top_v, top_i = lax.top_k(logits, TOP_K)
    gates = jax.nn.softmax(top_v, axis=-1)
    comb = jnp.sum(jax.nn.one_hot(top_i, N_EXPERTS, dtype=jnp.float32) * gates[..., None], axis=1)
    comb = comb.astype(h.dtype)
    y = jnp.zeros_like(hf)
    for e in range(N_EXPERTS):
        y = y + comb[:, e:e + 1] * swiglu(hf, we_gate[e], we_up[e], we_down[e])
    return y.reshape(B, T, D)

def setup_inputs(seed: int = 0) -> dict:
    key = jax.random.key(seed)
    ks = jax.random.split(key, 24)
    f32 = jnp.float32
    nrm = lambda k, s, sc: jax.random.normal(k, s, f32) * sc
    D = D_MODEL
    return {
        "x": jax.random.normal(ks[0], (BATCH, SEQ, D), f32),
        "ln1_w": 1.0 + nrm(ks[1], (DEPTH, D), 0.02),
        "w_in": nrm(ks[2], (DEPTH, D, IN_COLS), D ** -0.5),
        "w_gate_up": nrm(ks[3], (DEPTH, GATE_RANK, GLA_KEY), GATE_RANK ** -0.5),
        "b_gate": nrm(ks[4], (DEPTH, GLA_KEY), 0.1),
        "gla_norm_w": 1.0 + nrm(ks[5], (DEPTH, GLA_DV), 0.02),
        "conv_w": nrm(ks[6], (DEPTH, CONV_WIDTH, CONV_CH), CONV_WIDTH ** -0.5),
        "conv_b": nrm(ks[7], (DEPTH, CONV_CH), 0.02),
        "cn_w": 1.0 + nrm(ks[8], (DEPTH, CONV_CH), 0.02),
        "cn_b": nrm(ks[9], (DEPTH, CONV_CH), 0.02),
        "w_out": nrm(ks[10], (DEPTH, MIX_WIDTH, D), MIX_WIDTH ** -0.5),
        "ln2_w": 1.0 + nrm(ks[11], (DEPTH, D), 0.02),
        "wd_gate": nrm(ks[12], (N_DENSE, D, D_FF), D ** -0.5),
        "wd_up": nrm(ks[13], (N_DENSE, D, D_FF), D ** -0.5),
        "wd_down": nrm(ks[14], (N_DENSE, D_FF, D), D_FF ** -0.5),
        "w_router": nrm(ks[15], (N_MOE, D, N_EXPERTS), D ** -0.5),
        "we_gate": nrm(ks[16], (N_MOE, N_EXPERTS, D, D_FF), D ** -0.5),
        "we_up": nrm(ks[17], (N_MOE, N_EXPERTS, D, D_FF), D ** -0.5),
        "we_down": nrm(ks[18], (N_MOE, N_EXPERTS, D_FF, D), D_FF ** -0.5),
        "final_norm_w": 1.0 + nrm(ks[19], (D,), 0.02),
    }

def reference(x, ln1_w, w_in, w_gate_up, b_gate, gla_norm_w, conv_w, conv_b, cn_w, cn_b, w_out,
              ln2_w, wd_gate, wd_up, wd_down, w_router, we_gate, we_up, we_down, final_norm_w):
    for l in range(DEPTH):
        h = rmsnorm(x, ln1_w[l])
        x = x + token_mixer(h, w_in[l], w_gate_up[l], b_gate[l], gla_norm_w[l], conv_w[l], conv_b[l],
                            cn_w[l], cn_b[l], w_out[l])
        h = rmsnorm(x, ln2_w[l])
        if l % 2 == 0:
            i = l // 2
            x = x + swiglu(h, wd_gate[i], wd_up[i], wd_down[i])
        else:
            i = l // 2
            x = x + moe_swiglu(h, w_router[i], we_gate[i], we_up[i], we_down[i])
    return rmsnorm(x, final_norm_w)


_drawn_inputs = setup_inputs


def setup_inputs(seed=0):
    import zlib

    import numpy as np

    out = dict(_drawn_inputs(seed))
    spreads = {}
    factors = {}
    for name, (base, spread) in spreads.items():
        noise = np.random.default_rng([zlib.crc32(name.encode()), seed]).standard_normal(out[name].shape)
        drawn = base * np.exp(spread * noise) if base else spread * noise
        out[name] = __import__('jax').numpy.asarray(drawn.astype(out[name].dtype))
    for name, factor in factors.items():
        out[name] = (out[name] * factor).astype(out[name].dtype)
    return out
```

```python
from contextlib import ExitStack

import concourse.bass as bass
from concourse import mybir

F32 = mybir.dt.float32
F32R = mybir.dt.float32r
I32 = mybir.dt.int32
U8 = mybir.dt.uint8
ALU = mybir.AluOpType
ACT = mybir.ActivationFunctionType
AX = mybir.AxisListType.X

P = 128
UNIT = 2048
RAW = 11
RING = 3
EPS = 1e-6
NEG = -3.0e38


def trunk(nc, x, ln1_w, w_in, w_gate_up, b_gate, gla_norm_w, conv_w, conv_b, cn_w, cn_b, w_out,
          ln2_w, wd_gate, wd_up, wd_down, w_router, we_gate, we_up, we_down, final_norm_w, out):
    _, T, D = x.shape
    L, _, IN_COLS = w_in.shape
    RANK, KEY = w_gate_up.shape[1:]
    DV = gla_norm_w.shape[1]
    TAPS, CH = conv_w.shape[1:]
    VAL = w_out.shape[1] - CH
    HEADS = VAL // DV
    DK = KEY // HEADS
    FF = wd_gate.shape[2]
    NE = w_router.shape[2]
    TT, KD, CT, KT = T // P, D // P, CH // P, KEY // P
    HALF = D // 2
    assert (T, D, DK, DV, KEY, L) == (256, 1024, 64, P, 256, 2) and FF % 512 == 256 and NE == 8

    OFF_V, OFF_G = 2 * KEY, 2 * KEY + VAL
    OFF_R = OFF_G + VAL
    OFF_CA, OFF_CB = OFF_R + RANK, OFF_R + RANK + CH
    IN_UNITS = [OFF_CA, OFF_CB, OFF_CA + 256, OFF_CB + 256, 0, KEY, OFF_V, OFF_V + 256, OFF_G, OFF_G + 256]
    U_Q, U_K, U_V, U_G = 4, 5, 6, 8
    N_IN, N_OUT = len(IN_UNITS), w_out.shape[1] // 256
    N_MIX = N_IN + N_OUT
    CHUNKS = FF // 256
    N_FF = 3 * CHUNKS
    BASE = [0, N_MIX + N_FF]
    DENSE0 = N_MIX
    MOE0 = BASE[1] + N_MIX
    assert N_FF % RAW == 0 and N_FF % RING == 0

    EC = FF // 512 + 1
    plan = []
    for c in range(EC):
        parts = 2 if c < EC - 1 else 1
        plan += [("gate", c, p) for p in range(parts)] + [("up", c, p) for p in range(parts)]
        if c:
            plan += [("down", c - 1, 0), ("down", c - 1, 1)]
    plan += [("down", EC - 1, 0)]
    assert len(plan) == N_FF
    at = {what: u for u, what in enumerate(plan)}
    GATE_END = [at["gate", c, 1 if c < EC - 1 else 0] for c in range(EC)]
    UP_END = [at["up", c, 1 if c < EC - 1 else 0] for c in range(EC)]
    TURN = [GATE_END[c + 1] for c in range(EC - 1)] + [at["down", EC - 2, 0]]
    SCATTER = [2, 3, 4, 5]
    TURN_SEL, GATHER = 10, [16, 18]
    LAST_UP = UP_END[EC - 1]
    EXTRA = (2 * T) // (P + 1)
    ITEMS = NE + EXTRA

    ctx = ExitStack()
    with ctx:
        def sem(name):
            return ctx.enter_context(nc.semaphore(name))

        def on(stack):
            return lambda name, shape, dt=F32: stack.enter_context(nc.sbuf_tensor(name, shape, dt))

        sb = on(ctx)
        raw = sb("raw", [P, RAW, UNIT])
        w_hi = sb("w_hi", [P, RING, UNIT], F32R)
        w_lo = sb("w_lo", [P, RING, UNIT], F32R)
        X = sb("X", [P, TT, D])
        t_hi = sb("t_hi", [P, KD, T], F32R)
        t_lo = sb("t_lo", [P, KD, T], F32R)
        lnw = sb("lnw", [P, D])
        ident = sb("ident", [P, P])
        ones = sb("ones", [P, P])
        before = sb("before", [P, P])
        slot_no = sb("slot_no", [P, P])
        masks = sb("masks", [P, 8, P], U8)
        taps = sb("taps", [P, L, TAPS, CT])
        NPV = KT + 3 * CT + 1
        pv = sb("pv", [P, L, NPV])
        gr_hi = sb("gr_hi", [P, L, KD, RANK], F32R)
        gr_lo = sb("gr_lo", [P, L, KD, RANK], F32R)
        wgu = sb("wgu", [RANK, L, KEY])
        rt_hi = sb("rt_hi", [P, KD, NE], F32R)
        rt_lo = sb("rt_lo", [P, KD, NE], F32R)
        eps = sb("eps", [P, 1])
        ss = sb("ss", [P, TT])
        rstd = sb("rstd", [P, TT])
        slot_of = sb("slot_of", [P, ITEMS + 1, TT])
        gate_of = sb("gate_of", [P, ITEMS + 1, TT])
        meta = sb("meta", [P, 1 + EXTRA + 1], I32)

        s0 = ExitStack()
        sc = on(s0)
        tap_rows = sc("tap_rows", [P, L, P])
        pv_rows = sc("pv_rows", [P, P])
        gr_raw = sc("gr_raw", [P, L, KD, RANK])
        rt_raw = sc("rt_raw", [P, KD, NE])
        mask_f = sc("mask_f", [P, 8, P])
        s0.close()

        s1 = ExitStack()
        h = on(s1)("h", [P, TT, D])
        s1.close()

        s2 = ExitStack()
        sm = on(s2)
        qk = sm("qk", [P, 2, KT, T])
        o_sq = qk[:].rearrange("p a k t -> p (a k t)")
        qkE = sm("qkE", [P, 2, KT, T])
        o_rs = qkE[:].rearrange("p a k t -> p (a k t)")
        cgate = qkE[:, 0]
        Dif = sm("Dif", [P, KT, T])
        cum = sm("cum", [P, KT, T])
        att = sm("att", [P, 2, 2 * TT, P])
        og = att[:].rearrange("p r a i -> p (r a i)")
        attx = sm("attx", [P, 2, 2, P])
        v = sm("v", [P, TT, VAL])
        PAD = TAPS - 1
        cu = sm("cu", [P, CT, PAD + T])
        c_sq = cu[:].rearrange("p c t -> p (c t)")[:, 0:CT * T]
        acc = sm("acc", [P, CT, T])
        gr_t = sm("gr_t", [RANK, T])
        gr_s = sm("gr_s", [P, TT, RANK])
        s2.close()

        s3 = ExitStack()
        sd = on(s3)
        dg = sd("dg", [P, 512])
        dact = sd("dact", [P, 512])
        dT_hi = sd("dT_hi", [P, 2, T], F32R)
        dT_lo = sd("dT_lo", [P, 2, T], F32R)
        s3.close()

        s4 = ExitStack()
        se = on(s4)
        stage = se("stage", [P, KD, P])
        xs_hi = se("xs_hi", [P, KD, P], F32R)
        xs_lo = se("xs_lo", [P, KD, P], F32R)
        y_hi = se("y_hi", [P, D], F32R)
        y_lo = se("y_lo", [P, D], F32R)
        eg = se("eg", [P, 512])
        eact = se("eact", [P, 512])
        eT_hi = se("eT_hi", [P, 4, P], F32R)
        eT_lo = se("eT_lo", [P, 4, P], F32R)
        sel = se("sel", [P, TT, P], F32R)
        selT = se("selT", [P, TT, P], F32R)
        cur = se("cur", [P, 2, TT])
        slot_gate = se("slot_gate", [P, 1])
        started = se("started", [P, 2])
        rout = se("rout", [P, 24, TT, NE])
        s4.close()

        YB = ctx.enter_context(nc.psum_tensor("YB", [P, 4, 512], F32))
        WB = [ctx.enter_context(nc.psum_tensor(f"WB{i}", [P, 512], F32)) for i in range(4)]

        raw_ready = [sem(f"raw_ready{i}") for i in range(RAW)]
        x_ready, rows_ready, lnw_ready = sem("x_ready"), sem("rows_ready"), sem("lnw_ready")
        small_ready = sem("small_ready")
        hi_ready, lo_ready, unit_used = sem("hi_ready"), sem("lo_ready"), sem("unit_used")
        pool_step, consts_ready, turned_rows, params_ready = sem("pool_step"), sem("consts_ready"), sem("turned_rows"), sem("params_ready")
        small_hi, small_lo = sem("small_hi"), sem("small_lo")
        squared, rooted, inverted, normed = sem("squared"), sem("rooted"), sem("inverted"), sem("normed")
        h_turned, t_hi_ready, t_lo_ready = sem("h_turned"), sem("t_hi_ready"), sem("t_lo_ready")
        added = sem("added")
        gr_done, gr_copied, grT_done, grT_copied, logit_done = (sem(s) for s in ("gr_done", "gr_copied", "grT_done", "grT_copied", "logit_done"))
        cgate_ready, cu_ready, conv_step, pads_ready = (sem(s) for s in ("cgate_ready", "cu_ready", "conv_step", "pads_ready"))
        gate_abs, gate_exp, gate_ln, gate_min, gate_sub, cum_ready = (sem(s) for s in ("gate_abs", "gate_exp", "gate_ln", "gate_min", "gate_sub", "cum_ready"))
        qk_ready, v_ready = sem("qk_ready"), sem("v_ready")
        dif_ready, dif_abs, decay_ready, qE_ready, kE_ready, level_done, level_read = (sem(s) for s in (
            "dif_ready", "dif_abs", "decay_ready", "qE_ready", "kE_ready", "level_done", "level_read"))
        o_done, o_squared, o_summed, o_rooted, o_inverted, o_scaled, og_ready, o_gated, mix_hi, mix_lo = (sem(s) for s in (
            "o_done", "o_squared", "o_summed", "o_rooted", "o_inverted", "o_scaled", "og_ready", "o_gated", "mix_hi", "mix_lo"))
        c_summed, c_centred, c_squared, c_varied, c_rooted, c_inverted, c_scaled, c_silu, c_hi, c_lo = (sem(s) for s in (
            "c_summed", "c_centred", "c_squared", "c_varied", "c_rooted", "c_inverted", "c_scaled", "c_silu", "c_hi", "c_lo"))
        dgate_ready, dact_ready, dT_hi_ready, dT_lo_ready = (sem(s) for s in ("dgate_ready", "dact_ready", "dT_hi_ready", "dT_lo_ready"))
        logits_done, h_hi_ready, h_lo_ready, route_step, lead_exp, choice_ready, places_done, tables_ready, meta_ready, lead_ready = (sem(s) for s in (
            "logits_done", "h_hi_ready", "h_lo_ready", "route_step", "lead_exp", "choice_ready", "places_done", "tables_ready", "meta_ready", "lead_ready"))
        cur_ready, sel_ready, gathered, staged, xs_hi_ready, xs_lo_ready = (sem(s) for s in (
            "cur_ready", "sel_ready", "gathered", "staged", "xs_hi_ready", "xs_lo_ready"))
        egate_ready, eact_ready, eT_done, eT_hi_ready, eT_lo_ready = (sem(s) for s in (
            "egate_ready", "eact_ready", "eT_done", "eT_hi_ready", "eT_lo_ready"))
        y_zeroed, y_hi_ready, y_lo_ready, scattered, quad_added, selT_done, selT_ready = (sem(s) for s in (
            "y_zeroed", "y_hi_ready", "y_lo_ready", "scattered", "quad_added", "selT_done", "selT_ready"))
        out_stored = sem("out_stored")

        block = ctx.enter_context(nc.Block())

        LEVELS = [P, 64, 32, 16, 8, 4, 2, 1, 0]
        PV_BG, PV_CB, PV_CW, PV_CBB, PV_GN = 0, KT, KT + CT, KT + 2 * CT, KT + 3 * CT

        def slot_use(n):
            return n % RAW, n // RAW + 1

        wg_v = we_gate[0].rearrange("e (k p) f -> e p k f", p=P)
        wu_v = we_up[0].rearrange("e (k p) f -> e p k f", p=P)
        wd_v = we_down[0].rearrange("e (k p) n -> e p k n", p=P)

        @block.sync
        def _(sp):
            sp.dma_start(X[:], x[0].rearrange("(t p) d -> p t d", p=P)).then_inc(x_ready, 16)

            def load(n, src, k):
                slot, _ = slot_use(n)
                if n >= RAW:
                    sp.wait_ge(lo_ready, n - RAW + 1)
                sp.dma_start(raw[:, slot, :].rearrange("p (k c) -> p k c", k=k), src).then_inc(raw_ready[slot], 16)

            def load_mixer(l):
                for j, c0 in enumerate(IN_UNITS):
                    load(BASE[l] + j, w_in[l, :, c0:c0 + 256].rearrange("(k p) c -> p k c", p=P), 8)
                for j in range(N_OUT):
                    load(BASE[l] + N_IN + j, w_out[l, 256 * j:256 * (j + 1), :].rearrange("(k p) n -> p k n", p=P), 2)

            load_mixer(0)
            n = DENSE0
            for c in range(CHUNKS + 1):
                if c < CHUNKS:
                    load(n, wd_gate[0, :, 256 * c:256 * (c + 1)].rearrange("(k p) f -> p k f", p=P), 8)
                    load(n + 1, wd_up[0, :, 256 * c:256 * (c + 1)].rearrange("(k p) f -> p k f", p=P), 8)
                    n += 2
                if c:
                    load(n, wd_down[0, 256 * (c - 1):256 * c, :].rearrange("(k p) n -> p k n", p=P), 2)
                    n += 1
            load_mixer(1)

            def load_expert(e, item):
                for u, (what, c, part) in enumerate(plan):
                    slot, _ = slot_use(MOE0 + u)
                    sp.wait_ge(lo_ready, item * N_FF + (MOE0 + u - RAW + 1))
                    if what == "down":
                        k0 = 4 * c + 2 * part
                        src, k = wd_v[e, :, k0:k0 + 2, :], 2
                    else:
                        w = wg_v if what == "gate" else wu_v
                        if c < EC - 1:
                            src, k = w[e, :, 4 * part:4 * part + 4, 512 * c:512 * (c + 1)], 4
                        else:
                            src, k = w[e, :, :, 512 * c:FF], 8
                    sp.dma_start(raw[:, slot, :].rearrange("p (k c) -> p k c", k=k), src).then_inc(raw_ready[slot], 16)

            with sp.Fori(0, NE) as e:
                load_expert(e, e)
            sp.wait_ge(meta_ready, 1)
            n_items = sp.value_load(meta[0:1, 0:1], min_val=NE, max_val=ITEMS)
            with sp.If(n_items > NE):
                with sp.Fori(NE, n_items) as item:
                    e = sp.value_load(meta[0:1, bass.ds(item - (NE - 1), 1)], min_val=0, max_val=NE - 1)
                    load_expert(e, item)

            sp.wait_ge(normed, 5)
            sp.dma_start(out[0].rearrange("(t p) d -> p t d", p=P), h[:]).then_inc(out_stored, 16)
            sp.wait_ge(out_stored, 16)

        norm_weights = [ln1_w[0], ln2_w[0], ln1_w[1], ln2_w[1], final_norm_w]

        @block.gpsimd
        def _(pool):
            pool.dma_start(lnw[:], norm_weights[0].partition_broadcast(P)).then_inc(lnw_ready, 16)
            steps = [0]

            def step(ins):
                steps[0] += 1
                ins.then_inc(pool_step, 1)
                pool.wait_ge(pool_step, steps[0])

            step(pool.memset(ident[:], 0.0))
            step(pool.affine_select(out=ident[:], in_=ident[:], compare_op=ALU.not_equal, fill=1.0, base=0,
                                    pattern=[[-1, P]], channel_multiplier=1))
            step(pool.memset(eps[:], EPS))
            step(pool.memset(ones[:], 1.0))
            pool.affine_select(out=before[:], in_=ones[:], compare_op=ALU.is_gt, fill=0.0, base=0,
                               pattern=[[1, P]], channel_multiplier=-1).then_inc(consts_ready, 1)
            pool.iota(slot_no[:], pattern=[[1, P]], base=0, channel_multiplier=0,
                      allow_small_or_imprecise_dtypes=True).then_inc(consts_ready, 1)
            step(pool.memset(mask_f[:], 0.0))
            for n, s in enumerate(LEVELS[1:]):
                if s:
                    m = mask_f[:, n, :].rearrange("p (b s) -> p b s", s=2 * s)[:, :, s:2 * s]
                    nb = P // (2 * s)
                    step(pool.memset(m, 1.0))
                    step(pool.affine_select(out=m, in_=m, compare_op=ALU.is_ge, fill=0.0, base=0,
                                            pattern=[[-2 * s, nb], [0, s]], channel_multiplier=1))
                    step(pool.affine_select(out=m, in_=m, compare_op=ALU.is_ge, fill=0.0, base=s - 1,
                                            pattern=[[2 * s, nb], [0, s]], channel_multiplier=-1))
                else:
                    step(pool.tensor_copy(mask_f[:, n, :], ident[:]))
            step(pool.tensor_copy(masks[:], mask_f[:]))
            pool.memset(slot_of[:, ITEMS, :], -1.0).then_inc(consts_ready, 1)
            pool.memset(gate_of[:, ITEMS, :], 0.0).then_inc(consts_ready, 1)

            for l in range(L):
                if l == 0:
                    pool.wait_ge(params_ready, 1)
                    pool.wait_ge(small_lo, 3)
                else:
                    pool.wait_ge(added, 2)
                pool.memset(cu[:, :, 0:PAD], 0.0).then_inc(pads_ready, 1)
                pool.memset(att[:], 0.0).then_inc(pads_ready, 1)
                pool.wait_ge(normed, 2 * l + 1)
                pool.dma_start(lnw[:], norm_weights[2 * l + 1].partition_broadcast(P)).then_inc(lnw_ready, 16)
                for n in range(len(LEVELS) - 1):
                    pool.wait_ge(decay_ready, 8 * l + n + 1)
                    if n:
                        pool.wait_ge(level_done, 9 * l + n)
                    pool.tensor_tensor(qkE[:, 1], qk[:, 1], Dif[:], ALU.mult).then_inc(kE_ready, 1)
                pool.wait_ge(normed, 2 * l + 2)
                pool.dma_start(lnw[:], norm_weights[2 * l + 2].partition_broadcast(P)).then_inc(lnw_ready, 16)

        @block.scalar
        def _(act):
            for l in range(L):
                act.dma_start(tap_rows[0:TAPS * CT, l, :], conv_w[l].rearrange("w (c p) -> (w c) p", p=P)).then_inc(rows_ready, 16)
                r = l * NPV
                for src, at0, k in ((b_gate, PV_BG, KT), (conv_b, PV_CB, CT), (cn_w, PV_CW, CT), (cn_b, PV_CBB, CT), (gla_norm_w, PV_GN, 1)):
                    act.dma_start(pv_rows[r + at0:r + at0 + k, :], src[l].rearrange("(c p) -> c p", p=P)).then_inc(rows_ready, 16)
                act.dma_start(gr_raw[:, l], w_in[l, :, OFF_R:OFF_R + RANK].rearrange("(k p) c -> p k c", p=P)).then_inc(small_ready, 16)
            act.dma_start(wgu[:], w_gate_up.rearrange("l r c -> r l c")).then_inc(small_ready, 16)
            act.dma_start(rt_raw[:], w_router[0].rearrange("(k p) e -> p k e", p=P)).then_inc(small_ready, 16)

            def hi(n, item=None):
                slot, use = slot_use(n)
                if item is None:
                    act.wait_ge(raw_ready[slot], 16 * use)
                    if n >= RING:
                        act.wait_ge(unit_used, n - RING + 1)
                else:
                    act.wait_ge(raw_ready[slot], item * (16 * N_FF // RAW) + 16 * use)
                    act.wait_ge(unit_used, item * N_FF + (n - RING + 1))
                act.activation(w_hi[:, n % RING, :], raw[:, slot, :], ACT.Copy).then_inc(hi_ready, 1)

            def norm(j, ready, count):
                if ready is not None:
                    act.wait_ge(ready, count)
                for t in range(TT):
                    act.activation(h[:, t, :], X[:, t, :], ACT.Square, accum_out=ss[:, t:t + 1]).then_inc(squared, 1)
                act.wait_ge(squared, TT * (j + 1))
                act.activation(rstd[:], ss[:], ACT.Sqrt, scale=1.0 / D, bias=eps[:]).then_inc(rooted, 1)

            def turned(j):
                for q in range(4):
                    t, g = divmod(q, 2)
                    act.wait_ge(h_turned, 4 * j + q + 1)
                    act.activation(t_hi[:, 4 * g:4 * g + 4, P * t:P * (t + 1)], WB[q][:].rearrange("p (k t) -> p k t", k=4),
                                   ACT.Copy).then_inc(t_hi_ready, 1)

            def after_unit(n):
                act.wait_ge(unit_used, n + 1)

            def mixer(l):
                b = BASE[l]
                turned(2 * l)
                hi(b + 3)
                for g in range(2):
                    after_unit(b + 2 * g + 1)
                    if g or l:
                        act.wait_ge(cu_ready, 2 * l + g)
                    act.activation(cgate.rearrange("p k t -> p (k t)"), WB[2 * g + 1][:], ACT.Sigmoid).then_inc(cgate_ready, 1)
                    hi(b + 4 + g)
                act.wait_ge(logit_done, l + 1)
                for k in range(KT):
                    act.activation(Dif[:, k, :], YB[:, 2, T * k:T * (k + 1)], ACT.Abs,
                                   bias=pv[:, l, PV_BG + k:PV_BG + k + 1]).then_inc(gate_abs, 1)
                act.wait_ge(gate_abs, KT * (l + 1))
                act.activation(Dif[:], Dif[:], ACT.Exp, scale=-1.0).then_inc(gate_exp, 1)
                act.wait_ge(gate_exp, l + 1)
                act.activation(Dif[:], Dif[:], ACT.Ln, bias=1.0).then_inc(gate_ln, 1)
                hi(b + 6)
                after_unit(b + U_Q)
                act.activation(qk[:, 0].rearrange("p k t -> p (k t)"), WB[U_Q % 4][:], ACT.Copy, scale=DK ** -0.5).then_inc(qk_ready, 1)
                hi(b + 7)
                after_unit(b + U_K)
                act.activation(qk[:, 1].rearrange("p k t -> p (k t)"), WB[U_K % 4][:], ACT.Copy).then_inc(qk_ready, 1)

                def decays(n):
                    m = 8 * l + n + 1
                    act.wait_ge(dif_ready, m)
                    if n == 0:
                        act.activation(Dif[:, :, 0:P], Dif[:, :, 0:P], ACT.Abs).then_inc(dif_abs, 1)
                        act.activation(Dif[:, :, P:T], cum[:, :, P:T], ACT.Abs).then_inc(dif_abs, 1)
                    else:
                        act.activation(Dif[:], Dif[:], ACT.Abs).then_inc(dif_abs, 1)
                    act.wait_ge(dif_abs, m + l + 1)
                    act.activation(Dif[:], Dif[:], ACT.Exp, scale=-1.0 / 16.0).then_inc(decay_ready, 1)

                def v_half(g):
                    after_unit(b + U_V + g)
                    act.activation(v[:, :, 256 * g:256 * (g + 1)], WB[(U_V + g) % 4][:].rearrange("p (t c) -> p t c", t=TT),
                                   ACT.Copy).then_inc(v_ready, 1)

                decays(0)
                hi(b + 8)
                v_half(0)
                decays(1)
                hi(b + 9)
                decays(2)
                v_half(1)
                decays(3)
                for n in range(4, 8):
                    decays(n)
                    if n < 7:
                        hi(b + N_IN + n - 4)
                act.wait_ge(o_done, l + 1)
                act.activation(o_sq, YB[:, 0:2, :].rearrange("p a c -> p (a c)"), ACT.Square).then_inc(o_squared, 1)
                act.wait_ge(o_summed, l + 1)
                act.activation(o_rs, YB[:, 2:4, :].rearrange("p a c -> p (a c)"), ACT.Sqrt, scale=1.0 / DV, bias=eps[:]).then_inc(o_rooted, 1)
                act.wait_ge(c_centred, l + 1)
                act.activation(c_sq, acc[:].rearrange("p c t -> p (c t)"), ACT.Square).then_inc(c_squared, 1)
                act.wait_ge(c_varied, l + 1)
                act.activation(Dif[:, 0, :], WB[3][:, 0:T], ACT.Sqrt, scale=1.0 / CH, bias=eps[:]).then_inc(c_rooted, 1)
                for g in range(2):
                    act.activation(og[:, 512 * g:512 * (g + 1)], WB[g][:], ACT.Silu).then_inc(og_ready, 1)
                act.wait_ge(o_gated, l + 1)
                act.activation(t_hi[:, 0:HEADS, :], o_sq.rearrange("p (h t) -> p h t", h=HEADS), ACT.Copy).then_inc(mix_hi, 1)
                act.wait_ge(c_scaled, l + 1)
                for c in range(CT):
                    act.activation(c_sq.rearrange("p (c t) -> p c t", c=CT)[:, c, :], acc[:, c, :], ACT.Silu,
                                   scale=pv[:, l, PV_CW + c:PV_CW + c + 1], bias=pv[:, l, PV_CBB + c:PV_CBB + c + 1]).then_inc(c_silu, 1)
                act.wait_ge(c_silu, CT * (l + 1))
                act.activation(t_hi[:, HEADS:, :], c_sq.rearrange("p (c t) -> p c t", c=CT), ACT.Copy).then_inc(c_hi, 1)
                hi(b + N_IN + 3)

            act.wait_ge(small_ready, 16 * (L + 2))
            for l in range(L):
                act.activation(gr_hi[:, l], gr_raw[:, l], ACT.Copy).then_inc(small_hi, 1)
            act.activation(rt_hi[:], rt_raw[:], ACT.Copy).then_inc(small_hi, 1)
            act.wait_ge(pool_step, 3)
            act.wait_ge(small_lo, 3)
            act.wait_ge(params_ready, 1)
            act.wait_ge(consts_ready, 4)
            norm(0, x_ready, 16)
            for n in range(RING):
                hi(n)
            mixer(0)

            d0 = DENSE0
            hi(d0 + 0)
            hi(d0 + 1)
            norm(1, added, 1)
            hi(d0 + 2)
            turned(1)

            def dense_gate(c, n):
                after_unit(n)
                if c:
                    act.wait_ge(dact_ready, c)
                act.activation(dg[:], WB[c % 2][:], ACT.Silu).then_inc(dgate_ready, 1)

            def dense_turn(c, n_free):
                if n_free is not None:
                    after_unit(n_free)
                act.wait_ge(dact_ready, c + 1)
                act.activation(dT_hi[:].rearrange("p f t -> p (f t)"), dact[:], ACT.Copy).then_inc(dT_hi_ready, 1)

            gate_at = [d0] + [d0 + 3 * c - 1 for c in range(1, CHUNKS)]
            down_at = [d0 + 3 * c + 4 for c in range(CHUNKS - 1)] + [d0 + N_FF - 1]
            done = 3
            for c in range(CHUNKS):
                while done < min(gate_at[c] + 3 - d0, N_FF):
                    hi(d0 + done)
                    done += 1
                dense_gate(c, gate_at[c])
                if done < N_FF:
                    hi(d0 + done)
                    done += 1
                dense_turn(c, down_at[c - 1] if c else None)
            for n in range(BASE[1], BASE[1] + 2):
                hi(n)
            norm(2, added, 2)
            hi(BASE[1] + 2)
            mixer(1)

            for n in range(MOE0, MOE0 + 2):
                hi(n)
            norm(3, added, 3)
            turned(3)
            act.wait_ge(logits_done, 1)
            act.activation(t_hi[:].rearrange("p a b -> p (a b)"), h[:].rearrange("p t d -> p (t d)"), ACT.Copy).then_inc(h_hi_ready, 1)
            act.wait_ge(lead_ready, 1)
            act.activation(rout[:, 12, :, 1], rout[:, 12, :, 0], ACT.Exp).then_inc(lead_exp, 1)

            def stage_half(g, count):
                act.wait_ge(gathered, count)
                act.activation(stage[:, 4 * g:4 * g + 4, :], YB[:, 2, :].rearrange("p (k j) -> p k j", k=4), ACT.Copy).then_inc(staged, 1)

            act.wait_ge(h_lo_ready, 1)
            for g in range(2):
                stage_half(g, g + 1)
            act.wait_ge(staged, 2)
            act.activation(xs_hi[:], stage[:], ACT.Copy).then_inc(xs_hi_ready, 1)
            act.wait_ge(meta_ready, 1)
            n_items = act.value_load(meta[0:1, 0:1], min_val=NE, max_val=ITEMS)

            def y_part():
                act.activation(y_hi[:], YB[:, 0:2, :].rearrange("p a c -> p (a c)"), ACT.Copy, scale=slot_gate[:]).then_inc(y_hi_ready, 1)

            act.wait_ge(y_zeroed, 1)
            with act.Fori(0, n_items) as i:
                for u in range(N_FF):
                    if u >= 2:
                        hi(MOE0 + u, i)
                    if u == 2:
                        act.wait_ge(unit_used, i * N_FF + MOE0)
                        y_part()
                    for c in range(EC):
                        if TURN[c] + 2 == u:
                            act.wait_ge(eT_done, i * EC + (c + 1))
                            w = 4 if c < EC - 1 else 2
                            act.activation(eT_hi[:, 0:w, :], YB[:, 3, 0:P * w].rearrange("p (f t) -> p f t", f=w), ACT.Copy).then_inc(eT_hi_ready, 1)
                        if GATE_END[c] + 2 == u:
                            act.wait_ge(unit_used, i * N_FF + (MOE0 + GATE_END[c] + 1))
                            act.wait_ge(eact_ready, i * EC + (c + 1))
                            w = 512 if c < EC - 1 else 256
                            act.activation(eg[:, 0:w], WB[c % 2][:, 0:w], ACT.Silu).then_inc(egate_ready, 1)
                    for g in range(2):
                        if GATHER[g] + 2 == u:
                            act.wait_ge(xs_lo_ready, i + 1)
                            stage_half(g, i * 2 + (3 + g))
                    if LAST_UP + 2 == u:
                        act.wait_ge(unit_used, i * N_FF + (MOE0 + LAST_UP + 1))
                        act.wait_ge(staged, i * 2 + 4)
                        act.activation(xs_hi[:], stage[:], ACT.Copy).then_inc(xs_hi_ready, 1)
                with act.If(i < n_items - 1):
                    for u in range(2):
                        hi(MOE0 + N_FF + u, i)
            act.wait_ge(unit_used, n_items * N_FF + MOE0)
            y_part()
            norm(4, quad_added, n_items * 4 + 5)

        @block.vector
        def _(dve):
            def lo(n, item=None):
                slot, _ = slot_use(n)
                if item is None:
                    dve.wait_ge(hi_ready, n + 1)
                    if n >= RING:
                        dve.wait_ge(unit_used, n - RING + 1)
                else:
                    dve.wait_ge(hi_ready, item * N_FF + (n + 1))
                    dve.wait_ge(unit_used, item * N_FF + (n - RING + 1))
                dve.tensor_tensor(w_lo[:, n % RING, :], raw[:, slot, :], w_hi[:, n % RING, :].bitcast(F32), ALU.subtract).then_inc(lo_ready, 1)

            def norm(j):
                dve.wait_ge(rooted, j + 1)
                dve.reciprocal(rstd[:], rstd[:]).then_inc(inverted, 1)
                dve.wait_ge(inverted, j + 1)
                dve.wait_ge(lnw_ready, 16 * (j + 1))
                for t in range(TT):
                    ins = dve.scalar_tensor_tensor(out=h[:, t, :], in0=X[:, t, :], scalar=rstd[:, t:t + 1], in1=lnw[:],
                                                   op0=ALU.mult, op1=ALU.mult)
                ins.then_inc(normed, 1)

            def turned(j):
                for q in range(4):
                    t, g = divmod(q, 2)
                    dst = (slice(None), slice(4 * g, 4 * g + 4), slice(P * t, P * (t + 1)))
                    dve.wait_ge(t_hi_ready, 4 * j + q + 1)
                    dve.tensor_tensor(t_lo[dst], WB[q][:].rearrange("p (k t) -> p k t", k=4), t_hi[dst].bitcast(F32),
                                      ALU.subtract).then_inc(t_lo_ready, 1)

            def after_unit(n):
                dve.wait_ge(unit_used, n + 1)

            def residual():
                for t in range(TT):
                    ins = dve.tensor_tensor(X[:, t, :], X[:, t, :], YB[:, 2 * t:2 * t + 2, :].rearrange("p a c -> p (a c)"), ALU.add)
                ins.then_inc(added, 1)

            dve.wait_ge(turned_rows, 3)
            for l in range(L):
                dve.tensor_copy(taps[:, l].rearrange("p w c -> p (w c)"), WB[l][:, 0:TAPS * CT])
            dve.tensor_copy(pv[:].rearrange("p l c -> p (l c)"), WB[2][:, 0:L * NPV]).then_inc(params_ready, 1)
            dve.wait_ge(small_hi, 3)
            for l in range(L):
                dve.tensor_tensor(gr_lo[:, l], gr_raw[:, l], gr_hi[:, l].bitcast(F32), ALU.subtract).then_inc(small_lo, 1)
            dve.tensor_tensor(rt_lo[:], rt_raw[:], rt_hi[:].bitcast(F32), ALU.subtract).then_inc(small_lo, 1)

            def mixer(l):
                b = BASE[l]
                turned(2 * l)
                dve.wait_ge(gr_done, l + 1)
                dve.tensor_copy(gr_s[:].rearrange("p t r -> p (t r)"), YB[:, 3, 0:TT * RANK]).then_inc(gr_copied, 1)
                lo(b + 3)
                dve.wait_ge(grT_done, l + 1)
                dve.tensor_copy(gr_t[:], YB[0:RANK, 1, 0:T]).then_inc(grT_copied, 1)

                def conv_input(g):
                    dve.wait_ge(cgate_ready, 2 * l + g + 1)
                    dve.wait_ge(pads_ready, 2 * (l + 1))
                    dve.tensor_tensor(cu[:, 2 * g:2 * g + 2, PAD:], cgate, WB[2 * g][:].rearrange("p (c t) -> p c t", c=2),
                                      ALU.mult).then_inc(cu_ready, 1)

                conv_no = [0, 0]
                conv_all = [0]

                def conv(g, count):
                    for m in range(conv_no[g], min(conv_no[g] + count, 2 * TAPS)):
                        w, c = m // 2, 2 * g + m % 2
                        if w == 0:
                            dve.wait_ge(cu_ready, 2 * l + g + 1)
                            ins = dve.tensor_scalar(acc[:, c, :], cu[:, c, 0:T], taps[:, l, 0, c:c + 1],
                                                    pv[:, l, PV_CB + c:PV_CB + c + 1], ALU.mult, ALU.add)
                        else:
                            dve.wait_ge(conv_step, CT * TAPS * l + conv_all[0] - 1)
                            ins = dve.scalar_tensor_tensor(out=acc[:, c, :], in0=cu[:, c, w:w + T], scalar=taps[:, l, w, c:c + 1],
                                                           in1=acc[:, c, :], op0=ALU.mult, op1=ALU.add)
                        ins.then_inc(conv_step, 1)
                        conv_all[0] += 1
                    conv_no[g] = min(conv_no[g] + count, 2 * TAPS)

                conv_input(0)
                conv(0, 4)
                lo(b + 4)
                conv(0, 8)
                lo(b + 5)
                conv_input(1)
                dve.wait_ge(logit_done, l + 1)
                dve.wait_ge(gate_abs, KT * (l + 1))
                for k in range(KT):
                    ins = dve.tensor_scalar(cum[:, k, :], YB[:, 2, T * k:T * (k + 1)], pv[:, l, PV_BG + k:PV_BG + k + 1], 0.0,
                                            ALU.add, ALU.min)
                ins.then_inc(gate_min, 1)
                conv(0, 6)
                lo(b + 6)
                dve.wait_ge(gate_ln, l + 1)
                dve.wait_ge(gate_min, l + 1)
                dve.tensor_tensor(cum[:], cum[:], Dif[:], ALU.subtract).then_inc(gate_sub, 1)
                dve.wait_ge(gate_sub, l + 1)
                for k in range(KT):
                    for t in range(TT):
                        c = cum[:, k, P * t:P * (t + 1)]
                        ins = dve.tensor_tensor_scan(c, ones[:], c, 0.0, ALU.mult, ALU.add)
                ins.then_inc(cum_ready, 1)
                conv(0, 6)
                lo(b + 7)

                def differences(n):
                    s = LEVELS[n]
                    if n == 0:
                        dve.wait_ge(cum_ready, l + 1)
                    else:
                        dve.wait_ge(kE_ready, 8 * l + n)
                        dve.wait_ge(qE_ready, 8 * l + n)
                    if s == P:
                        ins = dve.tensor_tensor(Dif[:, :, 0:P], cum[:, :, 0:P], cum[:, :, P - 1:P].broadcast_to([P, KT, P]), ALU.subtract)
                    else:
                        blocks = cum[:].rearrange("p k (b s) -> p (k b) s", s=2 * s)
                        nb = KT * T // (2 * s)
                        ins = dve.tensor_tensor(Dif[:].rearrange("p k (b s) -> p (k b) s", s=2 * s), blocks,
                                                blocks[:, :, s - 1:s].broadcast_to([P, nb, 2 * s]), ALU.subtract)
                    ins.then_inc(dif_ready, 1)

                def q_decayed(n):
                    dve.wait_ge(decay_ready, 8 * l + n + 1)
                    if n == 0:
                        dve.wait_ge(qk_ready, 2 * (l + 1))
                    else:
                        dve.wait_ge(level_done, 9 * l + n)
                    dve.tensor_tensor(qkE[:, 0], qk[:, 0], Dif[:], ALU.mult).then_inc(qE_ready, 1)

                def level_read_out(n):
                    dve.wait_ge(level_done, 9 * l + n + 1)
                    if n == 1:
                        dve.wait_ge(pads_ready, 2 * (l + 1))
                    if n > 1:
                        dve.wait_ge(level_read, 2 * (9 * l + n))
                    for r in range(2):
                        bank = YB[:, 2 * (n % 2) + r, :]
                        if n == 0:
                            ins = dve.tensor_copy(attx[:, r].rearrange("p a i -> p (a i)"), bank[:, 0:2 * P])
                        else:
                            ins = dve.copy_predicated(att[:, r], masks[:, n - 1:n, :].broadcast_to([P, 2 * TT, P]),
                                                      bank.rearrange("p (a i) -> p a i", i=P))
                        ins.then_inc(level_read, 1)

                differences(0)
                conv(0, 4)
                q_decayed(0)
                differences(1)
                lo(b + 8)
                level_read_out(0)
                q_decayed(1)
                differences(2)
                conv(0, 2)
                level_read_out(1)
                q_decayed(2)
                lo(b + 9)
                differences(3)
                conv(0, 2)
                level_read_out(2)
                for n in range(3, 8):
                    q_decayed(n)
                    if n < 7:
                        differences(n + 1)
                    conv(0, 4)
                    level_read_out(n)
                    if n in (4, 5, 6):
                        lo(b + N_IN + n - 4)
                level_read_out(8)
                conv(0, 2 * TAPS)
                conv(1, 12)
                dve.wait_ge(o_rooted, l + 1)
                dve.reciprocal(o_rs, o_rs).then_inc(o_inverted, 1)
                conv(1, 2 * TAPS)
                dve.wait_ge(o_inverted, l + 1)
                dve.tensor_tensor(o_rs, YB[:, 0:2, :].rearrange("p a c -> p (a c)"), o_rs, ALU.mult).then_inc(o_scaled, 1)
                dve.wait_ge(c_summed, l + 1)
                dve.scalar_tensor_tensor(out=acc[:], in0=WB[2][:, 0:T].unsqueeze(1).broadcast_to([P, CT, T]), scalar=-1.0 / CH,
                                         in1=acc[:], op0=ALU.mult, op1=ALU.add).then_inc(c_centred, 1)
                dve.wait_ge(og_ready, 2 * (l + 1))
                dve.wait_ge(o_scaled, l + 1)
                dve.scalar_tensor_tensor(out=o_sq, in0=o_rs, scalar=pv[:, l, PV_GN:PV_GN + 1], in1=og,
                                         op0=ALU.mult, op1=ALU.mult).then_inc(o_gated, 1)
                dve.wait_ge(c_rooted, l + 1)
                dve.reciprocal(Dif[:, 0, :], Dif[:, 0, :]).then_inc(c_inverted, 1)
                dve.wait_ge(c_inverted, l + 1)
                dve.tensor_tensor(acc[:], acc[:], Dif[:, 0:1, :].broadcast_to([P, CT, T]), ALU.mult).then_inc(c_scaled, 1)
                dve.wait_ge(mix_hi, l + 1)
                dve.tensor_tensor(t_lo[:, 0:HEADS, :], o_sq.rearrange("p (h t) -> p h t", h=HEADS), t_hi[:, 0:HEADS, :].bitcast(F32),
                                  ALU.subtract).then_inc(mix_lo, 1)
                dve.wait_ge(c_hi, l + 1)
                dve.tensor_tensor(t_lo[:, HEADS:, :], c_sq.rearrange("p (c t) -> p c t", c=CT), t_hi[:, HEADS:, :].bitcast(F32),
                                  ALU.subtract).then_inc(c_lo, 1)
                lo(b + N_IN + 3)
                after_unit(b + N_MIX - 1)
                residual()

            for n in range(RING):
                if n == 1:
                    norm(0)
                lo(n)
            mixer(0)

            d0 = DENSE0
            lo(d0 + 0)
            norm(1)
            lo(d0 + 1)
            turned(1)
            lo(d0 + 2)

            def dense_act(c, n):
                after_unit(n)
                dve.wait_ge(dgate_ready, c + 1)
                if c:
                    dve.wait_ge(dT_lo_ready, c)
                dve.tensor_tensor(dact[:], dg[:], WB[2 + c % 2][:], ALU.mult).then_inc(dact_ready, 1)

            def dense_turn(c):
                dve.wait_ge(dT_hi_ready, c + 1)
                dve.tensor_tensor(dT_lo[:].rearrange("p f t -> p (f t)"), dact[:], dT_hi[:].rearrange("p f t -> p (f t)").bitcast(F32),
                                  ALU.subtract).then_inc(dT_lo_ready, 1)

            up_at = [d0 + 1] + [d0 + 3 * c for c in range(1, CHUNKS)]
            done = 3
            for c in range(CHUNKS):
                while done < min(up_at[c] + 3 - d0, N_FF):
                    lo(d0 + done)
                    done += 1
                dense_act(c, up_at[c])
                dense_turn(c)
            while done < N_FF:
                lo(d0 + done)
                done += 1
            after_unit(d0 + N_FF - 1)
            residual()
            for n in range(BASE[1], BASE[1] + RING):
                if n == BASE[1] + 1:
                    norm(2)
                lo(n)
            mixer(1)

            for n in range(MOE0, MOE0 + 2):
                lo(n)
            norm(3)
            turned(3)
            dve.wait_ge(h_hi_ready, 1)
            dve.tensor_tensor(t_lo[:].rearrange("p a b -> p (a b)"), h[:].rearrange("p t d -> p (t d)"),
                              t_hi[:].rearrange("p a b -> p (a b)").bitcast(F32), ALU.subtract).then_inc(h_lo_ready, 1)
            dve.wait_ge(h_lo_ready, 1)
            steps = [0]

            def step(ins):
                steps[0] += 1
                ins.then_inc(route_step, 1)
                dve.wait_ge(route_step, steps[0])

            lg, eq, score, first, l2, second, comb, chosen, place, over, rank = (rout[:, k] for k in range(11))
            lead = rout[:, 12]
            top = rout[:, 13]
            prefer = rout[:, 14]
            wide = (P, TT, NE)

            def each(col):
                return col.broadcast_to(list(wide))

            for e in range(NE):
                ins = dve.memset(prefer[:, :, e:e + 1], float(NE - e))
            step(ins)
            step(dve.tensor_copy(lg, YB[:, 0, 0:TT * NE].rearrange("p (t e) -> p t e", t=TT)))

            def largest(values, k, onehot):
                step(dve.tensor_reduce(top[:, :, k], values, AX, ALU.max))
                step(dve.tensor_tensor(eq, values, each(top[:, :, k:k + 1]), ALU.is_equal))
                step(dve.tensor_tensor(score, eq, prefer, ALU.mult))
                step(dve.tensor_reduce(top[:, :, 2 + k], score, AX, ALU.max))
                step(dve.tensor_tensor(onehot, score, each(top[:, :, 2 + k:3 + k]), ALU.is_equal))

            largest(lg, 0, first)
            step(dve.scalar_tensor_tensor(out=l2, in0=first, scalar=NEG, in1=lg, op0=ALU.mult, op1=ALU.add))
            largest(l2, 1, second)
            dve.tensor_tensor(lead[:, :, 0], top[:, :, 1], top[:, :, 0], ALU.subtract).then_inc(lead_ready, 1)
            dve.tensor_tensor(chosen, first, second, ALU.add).then_inc(choice_ready, 1)
            dve.wait_ge(lead_exp, 1)
            step(dve.tensor_scalar(lead[:, :, 2], lead[:, :, 1], 1.0, None, ALU.add))
            step(dve.reciprocal(lead[:, :, 3], lead[:, :, 2]))
            step(dve.tensor_tensor(lead[:, :, 4], lead[:, :, 3], lead[:, :, 1], ALU.mult))
            step(dve.tensor_tensor(first, first, each(lead[:, :, 3:4]), ALU.mult))
            step(dve.tensor_tensor(second, second, each(lead[:, :, 4:5]), ALU.mult))
            step(dve.tensor_tensor(comb, first, second, ALU.add))
            dve.wait_ge(places_done, 1)
            step(dve.scalar_tensor_tensor(out=place, in0=YB[:, 1, 0:TT * NE].rearrange("p (t e) -> p t e", t=TT), scalar=1.0,
                                          in1=chosen, op0=ALU.add, op1=ALU.mult))
            step(dve.tensor_scalar(place, place, -1.0, None, ALU.add))
            step(dve.tensor_copy(slot_of[:, 0:NE, :].rearrange("p e t -> p t e"), place))
            step(dve.tensor_copy(gate_of[:, 0:NE, :].rearrange("p e t -> p t e"), comb))
            step(dve.tensor_scalar(over[:, 0, :], YB[:, 1, TT * NE:TT * NE + NE], float(P), None, ALU.is_gt))
            step(dve.tensor_tensor_scan(rank[:, 0, :], ones[:, 0:NE], over[:, 0, :], 0.0, ALU.mult, ALU.add))
            for k in range(EXTRA):
                pick, prod = rout[:, 15 + k], rout[:, 18 + k]
                step(dve.scalar_tensor_tensor(out=pick[:, 0, :], in0=rank[:, 0, :], scalar=float(k + 1), in1=over[:, 0, :],
                                              op0=ALU.is_equal, op1=ALU.mult))
                for table, values in ((slot_of, place), (gate_of, comb)):
                    step(dve.tensor_tensor(prod, values, pick[:, 0:1, :].broadcast_to(list(wide)), ALU.mult))
                    step(dve.tensor_reduce(table[:, NE + k, :], prod, AX, ALU.add))
                step(dve.tensor_scalar(slot_of[:, NE + k, :], slot_of[:, NE + k, :], -float(P), None, ALU.add))
                step(dve.tensor_tensor(prod[:, 0, :], prefer[:, 0, :], pick[:, 0, :], ALU.mult))
                step(dve.tensor_reduce(top[:, 0:1, 5], prod[:, 0:1, :], AX, ALU.add))
                step(dve.tensor_scalar(top[:, 0:1, 5], top[:, 0:1, 5], -1.0, float(NE), ALU.mult, ALU.add))
                step(dve.tensor_scalar(top[:, 0:1, 5], top[:, 0:1, 5], float(NE - 1), None, ALU.min))
                step(dve.tensor_copy(meta[:, 1 + k:2 + k], top[:, 0:1, 5]))
            step(dve.tensor_scalar(top[:, 0:1, 6], rank[:, 0:1, NE - 1], float(NE), None, ALU.add))
            dve.tensor_copy(meta[:, 0:1], top[:, 0:1, 6]).then_inc(meta_ready, 1)
            dve.wait_ge(meta_ready, 1)
            n_items = dve.value_load(meta[0:1, 0:1], min_val=NE, max_val=ITEMS)

            def select(item, count):
                dve.tensor_copy(cur[:, 0, :], slot_of[:, bass.ds(item, 1), :].rearrange("p o t -> p (o t)"))
                dve.tensor_copy(cur[:, 1, :], gate_of[:, bass.ds(item, 1), :].rearrange("p o t -> p (o t)")).then_inc(cur_ready, 1)
                dve.wait_ge(cur_ready, count)
                for t in range(TT):
                    ins = dve.tensor_scalar(sel[:, t, :], slot_no[:], cur[:, 0, t:t + 1], None, ALU.is_equal)
                ins.then_inc(sel_ready, 1)

            dve.wait_ge(route_step, steps[0])
            select(0, 1)
            dve.memset(slot_gate[:], 0.0)
            dve.memset(selT[:].bitcast(F32), 0.0)
            dve.memset(YB[:, 0:2, :], 0.0).then_inc(y_zeroed, 1)

            def y_part(count):
                dve.wait_ge(y_hi_ready, count)
                dve.scalar_tensor_tensor(out=y_lo[:], in0=YB[:, 0:2, :].rearrange("p a c -> p (a c)"), scalar=slot_gate[:],
                                         in1=y_hi[:].bitcast(F32), op0=ALU.mult, op1=ALU.subtract).then_inc(y_lo_ready, 1)

            def xs_part(count):
                dve.wait_ge(xs_hi_ready, count)
                dve.tensor_tensor(xs_lo[:], stage[:], xs_hi[:].bitcast(F32), ALU.subtract).then_inc(xs_lo_ready, 1)

            def add_quad(r, count):
                t, half = divmod(r, 2)
                dve.wait_ge(scattered, count)
                dve.wait_ge(quad_added, count)
                dst = X[:, t, HALF * half:HALF * (half + 1)]
                dve.tensor_tensor(dst, dst, YB[:, 2, :], ALU.add).then_inc(quad_added, 1)

            xs_part(1)
            dve.memset(started[:, 0:1], 0.0).then_inc(eact_ready, 1)
            dve.memset(started[:, 1:2], 0.0).then_inc(quad_added, 1)
            dve.wait_ge(y_zeroed, 1)
            with dve.Fori(0, n_items) as i:
                for u in range(N_FF):
                    if u >= 2:
                        lo(MOE0 + u, i)
                    if u == 2:
                        y_part(i + 1)
                    for r in range(4):
                        if SCATTER[r] + 2 == u:
                            add_quad(r, i * 4 + (r + 1))
                    for c in range(EC):
                        if TURN[c] + 2 == u:
                            dve.wait_ge(eT_hi_ready, i * EC + (c + 1))
                            w = 4 if c < EC - 1 else 2
                            dve.tensor_tensor(eT_lo[:, 0:w, :], YB[:, 3, 0:P * w].rearrange("p (f t) -> p f t", f=w),
                                              eT_hi[:, 0:w, :].bitcast(F32), ALU.subtract).then_inc(eT_lo_ready, 1)
                        if UP_END[c] + 2 == u:
                            dve.wait_ge(egate_ready, i * EC + (c + 1))
                            dve.wait_ge(unit_used, i * N_FF + (MOE0 + UP_END[c] + 1))
                            w = 512 if c < EC - 1 else 256
                            dve.tensor_tensor(eact[:, 0:w], eg[:, 0:w], WB[2 + c % 2][:, 0:w], ALU.mult).then_inc(eact_ready, 1)
                    if TURN_SEL + 2 == u:
                        dve.wait_ge(selT_done, i + 1)
                        dve.tensor_copy(selT[:].rearrange("p t j -> p (t j)"), YB[:, 2, 0:TT * P])
                        dve.tensor_copy(slot_gate[:], YB[:, 2, TT * P:TT * P + 1]).then_inc(selT_ready, 1)
                        select(i + 1, i + 2)
                    if LAST_UP + 2 == u:
                        xs_part(i + 2)
                with dve.If(i < n_items - 1):
                    for u in range(2):
                        lo(MOE0 + N_FF + u, i)
            y_part(n_items + 1)
            for r in range(4):
                add_quad(r, n_items * 4 + (r + 1))
            norm(4)

        @block.tensor
        def _(pe):
            def unit(n, item=None):
                if item is None:
                    pe.wait_ge(hi_ready, n + 1)
                    pe.wait_ge(lo_ready, n + 1)
                else:
                    pe.wait_ge(hi_ready, item * N_FF + (n + 1))
                    pe.wait_ge(lo_ready, item * N_FF + (n + 1))
                return w_hi[:, n % RING, :], w_lo[:, n % RING, :]

            def channels_unit(n, bank, a_hi, a_lo):
                hi, lo = (w.rearrange("p (k c) -> p k c", k=KD) for w in unit(n))
                for f in range(2):
                    dst = bank[:, T * f:T * (f + 1)]
                    for k in range(KD):
                        cols = slice(P * f, P * (f + 1))
                        pe.matmul(dst, lo[:, k, cols], a_hi[:, k, :], start=(k == 0), stop=False)
                        pe.matmul(dst, hi[:, k, cols], a_hi[:, k, :], start=False, stop=False)
                        ins = pe.matmul(dst, hi[:, k, cols], a_lo[:, k, :], start=False, stop=(k == KD - 1))
                ins.then_inc(unit_used, 1)

            def tokens_unit(n, bank, a_hi, a_lo):
                hi, lo = (w.rearrange("p (k c) -> p k c", k=KD) for w in unit(n))
                for t in range(TT):
                    dst = bank[:, 256 * t:256 * (t + 1)]
                    for k in range(KD):
                        tok = slice(P * t, P * (t + 1))
                        pe.matmul(dst, a_hi[:, k, tok], hi[:, k, :], start=(k == 0), stop=False)
                        pe.matmul(dst, a_hi[:, k, tok], lo[:, k, :], start=False, stop=False)
                        ins = pe.matmul(dst, a_lo[:, k, tok], hi[:, k, :], start=False, stop=(k == KD - 1))
                ins.then_inc(unit_used, 1)

            def down_unit(n, a_hi, a_lo, k0, first, last):
                hi, lo = (w.rearrange("p (k c) -> p k c", k=2) for w in unit(n))
                for k in range(2):
                    for t in range(TT):
                        tok = slice(P * t, P * (t + 1))
                        for a, w, s, e in ((a_hi, hi, True, False), (a_hi, lo, False, False), (a_lo, hi, False, True)):
                            for half in range(2):
                                ins = pe.matmul(YB[:, 2 * t + half, :], a[:, k0 + k, tok], w[:, k, HALF * half:HALF * (half + 1)],
                                                start=(first and k == 0 and s), stop=(last and k == 1 and e))
                ins.then_inc(unit_used, 1)

            def turn_h(j):
                pe.wait_ge(normed, j + 1)
                for q in range(4):
                    t, g = divmod(q, 2)
                    for k in range(4):
                        ins = pe.transpose(WB[q][:, P * k:P * (k + 1)], h[:, t, P * (4 * g + k):P * (4 * g + k + 1)], ident[:])
                    ins.then_inc(h_turned, 1)
                pe.wait_ge(t_hi_ready, 4 * (j + 1))
                pe.wait_ge(t_lo_ready, 4 * (j + 1))

            def mixer(l):
                b = BASE[l]
                turn_h(2 * l)
                for t in range(TT):
                    tok = slice(P * t, P * (t + 1))
                    for k in range(KD):
                        dst = YB[:, 3, RANK * t:RANK * (t + 1)]
                        pe.matmul(dst, t_hi[:, k, tok], gr_hi[:, l, k, :], start=(k == 0), stop=False)
                        pe.matmul(dst, t_hi[:, k, tok], gr_lo[:, l, k, :], start=False, stop=False)
                        ins = pe.matmul(dst, t_lo[:, k, tok], gr_hi[:, l, k, :], start=False, stop=(k == KD - 1))
                ins.then_inc(gr_done, 1)
                channels_unit(b + 0, WB[0], t_hi, t_lo)
                pe.wait_ge(gr_copied, l + 1)
                for t in range(TT):
                    ins = pe.transpose(YB[0:RANK, 1, P * t:P * (t + 1)], gr_s[:, t, :], ident[:])
                ins.then_inc(grT_done, 1)
                channels_unit(b + 1, WB[1], t_hi, t_lo)
                pe.wait_ge(grT_copied, l + 1)
                for k in range(KT):
                    ins = pe.matmul(YB[:, 2, T * k:T * (k + 1)], wgu[:, l, P * k:P * (k + 1)], gr_t[:], start=True, stop=True)
                ins.then_inc(logit_done, 1)
                channels_unit(b + 2, WB[2], t_hi, t_lo)
                channels_unit(b + 3, WB[3], t_hi, t_lo)
                pe.wait_ge(cu_ready, 2 * l + 1)
                channels_unit(b + U_Q, WB[0], t_hi, t_lo)
                channels_unit(b + U_K, WB[1], t_hi, t_lo)
                pe.wait_ge(cu_ready, 2 * l + 2)
                tokens_unit(b + U_V, WB[2], t_hi, t_lo)

                def level(n):
                    if n < 8:
                        pe.wait_ge(qE_ready, 8 * l + n + 1)
                        pe.wait_ge(kE_ready, 8 * l + n + 1)
                        src = qkE
                    else:
                        src = qk
                    if n == 0:
                        pe.wait_ge(gate_min, l + 1)
                    if n >= 2:
                        pe.wait_ge(level_read, 2 * (9 * l + n - 1))
                    for r in range(2):
                        rows = slice(DK * r, DK * (r + 1))
                        bank = YB[:, 2 * (n % 2) + r, :]
                        if n == 0:
                            pairs = [(hp, hp, slice(0, P), slice(P, T)) for hp in range(2)]
                        else:
                            pairs = [(2 * t + hp, hp, slice(P * t, P * (t + 1)), slice(P * t, P * (t + 1))) for t in range(TT) for hp in range(2)]
                        for place, hp, js, is_ in pairs:
                            ins = pe.matmul(bank[:, P * place:P * (place + 1)], src[rows, 1, hp, js], src[rows, 0, hp, is_],
                                            start=True, stop=True)
                    ins.then_inc(level_done, 1)

                level(0)
                tokens_unit(b + U_V + 1, WB[3], t_hi, t_lo)
                level(1)
                pe.wait_ge(qk_ready, 2 * (l + 1))
                channels_unit(b + U_G, WB[0], t_hi, t_lo)
                level(2)
                channels_unit(b + U_G + 1, WB[1], t_hi, t_lo)
                for n in range(3, 9):
                    level(n)
                pe.wait_ge(level_read, 2 * 9 * (l + 1))
                pe.wait_ge(v_ready, 2 * (l + 1))
                for hd in range(HEADS):
                    hp, r = divmod(hd, 2)
                    o = YB[:, hd // 2, T * (hd % 2):T * (hd % 2) + T]
                    vs = slice(DV * hd, DV * (hd + 1))
                    pe.matmul(o[:, 0:P], v[:, 0, vs], att[:, r, hp, :], start=True, stop=True)
                    pe.matmul(o[:, P:T], v[:, 0, vs], attx[:, r, hp, :], start=True, stop=False)
                    ins = pe.matmul(o[:, P:T], v[:, 1, vs], att[:, r, 2 + hp, :], start=False, stop=True)
                ins.then_inc(o_done, 1)
                pe.wait_ge(o_squared, l + 1)
                for g in range(2):
                    ins = pe.matmul(YB[:, 2 + g, :], ones[:], o_sq[:, 512 * g:512 * (g + 1)], start=True, stop=True)
                ins.then_inc(o_summed, 1)
                pe.wait_ge(conv_step, CT * TAPS * (l + 1))
                for c in range(CT):
                    ins = pe.matmul(WB[2][:, 0:T], ones[:], acc[:, c, :], start=(c == 0), stop=(c == CT - 1))
                ins.then_inc(c_summed, 1)
                pe.wait_ge(c_squared, l + 1)
                for c in range(CT):
                    ins = pe.matmul(WB[3][:, 0:T], ones[:], c_sq[:, T * c:T * (c + 1)], start=(c == 0), stop=(c == CT - 1))
                ins.then_inc(c_varied, 1)
                pe.wait_ge(mix_hi, l + 1)
                pe.wait_ge(mix_lo, l + 1)
                for j in range(N_OUT):
                    if j == HEADS // 2:
                        pe.wait_ge(c_hi, l + 1)
                        pe.wait_ge(c_lo, l + 1)
                    down_unit(b + N_IN + j, t_hi, t_lo, 2 * j, j == 0, j == N_OUT - 1)

            pe.wait_ge(pool_step, 2)
            pe.wait_ge(rows_ready, 16 * 6 * L)
            for l in range(L):
                pe.transpose(WB[l][:, 0:TAPS * CT], tap_rows[0:TAPS * CT, l, :], ident[0:TAPS * CT, 0:TAPS * CT]).then_inc(turned_rows, 1)
            pe.transpose(WB[2][:, 0:L * NPV], pv_rows[0:L * NPV, :], ident[0:L * NPV, 0:L * NPV]).then_inc(turned_rows, 1)
            pe.wait_ge(params_ready, 1)
            pe.wait_ge(small_hi, 3)
            pe.wait_ge(small_lo, 3)
            mixer(0)

            turn_h(1)
            n = DENSE0
            for c in range(CHUNKS + 1):
                if c < CHUNKS:
                    if c >= 2:
                        pe.wait_ge(dact_ready, c - 1)
                    channels_unit(n, WB[c % 2], t_hi, t_lo)
                    channels_unit(n + 1, WB[2 + c % 2], t_hi, t_lo)
                    n += 2
                if c:
                    if c == 1:
                        pe.wait_ge(added, 1)
                    pe.wait_ge(dT_hi_ready, c)
                    pe.wait_ge(dT_lo_ready, c)
                    down_unit(n, dT_hi, dT_lo, 0, c == 1, c == CHUNKS)
                    n += 1
            mixer(1)

            turn_h(3)
            for t in range(TT):
                tok = slice(P * t, P * (t + 1))
                for k in range(KD):
                    dst = YB[:, 0, NE * t:NE * (t + 1)]
                    pe.matmul(dst, t_hi[:, k, tok], rt_hi[:, k, :], start=(k == 0), stop=False)
                    pe.matmul(dst, t_hi[:, k, tok], rt_lo[:, k, :], start=False, stop=False)
                    ins = pe.matmul(dst, t_lo[:, k, tok], rt_hi[:, k, :], start=False, stop=(k == KD - 1))
            ins.then_inc(logits_done, 1)
            pe.wait_ge(choice_ready, 1)
            ch = rout[:, 7]
            pe.matmul(YB[:, 1, 0:NE], before[:], ch[:, 0, :], start=True, stop=True)
            pe.matmul(YB[:, 1, NE:2 * NE], ones[:], ch[:, 0, :], start=True, stop=False)
            pe.matmul(YB[:, 1, NE:2 * NE], before[:], ch[:, 1, :], start=False, stop=True)
            pe.matmul(YB[:, 1, 2 * NE:3 * NE], ones[:], ch[:, 0, :], start=True, stop=False)
            pe.matmul(YB[:, 1, 2 * NE:3 * NE], ones[:], ch[:, 1, :], start=False, stop=True).then_inc(places_done, 1)

            h_hi = t_hi[:].rearrange("p a b -> p (a b)").rearrange("p (t d) -> p t d", t=TT)
            h_lo = t_lo[:].rearrange("p a b -> p (a b)").rearrange("p (t d) -> p t d", t=TT)

            def gather(g):
                for k in range(4):
                    dst = YB[:, 2, P * k:P * (k + 1)]
                    cs = slice(P * (4 * g + k), P * (4 * g + k + 1))
                    for t in range(TT):
                        pe.matmul(dst, h_hi[:, t, cs], sel[:, t, :], start=(t == 0), stop=False)
                        ins = pe.matmul(dst, h_lo[:, t, cs], sel[:, t, :], start=False, stop=(t == TT - 1))
                ins.then_inc(gathered, 1)

            def scatter(r):
                t, half = divmod(r, 2)
                cs = slice(HALF * half, HALF * (half + 1))
                pe.matmul(YB[:, 2, :], selT[:, t, :], y_hi[:, cs], start=True, stop=False)
                pe.matmul(YB[:, 2, :], selT[:, t, :], y_lo[:, cs], start=False, stop=True).then_inc(scattered, 1)

            pe.wait_ge(h_hi_ready, 1)
            pe.wait_ge(h_lo_ready, 1)
            pe.wait_ge(sel_ready, 1)
            gather(0)
            pe.wait_ge(staged, 1)
            gather(1)
            pe.wait_ge(meta_ready, 1)
            n_items = pe.value_load(meta[0:1, 0:1], min_val=NE, max_val=ITEMS)
            with pe.Fori(0, n_items) as i:
                pe.wait_ge(xs_hi_ready, i + 1)
                pe.wait_ge(xs_lo_ready, i + 1)
                for u, (what, c, part) in enumerate(plan):
                    hi, lo = unit(MOE0 + u, i)
                    if what != "down":
                        width, nk = (512, 4) if c < EC - 1 else (256, 8)
                        k0 = 4 * part
                        hi, lo = (w.rearrange("p (k c) -> p k c", k=nk) for w in (hi, lo))
                        bank = WB[(0 if what == "gate" else 2) + c % 2][:, 0:width]
                        for k in range(nk):
                            start, stop = k0 + k == 0, k0 + k == KD - 1
                            pe.matmul(bank, xs_hi[:, k0 + k, :], hi[:, k, :], start=start, stop=False)
                            pe.matmul(bank, xs_hi[:, k0 + k, :], lo[:, k, :], start=False, stop=False)
                            ins = pe.matmul(bank, xs_lo[:, k0 + k, :], hi[:, k, :], start=False, stop=stop)
                    else:
                        if part == 0:
                            pe.wait_ge(eT_hi_ready, i * EC + (c + 1))
                            pe.wait_ge(eT_lo_ready, i * EC + (c + 1))
                        hi, lo = (w.rearrange("p (k c) -> p k c", k=2) for w in (hi, lo))
                        for k in range(2):
                            f = 2 * part + k
                            first, last = c == 0 and f == 0, c == EC - 1 and k == 1
                            for a, w, s, e in ((eT_hi, hi, True, False), (eT_hi, lo, False, False), (eT_lo, hi, False, True)):
                                for half in range(2):
                                    ins = pe.matmul(YB[:, half, :], a[:, f, :], w[:, k, HALF * half:HALF * (half + 1)],
                                                    start=(first and s), stop=(last and e))
                    ins.then_inc(unit_used, 1)
                    if u in SCATTER:
                        r = SCATTER.index(u)
                        if r == 0:
                            pe.wait_ge(y_hi_ready, i + 1)
                            pe.wait_ge(y_lo_ready, i + 1)
                            pe.wait_ge(staged, i * 2 + 2)
                        else:
                            pe.wait_ge(quad_added, i * 4 + (r + 1))
                        scatter(r)
                    if u in TURN:
                        tc = TURN.index(u)
                        pe.wait_ge(eact_ready, i * EC + (tc + 2))
                        for f in range(4 if tc < EC - 1 else 2):
                            ins = pe.transpose(YB[:, 3, P * f:P * (f + 1)], eact[:, P * f:P * (f + 1)], ident[:])
                        ins.then_inc(eT_done, 1)
                    if u == TURN_SEL:
                        pe.wait_ge(quad_added, i * 4 + 5)
                        for t in range(TT):
                            pe.transpose(YB[:, 2, P * t:P * (t + 1)], sel[:, t, :].bitcast(F32), ident[:])
                        for t in range(TT):
                            ins = pe.matmul(YB[:, 2, TT * P:TT * P + 1], sel[:, t, :].bitcast(F32), cur[:, 1, t:t + 1],
                                            start=(t == 0), stop=(t == TT - 1))
                        ins.then_inc(selT_done, 1)
                    if u in GATHER:
                        g = GATHER.index(u)
                        if g == 0:
                            pe.wait_ge(selT_ready, i + 1)
                            pe.wait_ge(sel_ready, i + 2)
                        else:
                            pe.wait_ge(staged, i * 2 + 3)
                        gather(g)
            pe.wait_ge(y_hi_ready, n_items + 1)
            pe.wait_ge(y_lo_ready, n_items + 1)
            pe.wait_ge(staged, n_items * 2 + 2)
            for r in range(4):
                if r:
                    pe.wait_ge(quad_added, n_items * 4 + (r + 1))
                scatter(r)


_INS = ['x', 'ln1_w', 'w_in', 'w_gate_up', 'b_gate', 'gla_norm_w', 'conv_w', 'conv_b', 'cn_w', 'cn_b', 'w_out',
        'ln2_w', 'wd_gate', 'wd_up', 'wd_down', 'w_router', 'we_gate', 'we_up', 'we_down', 'final_norm_w']


def kernel(**inputs):
    import numpy as np
    import concourse.bacc as bacc
    from concourse.bass_utils import run_bass_kernel_spmd

    nc = bacc.Bacc("TRN2", target_bir_lowering=False, num_devices=1)
    arrays, args = {}, []
    for name in _INS:
        a = np.ascontiguousarray(inputs[name])
        arrays[f"in_{name}"] = a
        args.append(nc.dram_tensor(f"in_{name}", a.shape, mybir.dt.from_np(a.dtype), kind="ExternalInput").ap())
    out = nc.dram_tensor("out", inputs["x"].shape, F32, kind="ExternalOutput").ap()
    trunk(nc, *args, out)
    r = run_bass_kernel_spmd(nc, [arrays], core_ids=[0])
    return r.results[0]["out"]
```

```python
from contextlib import ExitStack

import concourse.bass as bass
from concourse import mybir

F32 = mybir.dt.float32
F32R = mybir.dt.float32r
I32 = mybir.dt.int32
U8 = mybir.dt.uint8
ALU = mybir.AluOpType
ACT = mybir.ActivationFunctionType
AX = mybir.AxisListType.X

P = 128
UNIT = 2048
RAW = 11
RING = 3
EPS = 1e-6
NEG = -3.0e38


def trunk(nc, x, ln1_w, w_in, w_gate_up, b_gate, gla_norm_w, conv_w, conv_b, cn_w, cn_b, w_out,
          ln2_w, wd_gate, wd_up, wd_down, w_router, we_gate, we_up, we_down, final_norm_w, out):
    _, T, D = x.shape
    L, _, IN_COLS = w_in.shape
    RANK, KEY = w_gate_up.shape[1:]
    DV = gla_norm_w.shape[1]
    TAPS, CH = conv_w.shape[1:]
    VAL = w_out.shape[1] - CH
    HEADS = VAL // DV
    DK = KEY // HEADS
    FF = wd_gate.shape[2]
    NE = w_router.shape[2]
    TT, KD, CT, KT = T // P, D // P, CH // P, KEY // P
    HALF = D // 2
    assert (T, D, DK, DV, KEY, L) == (256, 1024, 64, P, 256, 2) and FF % 512 == 256 and NE == 8

    OFF_V, OFF_G = 2 * KEY, 2 * KEY + VAL
    OFF_R = OFF_G + VAL
    OFF_CA, OFF_CB = OFF_R + RANK, OFF_R + RANK + CH
    IN_UNITS = [OFF_CA, OFF_CB, OFF_CA + 256, OFF_CB + 256, 0, KEY, OFF_V, OFF_V + 256, OFF_G, OFF_G + 256]
    U_Q, U_K, U_V, U_G = 4, 5, 6, 8
    N_IN, N_OUT = len(IN_UNITS), w_out.shape[1] // 256
    N_MIX = N_IN + N_OUT
    CHUNKS = FF // 256
    N_FF = 3 * CHUNKS
    BASE = [0, N_MIX + N_FF]
    DENSE0 = N_MIX
    MOE0 = BASE[1] + N_MIX
    assert N_FF % RAW == 0 and N_FF % RING == 0

    EC = FF // 512 + 1
    plan = []
    for c in range(EC):
        parts = 2 if c < EC - 1 else 1
        plan += [("gate", c, p) for p in range(parts)] + [("up", c, p) for p in range(parts)]
        if c:
            plan += [("down", c - 1, 0), ("down", c - 1, 1)]
    plan += [("down", EC - 1, 0)]
    assert len(plan) == N_FF
    at = {what: u for u, what in enumerate(plan)}
    GATE_END = [at["gate", c, 1 if c < EC - 1 else 0] for c in range(EC)]
    UP_END = [at["up", c, 1 if c < EC - 1 else 0] for c in range(EC)]
    TURN = [GATE_END[c + 1] for c in range(EC - 1)] + [at["down", EC - 2, 0]]
    SCATTER = [2, 3, 4, 5]
    TURN_SEL, GATHER = 10, [16, 18]
    LAST_UP = UP_END[EC - 1]
    EXTRA = (2 * T) // (P + 1)
    ITEMS = NE + EXTRA

    ctx = ExitStack()
    with ctx:
        def sem(name):
            return ctx.enter_context(nc.semaphore(name))

        def on(stack):
            return lambda name, shape, dt=F32: stack.enter_context(nc.sbuf_tensor(name, shape, dt))

        sb = on(ctx)
        raw = sb("raw", [P, RAW, UNIT])
        w_hi = sb("w_hi", [P, RING, UNIT], F32R)
        w_lo = sb("w_lo", [P, RING, UNIT], F32R)
        X = sb("X", [P, TT, D])
        t_hi = sb("t_hi", [P, KD, T], F32R)
        t_lo = sb("t_lo", [P, KD, T], F32R)
        lnw = sb("lnw", [P, D])
        ident = sb("ident", [P, P])
        ones = sb("ones", [P, P])
        before = sb("before", [P, P])
        slot_no = sb("slot_no", [P, P])
        masks = sb("masks", [P, 8, P], U8)
        taps = sb("taps", [P, L, TAPS, CT])
        NPV = KT + 3 * CT + 1
        pv = sb("pv", [P, L, NPV])
        gr_hi = sb("gr_hi", [P, L, KD, RANK], F32R)
        gr_lo = sb("gr_lo", [P, L, KD, RANK], F32R)
        wgu = sb("wgu", [RANK, L, KEY])
        rt_hi = sb("rt_hi", [P, KD, NE], F32R)
        rt_lo = sb("rt_lo", [P, KD, NE], F32R)
        eps = sb("eps", [P, 1])
        ss = sb("ss", [P, TT])
        rstd = sb("rstd", [P, TT])
        slot_of = sb("slot_of", [P, ITEMS + 1, TT])
        gate_of = sb("gate_of", [P, ITEMS + 1, TT])
        meta = sb("meta", [P, 1 + EXTRA + 1], I32)
        number = sb("number", [P, EXTRA, NE])
        idle = sb("idle", [P, 4])

        s0 = ExitStack()
        sc = on(s0)
        sc("beside_h", [P, TT, D])
        tap_rows = sc("tap_rows", [P, L, P])
        pv_rows = sc("pv_rows", [P, P])
        gr_raw = sc("gr_raw", [P, L, KD, RANK])
        rt_raw = sc("rt_raw", [P, KD, NE])
        sc("beside_cu", [P, 2880])
        mask_f = sc("mask_f", [P, 8, P])
        s0.close()

        s1 = ExitStack()
        h = on(s1)("h", [P, TT, D])
        s1.close()

        s2 = ExitStack()
        sm = on(s2)
        qk = sm("qk", [P, 2, KT, T])
        o_sq = qk[:].rearrange("p a k t -> p (a k t)")
        qkE = sm("qkE", [P, 2, KT, T])
        cgate = qkE[:, 0]
        Difs = sm("Difs", [P, 2, KT, T])
        cum = sm("cum", [P, KT, T])
        att = sm("att", [P, 2, 2 * TT, P])
        og = att[:].rearrange("p r a i -> p (r a i)")
        attx = sm("attx", [P, 2, 2, P])
        v = sm("v", [P, TT, VAL])
        PAD = TAPS - 1
        cu = sm("cu", [P, CT, PAD + T])
        c_sq = cu[:].rearrange("p c t -> p (c t)")[:, 0:CT * T]
        acc = sm("acc", [P, CT, T])
        gr_t = sm("gr_t", [RANK, T])
        gr_s = sm("gr_s", [P, TT, RANK])
        o_ss = sm("o_ss", [P, TT * HEADS])
        s2.close()

        s3 = ExitStack()
        sd = on(s3)
        dg = sd("dg", [P, 512])
        dact = sd("dact", [P, 512])
        dT_hi = sd("dT_hi", [P, 2, T], F32R)
        dT_lo = sd("dT_lo", [P, 2, T], F32R)
        s3.close()

        s4 = ExitStack()
        se = on(s4)
        se("beside_h4", [P, TT, D])
        stage = se("stage", [P, KD, P])
        xs_hi, y_hi = (t_hi[:].rearrange("p a b -> p (a b)")[:, D * k:D * (k + 1)] for k in range(2))
        xs_lo, y_lo = (t_lo[:].rearrange("p a b -> p (a b)")[:, D * k:D * (k + 1)] for k in range(2))
        xs_hi, xs_lo = (a.rearrange("p (k j) -> p k j", j=P) for a in (xs_hi, xs_lo))
        eg = se("eg", [P, 512])
        eact = se("eact", [P, 512])
        eT_hi = se("eT_hi", [P, 4, P], F32R)
        eT_lo = se("eT_lo", [P, 4, P], F32R)
        sel = se("sel", [P, TT, P])
        selT = se("selT", [P, TT, P], F32R)
        cur = se("cur", [P, 2, TT])
        slot_gate = se("slot_gate", [P, 1])
        started = se("started", [P, 2])
        rout = se("rout", [P, 24, TT, NE])
        s4.close()

        YB = ctx.enter_context(nc.psum_tensor("YB", [P, 4, 512], F32))
        WB = [ctx.enter_context(nc.psum_tensor(f"WB{i}", [P, 512], F32)) for i in range(4)]

        raw_ready = [sem(f"raw_ready{i}") for i in range(RAW)]
        x_ready, rows_ready, lnw_ready = sem("x_ready"), sem("rows_ready"), sem("lnw_ready")
        small_ready = sem("small_ready")
        hi_ready, lo_ready, unit_used = sem("hi_ready"), sem("lo_ready"), sem("unit_used")
        pool_step, consts_ready, turned_rows, params_ready = sem("pool_step"), sem("consts_ready"), sem("turned_rows"), sem("params_ready")
        small_hi, small_lo = sem("small_hi"), sem("small_lo")
        squared, rooted, inverted, normed = sem("squared"), sem("rooted"), sem("inverted"), sem("normed")
        h_turned, t_hi_ready, t_lo_ready = sem("h_turned"), sem("t_hi_ready"), sem("t_lo_ready")
        added = sem("added")
        gr_done, gr_copied, grT_done, grT_copied, logit_done = (sem(s) for s in ("gr_done", "gr_copied", "grT_done", "grT_copied", "logit_done"))
        cgate_ready, cu_ready, conv_step, pads_ready = (sem(s) for s in ("cgate_ready", "cu_ready", "conv_step", "pads_ready"))
        gate_abs, gate_exp, gate_ln, gate_min, gate_sub, cum_ready = (sem(s) for s in ("gate_abs", "gate_exp", "gate_ln", "gate_min", "gate_sub", "cum_ready"))
        qk_ready, v_ready = sem("qk_ready"), sem("v_ready")
        dif_ready, decay_ready, qE_ready, kE_ready, level_done, level_read = (sem(s) for s in (
            "dif_ready", "decay_ready", "qE_ready", "kE_ready", "level_done", "level_read"))
        o_done, o_squared, o_summed, o_rooted, o_inverted, og_ready, o_gated, o_turned, mix_hi, mix_lo = (sem(s) for s in (
            "o_done", "o_squared", "o_summed", "o_rooted", "o_inverted", "og_ready", "o_gated", "o_turned", "mix_hi", "mix_lo"))
        c_summed, c_centred, c_squared, c_varied, c_rooted, c_inverted, c_scaled, c_silu, c_hi, c_lo = (sem(s) for s in (
            "c_summed", "c_centred", "c_squared", "c_varied", "c_rooted", "c_inverted", "c_scaled", "c_silu", "c_hi", "c_lo"))
        dgate_ready, dact_ready, dT_hi_ready, dT_lo_ready = (sem(s) for s in ("dgate_ready", "dact_ready", "dT_hi_ready", "dT_lo_ready"))
        logits_done, route_step, lead_exp, choice_ready, places_done, tables_ready, meta_ready, lead_ready = (sem(s) for s in (
            "logits_done", "route_step", "lead_exp", "choice_ready", "places_done", "tables_ready", "meta_ready", "lead_ready"))
        cur_ready, sel_ready, gathered, staged, xs_hi_ready, xs_lo_ready = (sem(s) for s in (
            "cur_ready", "sel_ready", "gathered", "staged", "xs_hi_ready", "xs_lo_ready"))
        egate_ready, eact_ready, eT_done, eT_hi_ready, eT_lo_ready = (sem(s) for s in (
            "egate_ready", "eact_ready", "eT_done", "eT_hi_ready", "eT_lo_ready"))
        y_zeroed, y_hi_ready, y_lo_ready, scattered, quad_added, selT_done, selT_ready = (sem(s) for s in (
            "y_zeroed", "y_hi_ready", "y_lo_ready", "scattered", "quad_added", "selT_done", "selT_ready"))
        out_stored = sem("out_stored")

        block = ctx.enter_context(nc.Block())

        LEVELS = [P, 64, 32, 16, 8, 4, 2, 1, 0]
        PV_BG, PV_CB, PV_CW, PV_CBB, PV_GN = 0, KT, KT + CT, KT + 2 * CT, KT + 3 * CT

        def slot_use(n):
            return n % RAW, n // RAW + 1

        wg_v = we_gate[0].rearrange("e (k p) f -> e p k f", p=P)
        wu_v = we_up[0].rearrange("e (k p) f -> e p k f", p=P)
        wd_v = we_down[0].rearrange("e (k p) n -> e p k n", p=P)

        @block.sync
        def _(sp):
            def small(l):
                sp.dma_start(gr_raw[:, l], w_in[l, :, OFF_R:OFF_R + RANK].rearrange("(k p) c -> p k c", p=P)).then_inc(small_ready, 16)
                sp.dma_start(tap_rows[0:TAPS * CT, l, :], conv_w[l].rearrange("w (c p) -> (w c) p", p=P)).then_inc(rows_ready, 16)
                for src, at0, k in ((b_gate, PV_BG, KT), (conv_b, PV_CB, CT), (cn_w, PV_CW, CT), (cn_b, PV_CBB, CT), (gla_norm_w, PV_GN, 1)):
                    r = l * NPV + at0
                    sp.dma_start(pv_rows[r:r + k, :], src[l].rearrange("(c p) -> c p", p=P)).then_inc(rows_ready, 16)

            for t in range(TT):
                sp.dma_start(X[:, t, :], x[0, P * t:P * (t + 1), :]).then_inc(x_ready, 16)

            def load(n, src, k):
                slot, _ = slot_use(n)
                if n >= RAW:
                    sp.wait_ge(lo_ready, n - RAW + 1)
                sp.dma_start(raw[:, slot, :].rearrange("p (k c) -> p k c", k=k), src).then_inc(raw_ready[slot], 16)

            def load_mixer(l):
                for j, c0 in enumerate(IN_UNITS):
                    load(BASE[l] + j, w_in[l, :, c0:c0 + 256].rearrange("(k p) c -> p k c", p=P), 8)
                    if l == 0 and j == 0:
                        for layer in range(L):
                            small(layer)
                        sp.dma_start(wgu[:], w_gate_up.rearrange("l r c -> r l c")).then_inc(small_ready, 16)
                        sp.dma_start(rt_raw[:], w_router[0].rearrange("(k p) e -> p k e", p=P)).then_inc(small_ready, 16)
                for j in range(N_OUT):
                    load(BASE[l] + N_IN + j, w_out[l, 256 * j:256 * (j + 1), :].rearrange("(k p) n -> p k n", p=P), 2)

            load_mixer(0)
            n = DENSE0
            for c in range(CHUNKS + 1):
                if c < CHUNKS:
                    load(n, wd_gate[0, :, 256 * c:256 * (c + 1)].rearrange("(k p) f -> p k f", p=P), 8)
                    load(n + 1, wd_up[0, :, 256 * c:256 * (c + 1)].rearrange("(k p) f -> p k f", p=P), 8)
                    n += 2
                if c:
                    load(n, wd_down[0, 256 * (c - 1):256 * c, :].rearrange("(k p) n -> p k n", p=P), 2)
                    n += 1
            load_mixer(1)

            def load_expert(e, item):
                for u, (what, c, part) in enumerate(plan):
                    slot, _ = slot_use(MOE0 + u)
                    sp.wait_ge(lo_ready, item * N_FF + (MOE0 + u - RAW + 1))
                    if what == "down":
                        k0 = 4 * c + 2 * part
                        src, k = wd_v[e, :, k0:k0 + 2, :], 2
                    else:
                        w = wg_v if what == "gate" else wu_v
                        if c < EC - 1:
                            src, k = w[e, :, 4 * part:4 * part + 4, 512 * c:512 * (c + 1)], 4
                        else:
                            src, k = w[e, :, :, 512 * c:FF], 8
                    sp.dma_start(raw[:, slot, :].rearrange("p (k c) -> p k c", k=k), src).then_inc(raw_ready[slot], 16)

            with sp.Fori(0, NE) as e:
                load_expert(e, e)
            sp.wait_ge(meta_ready, 1)
            n_items = sp.value_load(meta[0:1, 0:1], min_val=NE, max_val=ITEMS)
            with sp.If(n_items > NE):
                with sp.Fori(NE, n_items) as item:
                    e = sp.value_load(meta[0:1, bass.ds(item - (NE - 1), 1)], min_val=0, max_val=NE - 1)
                    load_expert(e, item)

            for t in range(TT):
                sp.wait_ge(normed, 4 * TT + t + 1)
                sp.dma_start(out[0, P * t:P * (t + 1), :], h[:, t, :]).then_inc(out_stored, 16)
            sp.wait_ge(out_stored, 16 * TT)

        norm_weights = [ln1_w[0], ln2_w[0], ln1_w[1], ln2_w[1], final_norm_w]

        @block.gpsimd
        def _(pool):
            pool.dma_start(lnw[:], norm_weights[0].partition_broadcast(P)).then_inc(lnw_ready, 16)
            steps = [0]

            def step(ins):
                steps[0] += 1
                ins.then_inc(pool_step, 1)
                pool.wait_ge(pool_step, steps[0])

            step(pool.memset(ident[:], 0.0))
            step(pool.affine_select(out=ident[:], in_=ident[:], compare_op=ALU.not_equal, fill=1.0, base=0,
                                    pattern=[[-1, P]], channel_multiplier=1))
            step(pool.memset(eps[:], EPS))
            step(pool.memset(ones[:], 1.0))
            pool.affine_select(out=before[:], in_=ones[:], compare_op=ALU.is_gt, fill=0.0, base=0,
                               pattern=[[1, P]], channel_multiplier=-1).then_inc(consts_ready, 1)
            pool.iota(slot_no[:], pattern=[[1, P]], base=0, channel_multiplier=0,
                      allow_small_or_imprecise_dtypes=True).then_inc(consts_ready, 1)
            step(pool.memset(mask_f[:], 0.0))
            for n, s in enumerate(LEVELS[1:]):
                if s:
                    m = mask_f[:, n, :].rearrange("p (b s) -> p b s", s=2 * s)[:, :, s:2 * s]
                    nb = P // (2 * s)
                    step(pool.memset(m, 1.0))
                    step(pool.affine_select(out=m, in_=m, compare_op=ALU.is_ge, fill=0.0, base=0,
                                            pattern=[[-2 * s, nb], [0, s]], channel_multiplier=1))
                    step(pool.affine_select(out=m, in_=m, compare_op=ALU.is_ge, fill=0.0, base=s - 1,
                                            pattern=[[2 * s, nb], [0, s]], channel_multiplier=-1))
                else:
                    step(pool.tensor_copy(mask_f[:, n, :], ident[:]))
            step(pool.tensor_copy(masks[:], mask_f[:]))
            pool.memset(slot_of[:, ITEMS, :], -1.0).then_inc(consts_ready, 1)
            pool.memset(gate_of[:, ITEMS, :], 0.0).then_inc(consts_ready, 1)
            for k in range(EXTRA):
                pool.memset(number[:, k, :], float(k + 1)).then_inc(consts_ready, 1)

            for l in range(L):
                if l == 0:
                    pool.wait_ge(params_ready, 1)
                    pool.wait_ge(small_lo, 3)
                else:
                    pool.wait_ge(added, 2 * TT)
                pool.memset(cu[:, :, 0:PAD], 0.0).then_inc(pads_ready, 1)
                pool.memset(att[:], 0.0).then_inc(pads_ready, 1)
                pool.wait_ge(normed, TT * (2 * l + 1))
                pool.dma_start(lnw[:], norm_weights[2 * l + 1].partition_broadcast(P)).then_inc(lnw_ready, 16)
                for n in range(len(LEVELS) - 1):
                    pool.wait_ge(decay_ready, 8 * l + n + 1)
                    if n:
                        pool.wait_ge(level_done, 9 * l + n)
                    pool.tensor_tensor(qkE[:, 1], qk[:, 1], Difs[:, n % 2], ALU.mult).then_inc(kE_ready, 1)
                pool.wait_ge(normed, TT * (2 * l + 2))
                pool.dma_start(lnw[:], norm_weights[2 * l + 2].partition_broadcast(P)).then_inc(lnw_ready, 16)

        @block.scalar
        def _(act):
            def hi(n, item=None):
                slot, use = slot_use(n)
                if item is None:
                    act.wait_ge(raw_ready[slot], 16 * use)
                    if n >= RING:
                        act.wait_ge(unit_used, n - RING + 1)
                else:
                    act.wait_ge(raw_ready[slot], item * (16 * N_FF // RAW) + 16 * use)
                    act.wait_ge(unit_used, item * N_FF + (n - RING + 1))
                act.activation(w_hi[:, n % RING, :], raw[:, slot, :], ACT.Copy).then_inc(hi_ready, 1)

            def preload(func):
                act.activation(idle[:, 0:1], eps[:], func)

            def norm(j, ready, counts):
                preload(ACT.Sqrt)
                for t in range(TT):
                    act.wait_ge(ready, counts[t])
                    act.activation(h[:, t, :], X[:, t, :], ACT.Square, accum_out=ss[:, t:t + 1]).then_inc(squared, 1)
                for t in range(TT):
                    act.wait_ge(squared, TT * j + t + 1)
                    act.activation(rstd[:, t:t + 1], ss[:, t:t + 1], ACT.Sqrt, scale=1.0 / D, bias=eps[:]).then_inc(rooted, 1)

            def turned(j):
                for q in range(4):
                    t, g = divmod(q, 2)
                    act.wait_ge(h_turned, 4 * j + q + 1)
                    act.activation(t_hi[:, 4 * g:4 * g + 4, P * t:P * (t + 1)], WB[q][:].rearrange("p (k t) -> p k t", k=4),
                                   ACT.Copy).then_inc(t_hi_ready, 1)

            def after_unit(n):
                act.wait_ge(unit_used, n + 1)

            def mixer(l):
                b = BASE[l]
                turned(2 * l)
                hi(b + 3)
                for g in range(2):
                    after_unit(b + 2 * g + 1)
                    if g or l:
                        act.wait_ge(cu_ready, 2 * l + g)
                    act.activation(cgate.rearrange("p k t -> p (k t)"), WB[2 * g + 1][:], ACT.Sigmoid).then_inc(cgate_ready, 1)
                    hi(b + 4 + g)
                act.wait_ge(logit_done, l + 1)
                for k in range(KT):
                    act.activation(Difs[:, 0, k, :], YB[:, 2, T * k:T * (k + 1)], ACT.Abs,
                                   bias=pv[:, l, PV_BG + k:PV_BG + k + 1]).then_inc(gate_abs, 1)
                act.wait_ge(gate_abs, KT * (l + 1))
                act.activation(Difs[:, 0], Difs[:, 0], ACT.Exp, scale=-1.0).then_inc(gate_exp, 1)
                act.wait_ge(gate_exp, l + 1)
                act.activation(Difs[:, 0], Difs[:, 0], ACT.Ln, bias=1.0).then_inc(gate_ln, 1)
                hi(b + 6)
                after_unit(b + U_Q)
                act.activation(qk[:, 0].rearrange("p k t -> p (k t)"), WB[U_Q % 4][:], ACT.Copy, scale=DK ** -0.5).then_inc(qk_ready, 1)
                hi(b + 7)
                after_unit(b + U_K)
                act.activation(qk[:, 1].rearrange("p k t -> p (k t)"), WB[U_K % 4][:], ACT.Copy).then_inc(qk_ready, 1)

                def decays(n):
                    Dif = Difs[:, n % 2]
                    act.wait_ge(dif_ready, 8 * l + n + 1)
                    if n == 0:
                        act.activation(Dif[:, :, 0:P], Dif[:, :, 0:P], ACT.Exp, scale=1.0 / 16.0)
                        act.activation(Dif[:, :, P:T], cum[:, :, P:T], ACT.Exp, scale=1.0 / 16.0).then_inc(decay_ready, 1)
                    else:
                        act.activation(Dif, Dif, ACT.Exp, scale=1.0 / 16.0).then_inc(decay_ready, 1)

                def v_half(g):
                    after_unit(b + U_V + g)
                    act.activation(v[:, :, 256 * g:256 * (g + 1)], WB[(U_V + g) % 4][:].rearrange("p (t c) -> p t c", t=TT),
                                   ACT.Copy).then_inc(v_ready, 1)

                decays(0)
                decays(1)
                hi(b + 8)
                v_half(0)
                decays(2)
                decays(3)
                hi(b + 9)
                v_half(1)
                for n in range(4, 8):
                    decays(n)
                    if n < 7:
                        hi(b + N_IN + n - 4)
                act.wait_ge(o_done, l + 1)
                act.activation(o_sq, YB[:, 0:2, :].rearrange("p a c -> p (a c)"), ACT.Square).then_inc(o_squared, 1)
                for g in range(2):
                    after_unit(b + U_G + g)
                    act.activation(og[:, 512 * g:512 * (g + 1)], WB[g][:], ACT.Silu).then_inc(og_ready, 1)
                act.wait_ge(o_summed, l + 1)
                act.activation(o_ss[:], o_ss[:], ACT.Sqrt, scale=1.0 / DV, bias=eps[:]).then_inc(o_rooted, 1)
                act.wait_ge(o_turned, l + 1)
                act.activation(t_hi[:, 0:HEADS, :].rearrange("p h t -> p (h t)"), YB[:, 2:4, :].rearrange("p a c -> p (a c)"), ACT.Copy,
                               scale=pv[:, l, PV_GN:PV_GN + 1]).then_inc(mix_hi, 1)
                act.wait_ge(c_centred, l + 1)
                act.activation(c_sq, acc[:].rearrange("p c t -> p (c t)"), ACT.Square).then_inc(c_squared, 1)
                act.wait_ge(c_varied, l + 1)
                act.activation(Difs[:, 0, 0, :], WB[3][:, 0:T], ACT.Sqrt, scale=1.0 / CH, bias=eps[:]).then_inc(c_rooted, 1)
                preload(ACT.Silu)
                act.wait_ge(c_scaled, l + 1)
                for c in range(CT):
                    act.activation(c_sq.rearrange("p (c t) -> p c t", c=CT)[:, c, :], acc[:, c, :], ACT.Silu,
                                   scale=pv[:, l, PV_CW + c:PV_CW + c + 1], bias=pv[:, l, PV_CBB + c:PV_CBB + c + 1]).then_inc(c_silu, 1)
                act.wait_ge(c_silu, CT * (l + 1))
                act.activation(t_hi[:, HEADS:, :], c_sq.rearrange("p (c t) -> p c t", c=CT), ACT.Copy).then_inc(c_hi, 1)
                hi(b + N_IN + 3)

            act.wait_ge(small_ready, 16 * (L + 2))
            for l in range(L):
                act.activation(gr_hi[:, l], gr_raw[:, l], ACT.Copy).then_inc(small_hi, 1)
            act.activation(rt_hi[:], rt_raw[:], ACT.Copy).then_inc(small_hi, 1)
            act.wait_ge(pool_step, 3)
            act.wait_ge(small_lo, 3)
            act.wait_ge(params_ready, 1)
            norm(0, x_ready, [16, 32])
            for n in range(RING):
                hi(n)
            mixer(0)

            d0 = DENSE0
            hi(d0 + 0)
            hi(d0 + 1)
            norm(1, added, [1, 2])
            hi(d0 + 2)
            turned(1)

            def dense_gate(c, n):
                after_unit(n)
                if c:
                    act.wait_ge(dact_ready, c)
                act.activation(dg[:], WB[c % 2][:], ACT.Silu).then_inc(dgate_ready, 1)

            def dense_turn(c, n_free):
                if n_free is not None:
                    after_unit(n_free)
                act.wait_ge(dact_ready, c + 1)
                act.activation(dT_hi[:].rearrange("p f t -> p (f t)"), dact[:], ACT.Copy).then_inc(dT_hi_ready, 1)

            gate_at = [d0] + [d0 + 3 * c - 1 for c in range(1, CHUNKS)]
            down_at = [d0 + 3 * c + 4 for c in range(CHUNKS - 1)] + [d0 + N_FF - 1]
            done = 3
            for c in range(CHUNKS):
                while done < min(gate_at[c] + 3 - d0, N_FF):
                    hi(d0 + done)
                    done += 1
                dense_gate(c, gate_at[c])
                if done < N_FF:
                    hi(d0 + done)
                    done += 1
                dense_turn(c, down_at[c - 1] if c else None)
            for n in range(BASE[1], BASE[1] + 2):
                hi(n)
            norm(2, added, [3, 4])
            hi(BASE[1] + 2)
            mixer(1)

            for n in range(MOE0, MOE0 + 2):
                hi(n)
            norm(3, added, [5, 6])
            turned(3)
            preload(ACT.Exp)
            act.wait_ge(lead_ready, 1)
            act.activation(rout[:, 12, :, 1], rout[:, 12, :, 0], ACT.Exp).then_inc(lead_exp, 1)

            def stage_half(g, count):
                act.wait_ge(gathered, count)
                act.activation(stage[:, 4 * g:4 * g + 4, :], YB[:, 2, :].rearrange("p (k j) -> p k j", k=4), ACT.Copy).then_inc(staged, 1)

            for g in range(2):
                stage_half(g, g + 1)
            act.wait_ge(staged, 2)
            act.activation(xs_hi, stage[:], ACT.Copy).then_inc(xs_hi_ready, 1)
            act.wait_ge(meta_ready, 1)
            n_items = act.value_load(meta[0:1, 0:1], min_val=NE, max_val=ITEMS)

            def y_part():
                act.activation(y_hi, YB[:, 0:2, :].rearrange("p a c -> p (a c)"), ACT.Copy, scale=slot_gate[:]).then_inc(y_hi_ready, 1)

            act.wait_ge(y_zeroed, 1)
            with act.Fori(0, n_items) as i:
                for u in range(N_FF):
                    if u >= 2:
                        hi(MOE0 + u, i)
                    if u == 2:
                        act.wait_ge(unit_used, i * N_FF + MOE0)
                        y_part()
                    for c in range(EC):
                        if TURN[c] + 2 == u:
                            act.wait_ge(eT_done, i * EC + (c + 1))
                            w = 4 if c < EC - 1 else 2
                            act.activation(eT_hi[:, 0:w, :], YB[:, 3, 0:P * w].rearrange("p (f t) -> p f t", f=w), ACT.Copy).then_inc(eT_hi_ready, 1)
                        if GATE_END[c] + 2 == u:
                            act.wait_ge(unit_used, i * N_FF + (MOE0 + GATE_END[c] + 1))
                            act.wait_ge(eact_ready, i * EC + (c + 1))
                            w = 512 if c < EC - 1 else 256
                            act.activation(eg[:, 0:w], WB[c % 2][:, 0:w], ACT.Silu).then_inc(egate_ready, 1)
                    for g in range(2):
                        if GATHER[g] + 2 == u:
                            act.wait_ge(xs_lo_ready, i + 1)
                            stage_half(g, i * 2 + (3 + g))
                    if LAST_UP + 2 == u:
                        act.wait_ge(unit_used, i * N_FF + (MOE0 + LAST_UP + 1))
                        act.wait_ge(staged, i * 2 + 4)
                        act.activation(xs_hi, stage[:], ACT.Copy).then_inc(xs_hi_ready, 1)
                with act.If(i < n_items - 1):
                    for u in range(2):
                        hi(MOE0 + N_FF + u, i)
            act.wait_ge(unit_used, n_items * N_FF + MOE0)
            y_part()
            norm(4, quad_added, [n_items * 4 + 3, n_items * 4 + 5])

        @block.vector
        def _(dve):
            def lo(n, item=None):
                slot, _ = slot_use(n)
                if item is None:
                    dve.wait_ge(hi_ready, n + 1)
                    if n >= RING:
                        dve.wait_ge(unit_used, n - RING + 1)
                else:
                    dve.wait_ge(hi_ready, item * N_FF + (n + 1))
                    dve.wait_ge(unit_used, item * N_FF + (n - RING + 1))
                dve.tensor_tensor(w_lo[:, n % RING, :], raw[:, slot, :], w_hi[:, n % RING, :].bitcast(F32), ALU.subtract).then_inc(lo_ready, 1)

            def norm(j):
                for t in range(TT):
                    m = TT * j + t + 1
                    dve.wait_ge(rooted, m)
                    dve.reciprocal(rstd[:, t:t + 1], rstd[:, t:t + 1]).then_inc(inverted, 1)
                    dve.wait_ge(inverted, m)
                    if t == 0:
                        dve.wait_ge(lnw_ready, 16 * (j + 1))
                    dve.scalar_tensor_tensor(out=h[:, t, :], in0=X[:, t, :], scalar=rstd[:, t:t + 1], in1=lnw[:],
                                             op0=ALU.mult, op1=ALU.mult).then_inc(normed, 1)

            def turned(j):
                for q in range(4):
                    t, g = divmod(q, 2)
                    dst = (slice(None), slice(4 * g, 4 * g + 4), slice(P * t, P * (t + 1)))
                    dve.wait_ge(t_hi_ready, 4 * j + q + 1)
                    dve.tensor_tensor(t_lo[dst], WB[q][:].rearrange("p (k t) -> p k t", k=4), t_hi[dst].bitcast(F32),
                                      ALU.subtract).then_inc(t_lo_ready, 1)

            def after_unit(n):
                dve.wait_ge(unit_used, n + 1)

            def residual():
                for t in range(TT):
                    dve.tensor_tensor(X[:, t, :], X[:, t, :], YB[:, 2 * t:2 * t + 2, :].rearrange("p a c -> p (a c)"),
                                      ALU.add).then_inc(added, 1)

            dve.wait_ge(turned_rows, 3)
            for l in range(L):
                dve.tensor_copy(taps[:, l].rearrange("p w c -> p (w c)"), WB[l][:, 0:TAPS * CT])
            dve.tensor_copy(pv[:].rearrange("p l c -> p (l c)"), WB[2][:, 0:L * NPV]).then_inc(params_ready, 1)
            dve.wait_ge(small_hi, 3)
            for l in range(L):
                dve.tensor_tensor(gr_lo[:, l], gr_raw[:, l], gr_hi[:, l].bitcast(F32), ALU.subtract).then_inc(small_lo, 1)
            dve.tensor_tensor(rt_lo[:], rt_raw[:], rt_hi[:].bitcast(F32), ALU.subtract).then_inc(small_lo, 1)

            def mixer(l):
                b = BASE[l]
                turned(2 * l)
                dve.wait_ge(gr_done, l + 1)
                dve.tensor_copy(gr_s[:].rearrange("p t r -> p (t r)"), YB[:, 3, 0:TT * RANK]).then_inc(gr_copied, 1)
                lo(b + 3)
                dve.wait_ge(grT_done, l + 1)
                dve.tensor_copy(gr_t[:], YB[0:RANK, 1, 0:T]).then_inc(grT_copied, 1)

                def conv_input(g):
                    dve.wait_ge(cgate_ready, 2 * l + g + 1)
                    dve.wait_ge(pads_ready, 2 * (l + 1))
                    dve.tensor_tensor(cu[:, 2 * g:2 * g + 2, PAD:], cgate, WB[2 * g][:].rearrange("p (c t) -> p c t", c=2),
                                      ALU.mult).then_inc(cu_ready, 1)

                conv_no = [0, 0]
                conv_all = [0]

                def conv(g, count):
                    for m in range(conv_no[g], min(conv_no[g] + count, 2 * TAPS)):
                        w, c = m // 2, 2 * g + m % 2
                        if w == 0:
                            dve.wait_ge(cu_ready, 2 * l + g + 1)
                            ins = dve.tensor_scalar(acc[:, c, :], cu[:, c, 0:T], taps[:, l, 0, c:c + 1],
                                                    pv[:, l, PV_CB + c:PV_CB + c + 1], ALU.mult, ALU.add)
                        else:
                            dve.wait_ge(conv_step, CT * TAPS * l + conv_all[0] - 1)
                            ins = dve.scalar_tensor_tensor(out=acc[:, c, :], in0=cu[:, c, w:w + T], scalar=taps[:, l, w, c:c + 1],
                                                           in1=acc[:, c, :], op0=ALU.mult, op1=ALU.add)
                        ins.then_inc(conv_step, 1)
                        conv_all[0] += 1
                    conv_no[g] = min(conv_no[g] + count, 2 * TAPS)

                conv_input(0)
                conv(0, 4)
                lo(b + 4)
                conv(0, 8)
                lo(b + 5)
                conv_input(1)
                dve.wait_ge(logit_done, l + 1)
                dve.wait_ge(gate_abs, KT * (l + 1))
                for k in range(KT):
                    ins = dve.tensor_scalar(cum[:, k, :], YB[:, 2, T * k:T * (k + 1)], pv[:, l, PV_BG + k:PV_BG + k + 1], 0.0,
                                            ALU.add, ALU.min)
                ins.then_inc(gate_min, 1)
                conv(0, 6)
                lo(b + 6)
                dve.wait_ge(gate_ln, l + 1)
                dve.wait_ge(gate_min, l + 1)
                dve.tensor_tensor(cum[:], cum[:], Difs[:, 0], ALU.subtract).then_inc(gate_sub, 1)
                dve.wait_ge(gate_sub, l + 1)
                for k in range(KT):
                    for t in range(TT):
                        c = cum[:, k, P * t:P * (t + 1)]
                        ins = dve.tensor_tensor_scan(c, ones[:], c, 0.0, ALU.mult, ALU.add)
                ins.then_inc(cum_ready, 1)
                conv(0, 6)
                lo(b + 7)

                def differences(n):
                    s = LEVELS[n]
                    Dif = Difs[:, n % 2]
                    if n == 0:
                        dve.wait_ge(cum_ready, l + 1)
                    if n >= 2:
                        dve.wait_ge(kE_ready, 8 * l + n - 1)
                        dve.wait_ge(qE_ready, 8 * l + n - 1)
                    if s == P:
                        dve.tensor_tensor(Dif[:, :, 0:P], cum[:, :, P - 1:P].broadcast_to([P, KT, P]), cum[:, :, 0:P],
                                          ALU.subtract).then_inc(dif_ready, 1)
                        return
                    nb = KT * T // (2 * s)
                    blocks = cum[:].rearrange("p k (b s) -> p (k b) s", s=2 * s)
                    dst = Dif.rearrange("p k (b s) -> p (k b) s", s=2 * s)
                    ref = blocks[:, :, s - 1:s].broadcast_to([P, nb, s])
                    dve.tensor_tensor(dst[:, :, 0:s], ref, blocks[:, :, 0:s], ALU.subtract)
                    dve.tensor_tensor(dst[:, :, s:], blocks[:, :, s:], ref, ALU.subtract).then_inc(dif_ready, 1)

                def q_decayed(n):
                    dve.wait_ge(decay_ready, 8 * l + n + 1)
                    if n == 0:
                        dve.wait_ge(qk_ready, 2 * (l + 1))
                    else:
                        dve.wait_ge(level_done, 9 * l + n)
                    dve.tensor_tensor(qkE[:, 0], qk[:, 0], Difs[:, n % 2], ALU.mult).then_inc(qE_ready, 1)

                def level_read_out(n):
                    dve.wait_ge(level_done, 9 * l + n + 1)
                    if n == 1:
                        dve.wait_ge(pads_ready, 2 * (l + 1))
                    if n > 1:
                        dve.wait_ge(level_read, 2 * (9 * l + n))
                    for r in range(2):
                        bank = YB[:, 2 * (n % 2) + r, :]
                        if n == 0:
                            ins = dve.tensor_copy(attx[:, r].rearrange("p a i -> p (a i)"), bank[:, 0:2 * P])
                        else:
                            ins = dve.copy_predicated(att[:, r], masks[:, n - 1:n, :].broadcast_to([P, 2 * TT, P]),
                                                      bank.rearrange("p (a i) -> p a i", i=P))
                        ins.then_inc(level_read, 1)

                differences(0)
                differences(1)
                conv(0, 4)
                q_decayed(0)
                differences(2)
                lo(b + 8)
                q_decayed(1)
                level_read_out(0)
                differences(3)
                conv(0, 2)
                q_decayed(2)
                level_read_out(1)
                differences(4)
                lo(b + 9)
                q_decayed(3)
                level_read_out(2)
                differences(5)
                for n in range(4, 8):
                    conv(0, 2)
                    q_decayed(n)
                    level_read_out(n - 1)
                    if n < 6:
                        differences(n + 2)
                    if n > 4:
                        lo(b + N_IN + n - 5)
                level_read_out(7)
                level_read_out(8)
                conv(0, 2 * TAPS)
                conv(1, 12)
                dve.wait_ge(o_squared, l + 1)
                dve.tensor_reduce(o_ss[:], o_sq.rearrange("p (a c) -> p a c", c=DV), AX, ALU.add).then_inc(o_summed, 1)
                conv(1, 10)
                dve.wait_ge(o_rooted, l + 1)
                dve.reciprocal(o_ss[:], o_ss[:]).then_inc(o_inverted, 1)
                dve.wait_ge(o_inverted, l + 1)
                dve.wait_ge(og_ready, 2 * (l + 1))
                for t in range(TT):
                    for hd in range(HEADS):
                        a = HEADS * t + hd
                        gate = og.rearrange("p (g t c) -> p g t c", g=2, t=TT)[:, hd // 2, t, DV * (hd % 2):DV * (hd % 2 + 1)]
                        ins = dve.scalar_tensor_tensor(out=o_sq[:, DV * a:DV * (a + 1)], in0=YB[:, t, DV * hd:DV * (hd + 1)],
                                                       scalar=o_ss[:, a:a + 1], in1=gate, op0=ALU.mult, op1=ALU.mult)
                ins.then_inc(o_gated, 1)
                conv(1, 8)
                dve.wait_ge(mix_hi, l + 1)
                dve.scalar_tensor_tensor(out=t_lo[:, 0:HEADS, :].rearrange("p h t -> p (h t)"),
                                         in0=YB[:, 2:4, :].rearrange("p a c -> p (a c)"), scalar=pv[:, l, PV_GN:PV_GN + 1],
                                         in1=t_hi[:, 0:HEADS, :].rearrange("p h t -> p (h t)").bitcast(F32),
                                         op0=ALU.mult, op1=ALU.subtract).then_inc(mix_lo, 1)
                conv(1, 2 * TAPS)
                dve.wait_ge(c_summed, l + 1)
                dve.scalar_tensor_tensor(out=acc[:], in0=WB[2][:, 0:T].unsqueeze(1).broadcast_to([P, CT, T]), scalar=-1.0 / CH,
                                         in1=acc[:], op0=ALU.mult, op1=ALU.add).then_inc(c_centred, 1)
                dve.wait_ge(c_rooted, l + 1)
                dve.reciprocal(Difs[:, 0, 0, :], Difs[:, 0, 0, :]).then_inc(c_inverted, 1)
                dve.wait_ge(c_inverted, l + 1)
                dve.tensor_tensor(acc[:], acc[:], Difs[:, 0, 0:1, :].broadcast_to([P, CT, T]), ALU.mult).then_inc(c_scaled, 1)
                dve.wait_ge(c_hi, l + 1)
                dve.tensor_tensor(t_lo[:, HEADS:, :], c_sq.rearrange("p (c t) -> p c t", c=CT), t_hi[:, HEADS:, :].bitcast(F32),
                                  ALU.subtract).then_inc(c_lo, 1)
                lo(b + N_IN + 3)
                after_unit(b + N_MIX - 1)
                residual()

            for n in range(RING):
                if n == 1:
                    norm(0)
                lo(n)
            mixer(0)

            d0 = DENSE0
            lo(d0 + 0)
            norm(1)
            lo(d0 + 1)
            turned(1)
            lo(d0 + 2)

            def dense_act(c, n):
                after_unit(n)
                dve.wait_ge(dgate_ready, c + 1)
                if c:
                    dve.wait_ge(dT_lo_ready, c)
                dve.tensor_tensor(dact[:], dg[:], WB[2 + c % 2][:], ALU.mult).then_inc(dact_ready, 1)

            def dense_turn(c):
                dve.wait_ge(dT_hi_ready, c + 1)
                dve.tensor_tensor(dT_lo[:].rearrange("p f t -> p (f t)"), dact[:], dT_hi[:].rearrange("p f t -> p (f t)").bitcast(F32),
                                  ALU.subtract).then_inc(dT_lo_ready, 1)

            up_at = [d0 + 1] + [d0 + 3 * c for c in range(1, CHUNKS)]
            done = 3
            for c in range(CHUNKS):
                while done < min(up_at[c] + 3 - d0, N_FF):
                    lo(d0 + done)
                    done += 1
                dense_act(c, up_at[c])
                dense_turn(c)
            while done < N_FF:
                lo(d0 + done)
                done += 1
            after_unit(d0 + N_FF - 1)
            residual()
            for n in range(BASE[1], BASE[1] + RING):
                if n == BASE[1] + 1:
                    norm(2)
                lo(n)
            mixer(1)

            for n in range(MOE0, MOE0 + 2):
                lo(n)
            norm(3)
            turned(3)
            steps = [0]

            def step(ins):
                steps[0] += 1
                ins.then_inc(route_step, 1)
                dve.wait_ge(route_step, steps[0])

            lg, eq, score, first, l2, second, comb, chosen, place, over, rank = (rout[:, k] for k in range(11))
            lead = rout[:, 12]
            top = rout[:, 13]
            prefer = rout[:, 14]
            wide = (P, TT, NE)

            def each(col):
                return col.broadcast_to(list(wide))

            dve.wait_ge(consts_ready, 4 + EXTRA)
            for e in range(NE):
                ins = dve.memset(prefer[:, :, e:e + 1], float(NE - e))
            step(ins)
            dve.wait_ge(logits_done, 1)
            step(dve.tensor_copy(lg, YB[:, 0, 0:TT * NE].rearrange("p (t e) -> p t e", t=TT)))

            def largest(values, k, onehot):
                step(dve.tensor_reduce(top[:, :, k], values, AX, ALU.max))
                step(dve.tensor_tensor(eq, values, each(top[:, :, k:k + 1]), ALU.is_equal))
                step(dve.tensor_tensor(score, eq, prefer, ALU.mult))
                step(dve.tensor_reduce(top[:, :, 2 + k], score, AX, ALU.max))
                step(dve.tensor_tensor(onehot, score, each(top[:, :, 2 + k:3 + k]), ALU.is_equal))

            largest(lg, 0, first)
            step(dve.scalar_tensor_tensor(out=l2, in0=first, scalar=NEG, in1=lg, op0=ALU.mult, op1=ALU.add))
            largest(l2, 1, second)
            dve.tensor_tensor(lead[:, :, 0], top[:, :, 1], top[:, :, 0], ALU.subtract).then_inc(lead_ready, 1)
            dve.tensor_tensor(chosen, first, second, ALU.add).then_inc(choice_ready, 1)
            dve.wait_ge(lead_exp, 1)
            step(dve.tensor_scalar(lead[:, :, 2], lead[:, :, 1], 1.0, None, ALU.add))
            step(dve.reciprocal(lead[:, :, 3], lead[:, :, 2]))
            step(dve.tensor_tensor(lead[:, :, 4], lead[:, :, 3], lead[:, :, 1], ALU.mult))
            step(dve.tensor_tensor(first, first, each(lead[:, :, 3:4]), ALU.mult))
            step(dve.tensor_tensor(second, second, each(lead[:, :, 4:5]), ALU.mult))
            step(dve.tensor_tensor(comb, first, second, ALU.add))
            dve.wait_ge(places_done, 1)
            step(dve.scalar_tensor_tensor(out=place, in0=YB[:, 1, 0:TT * NE].rearrange("p (t e) -> p t e", t=TT), scalar=1.0,
                                          in1=chosen, op0=ALU.add, op1=ALU.mult))
            step(dve.tensor_scalar(place, place, -1.0, None, ALU.add))
            step(dve.tensor_copy(slot_of[:, 0:NE, :].rearrange("p e t -> p t e"), place))
            step(dve.tensor_copy(gate_of[:, 0:NE, :].rearrange("p e t -> p t e"), comb))
            def select(item, count):
                dve.tensor_copy(cur[:, 0, :], slot_of[:, bass.ds(item, 1), :].rearrange("p o t -> p (o t)"))
                dve.tensor_copy(cur[:, 1, :], gate_of[:, bass.ds(item, 1), :].rearrange("p o t -> p (o t)")).then_inc(cur_ready, 1)
                dve.wait_ge(cur_ready, count)
                for t in range(TT):
                    ins = dve.tensor_scalar(sel[:, t, :], slot_no[:], cur[:, 0, t:t + 1], None, ALU.is_equal)
                ins.then_inc(sel_ready, 1)

            select(0, 1)
            step(dve.tensor_scalar(over[:, 0, :], YB[:, 1, TT * NE:TT * NE + NE], float(P), None, ALU.is_gt))
            step(dve.tensor_tensor_scan(rank[:, 0, :], ones[:, 0:NE], over[:, 0, :], 0.0, ALU.mult, ALU.add))
            shape3 = [P, EXTRA, NE]
            pick = rout[:, 15:17].rearrange("p a t e -> p (a t) e")[:, 0:EXTRA, :]
            prod = rout[:, 17:20].rearrange("p k t e -> p t k e") if TT == EXTRA else rout[:, 17:20].rearrange("p a t e -> p (a t e)").rearrange(
                "p (t k e) -> p t k e", t=TT, k=EXTRA)
            step(dve.tensor_tensor(pick, rank[:, 0:1, :].broadcast_to(shape3), number[:], ALU.is_equal))
            step(dve.tensor_tensor(pick, pick, over[:, 0:1, :].broadcast_to(shape3), ALU.mult))
            for table, values in ((slot_of, place), (gate_of, comb)):
                for t in range(TT):
                    ins = dve.tensor_tensor(prod[:, t], values[:, t:t + 1, :].broadcast_to(shape3), pick, ALU.mult)
                step(ins)
                step(dve.tensor_reduce(table[:, NE:NE + EXTRA, :].rearrange("p k t -> p t k"), prod, AX, ALU.add))
            step(dve.tensor_scalar(slot_of[:, NE:NE + EXTRA, :], slot_of[:, NE:NE + EXTRA, :], -float(P), None, ALU.add))
            step(dve.tensor_tensor(prod[:, 0], prefer[:, 0:1, :].broadcast_to(shape3), pick, ALU.mult))
            step(dve.tensor_reduce(top[:, 0, 4:4 + EXTRA], prod[:, 0], AX, ALU.add))
            step(dve.tensor_scalar(top[:, 0, 4:4 + EXTRA], top[:, 0, 4:4 + EXTRA], -1.0, float(NE), ALU.mult, ALU.add))
            step(dve.tensor_scalar(meta[:, 1:1 + EXTRA], top[:, 0, 4:4 + EXTRA], float(NE - 1), None, ALU.min))
            dve.tensor_scalar(meta[:, 0:1], rank[:, 0:1, NE - 1], float(NE), None, ALU.add).then_inc(meta_ready, 1)
            dve.wait_ge(meta_ready, 1)
            n_items = dve.value_load(meta[0:1, 0:1], min_val=NE, max_val=ITEMS)
            dve.memset(slot_gate[:], 0.0)
            dve.memset(selT[:].bitcast(F32), 0.0)
            dve.memset(YB[:, 0:2, :], 0.0).then_inc(y_zeroed, 1)

            def y_part(count):
                dve.wait_ge(y_hi_ready, count)
                dve.scalar_tensor_tensor(out=y_lo, in0=YB[:, 0:2, :].rearrange("p a c -> p (a c)"), scalar=slot_gate[:],
                                         in1=y_hi.bitcast(F32), op0=ALU.mult, op1=ALU.subtract).then_inc(y_lo_ready, 1)

            def xs_part(count):
                dve.wait_ge(xs_hi_ready, count)
                dve.tensor_tensor(xs_lo, stage[:], xs_hi.bitcast(F32), ALU.subtract).then_inc(xs_lo_ready, 1)

            def add_quad(r, count):
                t, half = divmod(r, 2)
                dve.wait_ge(scattered, count)
                dve.wait_ge(quad_added, count)
                dst = X[:, t, HALF * half:HALF * (half + 1)]
                dve.tensor_tensor(dst, dst, YB[:, 2, :], ALU.add).then_inc(quad_added, 1)

            xs_part(1)
            dve.memset(started[:, 0:1], 0.0).then_inc(eact_ready, 1)
            dve.memset(started[:, 1:2], 0.0).then_inc(quad_added, 1)
            dve.wait_ge(y_zeroed, 1)
            with dve.Fori(0, n_items) as i:
                for u in range(N_FF):
                    if u >= 2:
                        lo(MOE0 + u, i)
                    if u == 2:
                        y_part(i + 1)
                    for r in range(4):
                        if SCATTER[r] + 2 == u:
                            add_quad(r, i * 4 + (r + 1))
                    for c in range(EC):
                        if TURN[c] + 2 == u:
                            dve.wait_ge(eT_hi_ready, i * EC + (c + 1))
                            w = 4 if c < EC - 1 else 2
                            dve.tensor_tensor(eT_lo[:, 0:w, :], YB[:, 3, 0:P * w].rearrange("p (f t) -> p f t", f=w),
                                              eT_hi[:, 0:w, :].bitcast(F32), ALU.subtract).then_inc(eT_lo_ready, 1)
                        if UP_END[c] + 2 == u:
                            dve.wait_ge(egate_ready, i * EC + (c + 1))
                            dve.wait_ge(unit_used, i * N_FF + (MOE0 + UP_END[c] + 1))
                            w = 512 if c < EC - 1 else 256
                            dve.tensor_tensor(eact[:, 0:w], eg[:, 0:w], WB[2 + c % 2][:, 0:w], ALU.mult).then_inc(eact_ready, 1)
                    if TURN_SEL + 2 == u:
                        dve.wait_ge(selT_done, i + 1)
                        dve.tensor_copy(selT[:].rearrange("p t j -> p (t j)"), YB[:, 2, 0:TT * P])
                        dve.tensor_copy(slot_gate[:], YB[:, 2, TT * P:TT * P + 1]).then_inc(selT_ready, 1)
                        select(i + 1, i + 2)
                    if LAST_UP + 2 == u:
                        xs_part(i + 2)
                with dve.If(i < n_items - 1):
                    for u in range(2):
                        lo(MOE0 + N_FF + u, i)
            y_part(n_items + 1)
            for r in range(4):
                add_quad(r, n_items * 4 + (r + 1))
            norm(4)

        @block.tensor
        def _(pe):
            def unit(n, item=None):
                if item is None:
                    pe.wait_ge(hi_ready, n + 1)
                    pe.wait_ge(lo_ready, n + 1)
                else:
                    pe.wait_ge(hi_ready, item * N_FF + (n + 1))
                    pe.wait_ge(lo_ready, item * N_FF + (n + 1))
                return w_hi[:, n % RING, :], w_lo[:, n % RING, :]

            def channels_unit(n, bank, a_hi, a_lo):
                hi, lo = (w.rearrange("p (k c) -> p k c", k=KD) for w in unit(n))
                for f in range(2):
                    dst = bank[:, T * f:T * (f + 1)]
                    for k in range(KD):
                        cols = slice(P * f, P * (f + 1))
                        pe.matmul(dst, lo[:, k, cols], a_hi[:, k, :], start=(k == 0), stop=False)
                        pe.matmul(dst, hi[:, k, cols], a_hi[:, k, :], start=False, stop=False)
                        ins = pe.matmul(dst, hi[:, k, cols], a_lo[:, k, :], start=False, stop=(k == KD - 1))
                ins.then_inc(unit_used, 1)

            def tokens_unit(n, bank, a_hi, a_lo):
                hi, lo = (w.rearrange("p (k c) -> p k c", k=KD) for w in unit(n))
                for t in range(TT):
                    dst = bank[:, 256 * t:256 * (t + 1)]
                    for k in range(KD):
                        tok = slice(P * t, P * (t + 1))
                        pe.matmul(dst, a_hi[:, k, tok], hi[:, k, :], start=(k == 0), stop=False)
                        pe.matmul(dst, a_hi[:, k, tok], lo[:, k, :], start=False, stop=False)
                        ins = pe.matmul(dst, a_lo[:, k, tok], hi[:, k, :], start=False, stop=(k == KD - 1))
                ins.then_inc(unit_used, 1)

            def down_unit(n, a_hi, a_lo, k0, first, last):
                hi, lo = (w.rearrange("p (k c) -> p k c", k=2) for w in unit(n))
                for k in range(2):
                    for t in range(TT):
                        tok = slice(P * t, P * (t + 1))
                        for a, w, s, e in ((a_hi, hi, True, False), (a_hi, lo, False, False), (a_lo, hi, False, True)):
                            for half in range(2):
                                ins = pe.matmul(YB[:, 2 * t + half, :], a[:, k0 + k, tok], w[:, k, HALF * half:HALF * (half + 1)],
                                                start=(first and k == 0 and s), stop=(last and k == 1 and e))
                ins.then_inc(unit_used, 1)

            def turn_h(j):
                for q in range(4):
                    t, g = divmod(q, 2)
                    if g == 0:
                        pe.wait_ge(normed, TT * j + t + 1)
                    for k in range(4):
                        ins = pe.transpose(WB[q][:, P * k:P * (k + 1)], h[:, t, P * (4 * g + k):P * (4 * g + k + 1)], ident[:])
                    ins.then_inc(h_turned, 1)
                pe.wait_ge(t_hi_ready, 4 * (j + 1))
                pe.wait_ge(t_lo_ready, 4 * (j + 1))

            def mixer(l):
                b = BASE[l]
                turn_h(2 * l)
                for t in range(TT):
                    tok = slice(P * t, P * (t + 1))
                    for k in range(KD):
                        dst = YB[:, 3, RANK * t:RANK * (t + 1)]
                        pe.matmul(dst, t_hi[:, k, tok], gr_hi[:, l, k, :], start=(k == 0), stop=False)
                        pe.matmul(dst, t_hi[:, k, tok], gr_lo[:, l, k, :], start=False, stop=False)
                        ins = pe.matmul(dst, t_lo[:, k, tok], gr_hi[:, l, k, :], start=False, stop=(k == KD - 1))
                ins.then_inc(gr_done, 1)
                channels_unit(b + 0, WB[0], t_hi, t_lo)
                pe.wait_ge(gr_copied, l + 1)
                for t in range(TT):
                    ins = pe.transpose(YB[0:RANK, 1, P * t:P * (t + 1)], gr_s[:, t, :], ident[:])
                ins.then_inc(grT_done, 1)
                channels_unit(b + 1, WB[1], t_hi, t_lo)
                pe.wait_ge(grT_copied, l + 1)
                for k in range(KT):
                    ins = pe.matmul(YB[:, 2, T * k:T * (k + 1)], wgu[:, l, P * k:P * (k + 1)], gr_t[:], start=True, stop=True)
                ins.then_inc(logit_done, 1)
                channels_unit(b + 2, WB[2], t_hi, t_lo)
                channels_unit(b + 3, WB[3], t_hi, t_lo)
                pe.wait_ge(cu_ready, 2 * l + 1)
                channels_unit(b + U_Q, WB[0], t_hi, t_lo)
                channels_unit(b + U_K, WB[1], t_hi, t_lo)
                pe.wait_ge(cu_ready, 2 * l + 2)
                tokens_unit(b + U_V, WB[2], t_hi, t_lo)

                def level(n):
                    if n < 8:
                        pe.wait_ge(qE_ready, 8 * l + n + 1)
                        pe.wait_ge(kE_ready, 8 * l + n + 1)
                        src = qkE
                    else:
                        src = qk
                    if n == 0:
                        pe.wait_ge(gate_min, l + 1)
                    if n >= 2:
                        pe.wait_ge(level_read, 2 * (9 * l + n - 1))
                    for r in range(2):
                        rows = slice(DK * r, DK * (r + 1))
                        bank = YB[:, 2 * (n % 2) + r, :]
                        if n == 0:
                            pairs = [(hp, hp, slice(0, P), slice(P, T)) for hp in range(2)]
                        else:
                            pairs = [(2 * t + hp, hp, slice(P * t, P * (t + 1)), slice(P * t, P * (t + 1))) for t in range(TT) for hp in range(2)]
                        for place, hp, js, is_ in pairs:
                            ins = pe.matmul(bank[:, P * place:P * (place + 1)], src[rows, 1, hp, js], src[rows, 0, hp, is_],
                                            start=True, stop=True)
                    ins.then_inc(level_done, 1)

                level(0)
                tokens_unit(b + U_V + 1, WB[3], t_hi, t_lo)
                level(1)
                pe.wait_ge(qk_ready, 2 * (l + 1))
                tokens_unit(b + U_G, WB[0], t_hi, t_lo)
                level(2)
                tokens_unit(b + U_G + 1, WB[1], t_hi, t_lo)
                for n in range(3, 9):
                    level(n)
                pe.wait_ge(level_read, 2 * 9 * (l + 1))
                pe.wait_ge(v_ready, 2 * (l + 1))
                for hd in range(HEADS):
                    hp, r = divmod(hd, 2)
                    vs = slice(DV * hd, DV * (hd + 1))
                    pe.matmul(YB[:, 0, vs], att[:, r, hp, :], v[:, 0, vs], start=True, stop=True)
                    pe.matmul(YB[:, 1, vs], attx[:, r, hp, :], v[:, 0, vs], start=True, stop=False)
                    ins = pe.matmul(YB[:, 1, vs], att[:, r, 2 + hp, :], v[:, 1, vs], start=False, stop=True)
                ins.then_inc(o_done, 1)
                pe.wait_ge(o_gated, l + 1)
                for hd in range(HEADS):
                    for t in range(TT):
                        a = HEADS * t + hd
                        c0 = T * (hd % 2) + P * t
                        ins = pe.transpose(YB[:, 2 + hd // 2, c0:c0 + P], o_sq[:, DV * a:DV * (a + 1)], ident[:])
                ins.then_inc(o_turned, 1)
                for j in range(HEADS // 2):
                    if j == 0:
                        pe.wait_ge(mix_hi, l + 1)
                        pe.wait_ge(mix_lo, l + 1)
                    down_unit(b + N_IN + j, t_hi, t_lo, 2 * j, j == 0, False)
                pe.wait_ge(conv_step, CT * TAPS * (l + 1))
                for c in range(CT):
                    ins = pe.matmul(WB[2][:, 0:T], ones[:], acc[:, c, :], start=(c == 0), stop=(c == CT - 1))
                ins.then_inc(c_summed, 1)
                pe.wait_ge(c_squared, l + 1)
                for c in range(CT):
                    ins = pe.matmul(WB[3][:, 0:T], ones[:], c_sq[:, T * c:T * (c + 1)], start=(c == 0), stop=(c == CT - 1))
                ins.then_inc(c_varied, 1)
                pe.wait_ge(c_hi, l + 1)
                pe.wait_ge(c_lo, l + 1)
                for j in range(HEADS // 2, N_OUT):
                    down_unit(b + N_IN + j, t_hi, t_lo, 2 * j, False, j == N_OUT - 1)

            pe.wait_ge(pool_step, 2)
            pe.wait_ge(rows_ready, 16 * 6 * L)
            for l in range(L):
                pe.transpose(WB[l][:, 0:TAPS * CT], tap_rows[0:TAPS * CT, l, :], ident[0:TAPS * CT, 0:TAPS * CT]).then_inc(turned_rows, 1)
            pe.transpose(WB[2][:, 0:L * NPV], pv_rows[0:L * NPV, :], ident[0:L * NPV, 0:L * NPV]).then_inc(turned_rows, 1)
            pe.wait_ge(params_ready, 1)
            pe.wait_ge(small_hi, 3)
            pe.wait_ge(small_lo, 3)
            mixer(0)

            turn_h(1)
            n = DENSE0
            for c in range(CHUNKS + 1):
                if c < CHUNKS:
                    if c >= 2:
                        pe.wait_ge(dact_ready, c - 1)
                    channels_unit(n, WB[c % 2], t_hi, t_lo)
                    channels_unit(n + 1, WB[2 + c % 2], t_hi, t_lo)
                    n += 2
                if c:
                    if c == 1:
                        pe.wait_ge(added, TT)
                    pe.wait_ge(dT_hi_ready, c)
                    pe.wait_ge(dT_lo_ready, c)
                    down_unit(n, dT_hi, dT_lo, 0, c == 1, c == CHUNKS)
                    n += 1
            mixer(1)

            turn_h(3)
            for t in range(TT):
                tok = slice(P * t, P * (t + 1))
                for k in range(KD):
                    dst = YB[:, 0, NE * t:NE * (t + 1)]
                    pe.matmul(dst, t_hi[:, k, tok], rt_hi[:, k, :], start=(k == 0), stop=False)
                    pe.matmul(dst, t_hi[:, k, tok], rt_lo[:, k, :], start=False, stop=False)
                    ins = pe.matmul(dst, t_lo[:, k, tok], rt_hi[:, k, :], start=False, stop=(k == KD - 1))
            ins.then_inc(logits_done, 1)
            pe.wait_ge(choice_ready, 1)
            ch = rout[:, 7]
            pe.matmul(YB[:, 1, 0:NE], before[:], ch[:, 0, :], start=True, stop=True)
            pe.matmul(YB[:, 1, NE:2 * NE], ones[:], ch[:, 0, :], start=True, stop=False)
            pe.matmul(YB[:, 1, NE:2 * NE], before[:], ch[:, 1, :], start=False, stop=True)
            pe.matmul(YB[:, 1, 2 * NE:3 * NE], ones[:], ch[:, 0, :], start=True, stop=False)
            pe.matmul(YB[:, 1, 2 * NE:3 * NE], ones[:], ch[:, 1, :], start=False, stop=True).then_inc(places_done, 1)

            def gather(g):
                for k in range(4):
                    cs = slice(P * (4 * g + k), P * (4 * g + k + 1))
                    for t in range(TT):
                        ins = pe.matmul(YB[:, 2, P * k:P * (k + 1)], h[:, t, cs], sel[:, t, :], start=(t == 0), stop=(t == TT - 1))
                ins.then_inc(gathered, 1)

            def scatter(r):
                t, half = divmod(r, 2)
                cs = slice(HALF * half, HALF * (half + 1))
                pe.matmul(YB[:, 2, :], selT[:, t, :], y_hi[:, cs], start=True, stop=False)
                pe.matmul(YB[:, 2, :], selT[:, t, :], y_lo[:, cs], start=False, stop=True).then_inc(scattered, 1)

            pe.wait_ge(sel_ready, 1)
            gather(0)
            pe.wait_ge(staged, 1)
            gather(1)
            pe.wait_ge(meta_ready, 1)
            n_items = pe.value_load(meta[0:1, 0:1], min_val=NE, max_val=ITEMS)
            with pe.Fori(0, n_items) as i:
                pe.wait_ge(xs_hi_ready, i + 1)
                pe.wait_ge(xs_lo_ready, i + 1)
                for u, (what, c, part) in enumerate(plan):
                    hi, lo = unit(MOE0 + u, i)
                    if what != "down":
                        width, nk = (512, 4) if c < EC - 1 else (256, 8)
                        k0 = 4 * part
                        hi, lo = (w.rearrange("p (k c) -> p k c", k=nk) for w in (hi, lo))
                        bank = WB[(0 if what == "gate" else 2) + c % 2][:, 0:width]
                        for k in range(nk):
                            start, stop = k0 + k == 0, k0 + k == KD - 1
                            pe.matmul(bank, xs_hi[:, k0 + k, :], hi[:, k, :], start=start, stop=False)
                            pe.matmul(bank, xs_hi[:, k0 + k, :], lo[:, k, :], start=False, stop=False)
                            ins = pe.matmul(bank, xs_lo[:, k0 + k, :], hi[:, k, :], start=False, stop=stop)
                    else:
                        if part == 0:
                            pe.wait_ge(eT_hi_ready, i * EC + (c + 1))
                            pe.wait_ge(eT_lo_ready, i * EC + (c + 1))
                        hi, lo = (w.rearrange("p (k c) -> p k c", k=2) for w in (hi, lo))
                        for k in range(2):
                            f = 2 * part + k
                            first, last = c == 0 and f == 0, c == EC - 1 and k == 1
                            for a, w, s, e in ((eT_hi, hi, True, False), (eT_hi, lo, False, False), (eT_lo, hi, False, True)):
                                for half in range(2):
                                    ins = pe.matmul(YB[:, half, :], a[:, f, :], w[:, k, HALF * half:HALF * (half + 1)],
                                                    start=(first and s), stop=(last and e))
                    ins.then_inc(unit_used, 1)
                    if u in SCATTER:
                        r = SCATTER.index(u)
                        if r == 0:
                            pe.wait_ge(y_hi_ready, i + 1)
                            pe.wait_ge(y_lo_ready, i + 1)
                            pe.wait_ge(staged, i * 2 + 2)
                        else:
                            pe.wait_ge(quad_added, i * 4 + (r + 1))
                        scatter(r)
                    if u in TURN:
                        tc = TURN.index(u)
                        pe.wait_ge(eact_ready, i * EC + (tc + 2))
                        for f in range(4 if tc < EC - 1 else 2):
                            ins = pe.transpose(YB[:, 3, P * f:P * (f + 1)], eact[:, P * f:P * (f + 1)], ident[:])
                        ins.then_inc(eT_done, 1)
                    if u == TURN_SEL:
                        pe.wait_ge(quad_added, i * 4 + 5)
                        for t in range(TT):
                            pe.transpose(YB[:, 2, P * t:P * (t + 1)], sel[:, t, :], ident[:])
                        for t in range(TT):
                            ins = pe.matmul(YB[:, 2, TT * P:TT * P + 1], sel[:, t, :], cur[:, 1, t:t + 1],
                                            start=(t == 0), stop=(t == TT - 1))
                        ins.then_inc(selT_done, 1)
                    if u in GATHER:
                        g = GATHER.index(u)
                        if g == 0:
                            pe.wait_ge(selT_ready, i + 1)
                            pe.wait_ge(sel_ready, i + 2)
                        else:
                            pe.wait_ge(staged, i * 2 + 3)
                        gather(g)
            pe.wait_ge(y_hi_ready, n_items + 1)
            pe.wait_ge(y_lo_ready, n_items + 1)
            pe.wait_ge(staged, n_items * 2 + 2)
            for r in range(4):
                if r:
                    pe.wait_ge(quad_added, n_items * 4 + (r + 1))
                scatter(r)


_INS = ['x', 'ln1_w', 'w_in', 'w_gate_up', 'b_gate', 'gla_norm_w', 'conv_w', 'conv_b', 'cn_w', 'cn_b', 'w_out',
        'ln2_w', 'wd_gate', 'wd_up', 'wd_down', 'w_router', 'we_gate', 'we_up', 'we_down', 'final_norm_w']


def kernel(**inputs):
    import numpy as np
    import concourse.bacc as bacc
    from concourse.bass_utils import run_bass_kernel_spmd

    nc = bacc.Bacc("TRN2", target_bir_lowering=False, num_devices=1)
    arrays, args = {}, []
    for name in _INS:
        a = np.ascontiguousarray(inputs[name])
        arrays[f"in_{name}"] = a
        args.append(nc.dram_tensor(f"in_{name}", a.shape, mybir.dt.from_np(a.dtype), kind="ExternalInput").ap())
    out = nc.dram_tensor("out", inputs["x"].shape, F32, kind="ExternalOutput").ap()
    trunk(nc, *args, out)
    r = run_bass_kernel_spmd(nc, [arrays], core_ids=[0])
    return r.results[0]["out"]
```

```python
from contextlib import ExitStack

import concourse.bass as bass
from concourse import mybir

F32 = mybir.dt.float32
F32R = mybir.dt.float32r
I32 = mybir.dt.int32
U8 = mybir.dt.uint8
ALU = mybir.AluOpType
ACT = mybir.ActivationFunctionType
AX = mybir.AxisListType.X

P = 128
UNIT = 2048
RAW = 11
RING = 3
EPS = 1e-6
NEG = -3.0e38


def trunk(nc, x, ln1_w, w_in, w_gate_up, b_gate, gla_norm_w, conv_w, conv_b, cn_w, cn_b, w_out,
          ln2_w, wd_gate, wd_up, wd_down, w_router, we_gate, we_up, we_down, final_norm_w, out):
    _, T, D = x.shape
    L, _, IN_COLS = w_in.shape
    RANK, KEY = w_gate_up.shape[1:]
    DV = gla_norm_w.shape[1]
    TAPS, CH = conv_w.shape[1:]
    VAL = w_out.shape[1] - CH
    HEADS = VAL // DV
    DK = KEY // HEADS
    FF = wd_gate.shape[2]
    NE = w_router.shape[2]
    TT, KD, CT, KT = T // P, D // P, CH // P, KEY // P
    HALF = D // 2
    assert (T, D, DK, DV, KEY, L) == (256, 1024, 64, P, 256, 2) and FF % 512 == 256 and NE == 8

    OFF_V, OFF_G = 2 * KEY, 2 * KEY + VAL
    OFF_R = OFF_G + VAL
    OFF_CA, OFF_CB = OFF_R + RANK, OFF_R + RANK + CH
    IN_UNITS = [OFF_CA, OFF_CB, OFF_CA + 256, OFF_CB + 256, 0, KEY, OFF_V, OFF_V + 256, OFF_G, OFF_G + 256]
    U_Q, U_K, U_V, U_G = 4, 5, 6, 8
    N_IN, N_OUT = len(IN_UNITS), w_out.shape[1] // 256
    N_MIX = N_IN + N_OUT
    CHUNKS = FF // 256
    N_FF = 3 * CHUNKS
    BASE = [0, N_MIX + N_FF]
    DENSE0 = N_MIX
    MOE0 = BASE[1] + N_MIX
    assert N_FF % RAW == 0 and N_FF % RING == 0

    EC = FF // 512 + 1
    plan = []
    for c in range(EC):
        parts = 2 if c < EC - 1 else 1
        plan += [("gate", c, p) for p in range(parts)] + [("up", c, p) for p in range(parts)]
        if c:
            plan += [("down", c - 1, 0), ("down", c - 1, 1)]
    plan += [("down", EC - 1, 0)]
    assert len(plan) == N_FF
    at = {what: u for u, what in enumerate(plan)}
    GATE_END = [at["gate", c, 1 if c < EC - 1 else 0] for c in range(EC)]
    UP_END = [at["up", c, 1 if c < EC - 1 else 0] for c in range(EC)]
    TURN = [GATE_END[c + 1] for c in range(EC - 1)] + [at["down", EC - 2, 0]]
    SCATTER = [2, 3, 4, 5]
    TURN_SEL, GATHER = 10, [16, 18]
    LAST_UP = UP_END[EC - 1]
    EXTRA = (2 * T) // (P + 1)
    ITEMS = NE + EXTRA

    ctx = ExitStack()
    with ctx:
        def sem(name):
            return ctx.enter_context(nc.semaphore(name))

        def on(stack):
            return lambda name, shape, dt=F32: stack.enter_context(nc.sbuf_tensor(name, shape, dt))

        sb = on(ctx)
        raw = sb("raw", [P, RAW, UNIT])
        w_hi = sb("w_hi", [P, RING, UNIT], F32R)
        w_lo = sb("w_lo", [P, RING, UNIT], F32R)
        X = sb("X", [P, TT, D])
        t_hi = sb("t_hi", [P, KD, T], F32R)
        t_lo = sb("t_lo", [P, KD, T], F32R)
        lnw = sb("lnw", [P, D])
        ident = sb("ident", [P, P])
        ones = sb("ones", [P, P])
        masks = sb("masks", [P, 8, P], U8)
        taps = sb("taps", [P, L, TAPS, CT])
        NPV = KT + 3 * CT + 1
        pv = sb("pv", [P, L, NPV])
        gr_hi = sb("gr_hi", [P, L, KD, RANK], F32R)
        gr_lo = sb("gr_lo", [P, L, KD, RANK], F32R)
        wgu = sb("wgu", [RANK, L, KEY])
        rt_hi = sb("rt_hi", [P, KD, NE], F32R)
        rt_lo = sb("rt_lo", [P, KD, NE], F32R)
        eps = sb("eps", [P, 1])
        ss = sb("ss", [P, TT])
        rstd = sb("rstd", [P, TT])
        slot_of = sb("slot_of", [P, ITEMS + 1, TT])
        gate_of = sb("gate_of", [P, ITEMS + 1, TT])
        meta = sb("meta", [P, 1 + EXTRA + 1], I32)
        number = sb("number", [P, EXTRA, NE])
        idle = sb("idle", [P, 24])

        s0 = ExitStack()
        sc = on(s0)
        sc("beside_h", [P, TT, D])
        tap_rows = sc("tap_rows", [P, L, P])
        pv_rows = sc("pv_rows", [P, P])
        gr_raw = sc("gr_raw", [P, L, KD, RANK])
        rt_raw = sc("rt_raw", [P, KD, NE])
        sc("beside_cu", [P, 2880])
        mask_f = sc("mask_f", [P, 8, P])
        s0.close()

        s1 = ExitStack()
        h = on(s1)("h", [P, TT, D])
        s1.close()

        s2 = ExitStack()
        sm = on(s2)
        qk = sm("qk", [P, 2, KT, T])
        o_sq = qk[:].rearrange("p a k t -> p (a k t)")
        qkE = [sm("qkE", [P, 2, KT, T])[:], lnw[:].rearrange("p (a k t) -> p a k t", a=2, k=KT)]
        cgate = qkE[0][:, 0]
        og = qkE[0].rearrange("p a k t -> p (a k t)")
        Difs = sm("Difs", [P, 2, KT, T])
        cum = sm("cum", [P, KT, T])
        att = sm("att", [P, 2, 2 * TT, P])
        attx = sm("attx", [P, 2, 2, P])
        v = sm("v", [P, TT, VAL])
        PAD = TAPS - 1
        cu = sm("cu", [P, CT, PAD + T])
        c_sq = cu[:].rearrange("p c t -> p (c t)")[:, 0:CT * T]
        acc = sm("acc", [P, CT, T])
        c_rms = cum[:, 0, :]
        gr_t = Difs[0:RANK, 1, 0, :]
        diag = sm("diag", [P, 2, 2, P])
        o_ss = sm("o_ss", [P, TT * HEADS])
        s2.close()

        s3 = ExitStack()
        sd = on(s3)
        dg = sd("dg", [P, 512])
        dact = sd("dact", [P, 512])
        dT_hi = sd("dT_hi", [P, 2, T], F32R)
        dT_lo = sd("dT_lo", [P, 2, T], F32R)
        s3.close()

        s4 = ExitStack()
        se = on(s4)
        se("beside_h4", [P, TT, D])
        stage = se("stage", [P, KD, P])
        xs_hi, y_hi = (t_hi[:].rearrange("p a b -> p (a b)")[:, D * k:D * (k + 1)] for k in range(2))
        xs_lo, y_lo = (t_lo[:].rearrange("p a b -> p (a b)")[:, D * k:D * (k + 1)] for k in range(2))
        xs_hi, xs_lo = (a.rearrange("p (k j) -> p k j", j=P) for a in (xs_hi, xs_lo))
        eg = se("eg", [P, 512])
        eact = se("eact", [P, 512])
        eT_hi = se("eT_hi", [P, 4, P], F32R)
        eT_lo = se("eT_lo", [P, 4, P], F32R)
        sel = se("sel", [P, TT, P])
        selT = se("selT", [P, TT, P], F32R)
        cur = se("cur", [P, 2, TT])
        slot_gate = se("slot_gate", [P, 1])
        started = se("started", [P, 2])
        rout = se("rout", [P, 24, TT, NE])
        lgT = se("lgT", [NE, T])
        before = se("before", [P, P])
        slot_no = se("slot_no", [P, P])
        s4.close()

        YB = ctx.enter_context(nc.psum_tensor("YB", [P, 4, 512], F32))
        WBS = ctx.enter_context(nc.psum_tensor("WBS", [P, 4, 512], F32))
        WB = [WBS[:, i, :] for i in range(4)]

        raw_ready = [sem(f"raw_ready{i}") for i in range(RAW)]
        x_ready = [sem(f"x_ready{t}") for t in range(TT)]
        rows_ready, lnw_ready = sem("rows_ready"), sem("lnw_ready")
        small_ready = sem("small_ready")
        hi_ready, lo_ready, unit_used = sem("hi_ready"), sem("lo_ready"), sem("unit_used")
        pool_step, consts_ready, turned_rows, params_ready = sem("pool_step"), sem("consts_ready"), sem("turned_rows"), sem("params_ready")
        small_hi, small_lo = sem("small_hi"), sem("small_lo")
        squared, rooted, inverted, normed = sem("squared"), sem("rooted"), sem("inverted"), sem("normed")
        h_turned, t_hi_ready, t_lo_ready = sem("h_turned"), sem("t_hi_ready"), sem("t_lo_ready")
        tile_done = sem("tile_done")
        added = sem("added")
        gr_done, gr_copied, logit_done = (sem(s) for s in ("gr_done", "gr_copied", "logit_done"))
        cgate_ready, cu_ready, pads_ready = (sem(s) for s in ("cgate_ready", "cu_ready", "pads_ready"))
        diag_ready, diag_used = sem("diag_ready"), sem("diag_used")
        conv_step = [sem(f"conv_step{c}") for c in range(CT)]
        gate_abs, gate_exp, gate_ln, gate_min, gate_sub, cum_ready = (sem(s) for s in ("gate_abs", "gate_exp", "gate_ln", "gate_min", "gate_sub", "cum_ready"))
        qk_ready, v_ready = sem("qk_ready"), sem("v_ready")
        dif_ready, decay_ready, qE_ready, kE_ready, level_done, level_read = (sem(s) for s in (
            "dif_ready", "decay_ready", "qE_ready", "kE_ready", "level_done", "level_read"))
        o_done, o_squared, o_summed, o_rooted, o_inverted, og_ready, o_gated, o_turned, mix_hi, mix_lo = (sem(s) for s in (
            "o_done", "o_squared", "o_summed", "o_rooted", "o_inverted", "og_ready", "o_gated", "o_turned", "mix_hi", "mix_lo"))
        c_summed, c_centred, c_squared, c_varied, c_rooted, c_inverted, c_scaled, c_silu, c_hi, c_lo = (sem(s) for s in (
            "c_summed", "c_centred", "c_squared", "c_varied", "c_rooted", "c_inverted", "c_scaled", "c_silu", "c_hi", "c_lo"))
        dgate_ready, dact_ready, dT_hi_ready, dT_lo_ready = (sem(s) for s in ("dgate_ready", "dact_ready", "dT_hi_ready", "dT_lo_ready"))
        counts_done = sem("counts_done")
        lgT_copied, logits_turned = sem("lgT_copied"), sem("logits_turned")
        logits_done, route_step, lead_exp, choice_ready, places_done, tables_ready, meta_ready, lead_ready = (sem(s) for s in (
            "logits_done", "route_step", "lead_exp", "choice_ready", "places_done", "tables_ready", "meta_ready", "lead_ready"))
        cur_ready, sel_ready, gathered, staged, xs_hi_ready, xs_lo_ready = (sem(s) for s in (
            "cur_ready", "sel_ready", "gathered", "staged", "xs_hi_ready", "xs_lo_ready"))
        egate_ready, eact_ready, eT_done, eT_hi_ready, eT_lo_ready = (sem(s) for s in (
            "egate_ready", "eact_ready", "eT_done", "eT_hi_ready", "eT_lo_ready"))
        y_zeroed, y_hi_ready, y_lo_ready, scattered, quad_added, selT_done, selT_ready = (sem(s) for s in (
            "y_zeroed", "y_hi_ready", "y_lo_ready", "scattered", "quad_added", "selT_done", "selT_ready"))
        out_stored = sem("out_stored")

        block = ctx.enter_context(nc.Block())

        LEVELS = [P, 64, 32, 16, 8, 4, 2, 1, 0]
        PV_BG, PV_CB, PV_CW, PV_CBB, PV_GN = 0, KT, KT + CT, KT + 2 * CT, KT + 3 * CT

        BY_VECTOR = 19
        LATE = TAPS - BY_VECTOR
        DVE_CONV = ([(c, w) for w in range(LATE) for c in (0, 1)]
                    + [(c, w if c < 2 else w - LATE) for w in range(LATE, TAPS) for c in (0, 1, 2)])
        PAIRS = [(TAPS + 1) // 2, (TAPS - BY_VECTOR + 1) // 2]
        STEPS = [TAPS, TAPS, BY_VECTOR + 1, 1]
        PE_TAPS = 12

        def o_banks(k):
            return WBS[:, k:k + 2, :].rearrange("p a c -> p (a c)")

        def slot_use(n):
            return n % RAW, n // RAW + 1

        wg_v = we_gate[0].rearrange("e (k p) f -> e p k f", p=P)
        wu_v = we_up[0].rearrange("e (k p) f -> e p k f", p=P)
        wd_v = we_down[0].rearrange("e (k p) n -> e p k n", p=P)

        @block.sync
        def _(sp):
            def small(l):
                sp.dma_start(gr_raw[:, l], w_in[l, :, OFF_R:OFF_R + RANK].rearrange("(k p) c -> p k c", p=P)).then_inc(small_ready, 16)
                sp.dma_start(tap_rows[0:TAPS * CT, l, :], conv_w[l].rearrange("w (c p) -> (w c) p", p=P)).then_inc(rows_ready, 16)
                for src, at0, k in ((b_gate, PV_BG, KT), (conv_b, PV_CB, CT), (cn_w, PV_CW, CT), (cn_b, PV_CBB, CT), (gla_norm_w, PV_GN, 1)):
                    r = l * NPV + at0
                    sp.dma_start(pv_rows[r:r + k, :], src[l].rearrange("(c p) -> c p", p=P)).then_inc(rows_ready, 16)

            for t in range(TT):
                sp.dma_start(X[:, t, :], x[0, P * t:P * (t + 1), :]).then_inc(x_ready[t], 16)

            def load(n, src, k):
                slot, _ = slot_use(n)
                if n >= RAW:
                    sp.wait_ge(lo_ready, n - RAW + 1)
                sp.dma_start(raw[:, slot, :].rearrange("p (k c) -> p k c", k=k), src).then_inc(raw_ready[slot], 16)

            def load_mixer(l):
                for j, c0 in enumerate(IN_UNITS):
                    load(BASE[l] + j, w_in[l, :, c0:c0 + 256].rearrange("(k p) c -> p k c", p=P), 8)
                    if l == 0 and j == 0:
                        for layer in range(L):
                            small(layer)
                        sp.dma_start(wgu[:], w_gate_up.rearrange("l r c -> r l c")).then_inc(small_ready, 16)
                        sp.dma_start(rt_raw[:], w_router[0].rearrange("(k p) e -> p k e", p=P)).then_inc(small_ready, 16)
                for i, j in enumerate([2, 3, 0, 1]):
                    load(BASE[l] + N_IN + i, w_out[l, 256 * j:256 * (j + 1), :].rearrange("(k p) n -> p k n", p=P), 2)

            load_mixer(0)
            n = DENSE0
            for c in range(CHUNKS + 1):
                if c < CHUNKS:
                    load(n, wd_gate[0, :, 256 * c:256 * (c + 1)].rearrange("(k p) f -> p k f", p=P), 8)
                    load(n + 1, wd_up[0, :, 256 * c:256 * (c + 1)].rearrange("(k p) f -> p k f", p=P), 8)
                    n += 2
                if c:
                    load(n, wd_down[0, 256 * (c - 1):256 * c, :].rearrange("(k p) n -> p k n", p=P), 2)
                    n += 1
            load_mixer(1)

            def load_expert(e, item):
                for u, (what, c, part) in enumerate(plan):
                    slot, _ = slot_use(MOE0 + u)
                    sp.wait_ge(lo_ready, item * N_FF + (MOE0 + u - RAW + 1))
                    if what == "down":
                        k0 = 4 * c + 2 * part
                        src, k = wd_v[e, :, k0:k0 + 2, :], 2
                    else:
                        w = wg_v if what == "gate" else wu_v
                        if c < EC - 1:
                            src, k = w[e, :, 4 * part:4 * part + 4, 512 * c:512 * (c + 1)], 4
                        else:
                            src, k = w[e, :, :, 512 * c:FF], 8
                    sp.dma_start(raw[:, slot, :].rearrange("p (k c) -> p k c", k=k), src).then_inc(raw_ready[slot], 16)

            with sp.Fori(0, NE) as e:
                load_expert(e, e)
            sp.wait_ge(meta_ready, 1)
            n_items = sp.value_load(meta[0:1, 0:1], min_val=NE, max_val=ITEMS)
            with sp.If(n_items > NE):
                with sp.Fori(NE, n_items) as item:
                    e = sp.value_load(meta[0:1, bass.ds(item - (NE - 1), 1)], min_val=0, max_val=NE - 1)
                    load_expert(e, item)

            for t in range(TT):
                sp.wait_ge(normed, 4 * TT + t + 1)
                sp.dma_start(out[0, P * t:P * (t + 1), :], h[:, t, :]).then_inc(out_stored, 16)
            sp.wait_ge(out_stored, 16 * TT)

        norm_weights = [ln1_w[0], ln2_w[0], ln1_w[1], ln2_w[1], final_norm_w]

        @block.gpsimd
        def _(pool):
            pool.dma_start(lnw[:], norm_weights[0].partition_broadcast(P)).then_inc(lnw_ready, 16)
            steps = [0]

            def step(ins):
                steps[0] += 1
                ins.then_inc(pool_step, 1)
                pool.wait_ge(pool_step, steps[0])

            step(pool.memset(ident[:], 0.0))
            step(pool.affine_select(out=ident[:], in_=ident[:], compare_op=ALU.not_equal, fill=1.0, base=0,
                                    pattern=[[-1, P]], channel_multiplier=1))
            step(pool.memset(eps[:], EPS))
            step(pool.memset(ones[:], 1.0))
            step(pool.memset(mask_f[:], 0.0))
            for n, s in enumerate(LEVELS[1:]):
                if s:
                    m = mask_f[:, n, :].rearrange("p (b s) -> p b s", s=2 * s)[:, :, s:2 * s]
                    nb = P // (2 * s)
                    step(pool.memset(m, 1.0))
                    step(pool.affine_select(out=m, in_=m, compare_op=ALU.is_ge, fill=0.0, base=0,
                                            pattern=[[-2 * s, nb], [0, s]], channel_multiplier=1))
                    step(pool.affine_select(out=m, in_=m, compare_op=ALU.is_ge, fill=0.0, base=s - 1,
                                            pattern=[[2 * s, nb], [0, s]], channel_multiplier=-1))
                else:
                    step(pool.tensor_copy(mask_f[:, n, :], ident[:]))
            step(pool.tensor_copy(masks[:], mask_f[:]))
            pool.memset(slot_of[:, ITEMS, :], -1.0).then_inc(consts_ready, 1)
            pool.memset(gate_of[:, ITEMS, :], 0.0).then_inc(consts_ready, 1)
            for k in range(EXTRA):
                pool.memset(number[:, k, :], float(k + 1)).then_inc(consts_ready, 1)

            for l in range(L):
                if l:
                    pool.wait_ge(added, 2 * TT)
                pool.memset(cu[:, :, 0:PAD], 0.0).then_inc(pads_ready, 1)
                pool.memset(att[:], 0.0).then_inc(pads_ready, 1)

                def diagonals(m):
                    c, w = (3, 2 * m) if m < PAIRS[0] else (2, BY_VECTOR + 2 * (m - PAIRS[0]))
                    n = min(2, TAPS - w)
                    if m >= 2 or l:
                        pool.wait_ge(diag_used, sum(PAIRS) * l + m - 1)
                    pool.tensor_tensor(diag[:, m % 2, 0:n, :], ident[:].unsqueeze(1).broadcast_to([P, n, P]),
                                       taps[:, l, w:w + n, c:c + 1].broadcast_to([P, n, P]), ALU.mult).then_inc(diag_ready, 1)

                pool.wait_ge(params_ready, 1)
                for m in range(PAIRS[0] + 2):
                    diagonals(m)
                m = PAIRS[0] + 2
                for n in range(len(LEVELS) - 1):
                    pool.wait_ge(decay_ready, 8 * l + n + 1)
                    if n >= 2:
                        pool.wait_ge(level_done, 9 * l + n - 1)
                    pool.tensor_tensor(qkE[n % 2][:, 1], qk[:, 1], Difs[:, n % 2], ALU.mult).then_inc(kE_ready, 1)
                    for _ in range(sum(PAIRS) - m if n == 3 else 0):
                        diagonals(m)
                        m += 1
                pool.wait_ge(level_done, 9 * (l + 1))
                pool.dma_start(lnw[:], norm_weights[2 * l + 1].partition_broadcast(P)).then_inc(lnw_ready, 16)
                pool.wait_ge(normed, TT * (2 * l + 2))
                pool.dma_start(lnw[:], norm_weights[2 * l + 2].partition_broadcast(P)).then_inc(lnw_ready, 16)

            pool.wait_ge(added, 3 * TT)
            pool.affine_select(out=before[:], in_=ones[:], compare_op=ALU.is_gt, fill=0.0, base=0,
                               pattern=[[1, P]], channel_multiplier=-1).then_inc(consts_ready, 1)
            pool.iota(slot_no[:], pattern=[[1, P]], base=0, channel_multiplier=0,
                      allow_small_or_imprecise_dtypes=True).then_inc(consts_ready, 1)

        @block.scalar
        def _(act):
            def hi(n, item=None):
                slot, use = slot_use(n)
                if item is None:
                    act.wait_ge(raw_ready[slot], 16 * use)
                    if n >= RING:
                        act.wait_ge(unit_used, n - RING + 1)
                else:
                    act.wait_ge(raw_ready[slot], item * (16 * N_FF // RAW) + 16 * use)
                    act.wait_ge(unit_used, item * N_FF + (n - RING + 1))
                act.activation(w_hi[:, n % RING, :], raw[:, slot, :], ACT.Copy).then_inc(hi_ready, 1)

            preloads = []

            def preload(func):
                act.activation(idle[:, len(preloads):len(preloads) + 1], eps[:], func)
                preloads.append(func)

            def norm(j, ready, counts):
                preload(ACT.Sqrt)
                for t in range(TT):
                    act.wait_ge(ready[t], counts[t])
                    act.activation(h[:, t, :], X[:, t, :], ACT.Square, accum_out=ss[:, t:t + 1]).then_inc(squared, 1)
                    act.wait_ge(squared, TT * j + t + 1)
                    act.activation(rstd[:, t:t + 1], ss[:, t:t + 1], ACT.Sqrt, scale=1.0 / D, bias=eps[:]).then_inc(rooted, 1)

            def turned(j):
                for q in range(4):
                    t, g = divmod(q, 2)
                    act.wait_ge(h_turned, 4 * j + q + 1)
                    act.activation(t_hi[:, 4 * g:4 * g + 4, P * t:P * (t + 1)], WB[q][:].rearrange("p (k t) -> p k t", k=4),
                                   ACT.Copy).then_inc(t_hi_ready, 1)

            def after_unit(n):
                act.wait_ge(unit_used, n + 1)

            def mixer(l):
                b = BASE[l]
                hi(b + 3)
                for g in range(2):
                    after_unit(b + 2 * g + 1)
                    if g or l:
                        act.wait_ge(cu_ready, 2 * l + g)
                    act.activation(cgate.rearrange("p k t -> p (k t)"), WB[2 * g + 1][:], ACT.Sigmoid).then_inc(cgate_ready, 1)
                    hi(b + 4 + g)
                act.wait_ge(logit_done, l + 1)
                for k in range(KT):
                    act.activation(Difs[:, 0, k, :], YB[:, 2, T * k:T * (k + 1)], ACT.Abs,
                                   bias=pv[:, l, PV_BG + k:PV_BG + k + 1]).then_inc(gate_abs, 1)
                act.wait_ge(gate_abs, KT * (l + 1))
                act.activation(Difs[:, 0], Difs[:, 0], ACT.Exp, scale=-1.0).then_inc(gate_exp, 1)
                act.wait_ge(gate_exp, l + 1)
                act.activation(Difs[:, 0], Difs[:, 0], ACT.Ln, bias=1.0).then_inc(gate_ln, 1)
                hi(b + 6)
                after_unit(b + U_Q)
                act.activation(qk[:, 0].rearrange("p k t -> p (k t)"), WB[U_Q % 4][:], ACT.Copy, scale=DK ** -0.5).then_inc(qk_ready, 1)
                hi(b + 7)
                after_unit(b + U_K)
                act.activation(qk[:, 1].rearrange("p k t -> p (k t)"), WB[U_K % 4][:], ACT.Copy).then_inc(qk_ready, 1)

                def decays(n):
                    Dif = Difs[:, n % 2]
                    act.wait_ge(dif_ready, 8 * l + n + 1)
                    if n == 0:
                        act.activation(Dif[:, :, 0:P], Dif[:, :, 0:P], ACT.Exp, scale=1.0 / 16.0)
                        act.activation(Dif[:, :, P:T], cum[:, :, P:T], ACT.Exp, scale=1.0 / 16.0).then_inc(decay_ready, 1)
                    else:
                        act.activation(Dif, Dif, ACT.Exp, scale=1.0 / 16.0).then_inc(decay_ready, 1)

                def v_half(g):
                    after_unit(b + U_V + g)
                    act.activation(v[:, :, 256 * g:256 * (g + 1)], WB[(U_V + g) % 4][:].rearrange("p (t c) -> p t c", t=TT),
                                   ACT.Copy).then_inc(v_ready, 1)

                decays(0)
                decays(1)
                hi(b + 8)
                v_half(0)
                act.wait_ge(diag_used, sum(PAIRS) * l + PAIRS[0])
                act.activation(acc[:, 3, :], YB[:, 3, T:2 * T], ACT.Identity, bias=pv[:, l, PV_CB + 3:PV_CB + 4]).then_inc(conv_step[3], 1)
                decays(2)
                v_half(1)
                hi(b + 9)
                for n in range(3, 6):
                    decays(n)
                decays(6)
                hi(b + 10)
                decays(7)
                hi(b + 11)
                hi(b + 12)
                act.wait_ge(c_centred, l + 1)
                act.activation(c_sq, acc[:].rearrange("p c t -> p (c t)"), ACT.Square).then_inc(c_squared, 1)
                preload(ACT.Sqrt)
                act.wait_ge(c_varied, l + 1)
                act.activation(c_rms, WB[3][:, 0:T], ACT.Sqrt, scale=1.0 / CH, bias=eps[:]).then_inc(c_rooted, 1)
                act.wait_ge(level_done, 9 * l + 7)
                preload(ACT.Silu)
                for g in range(2):
                    after_unit(b + U_G + 1)
                    act.activation(og[:, 512 * g:512 * (g + 1)], WB[g][:], ACT.Silu).then_inc(og_ready, 1)
                act.wait_ge(c_scaled, l + 1)
                for c in range(CT):
                    act.activation(c_sq.rearrange("p (c t) -> p c t", c=CT)[:, c, :], acc[:, c, :], ACT.Silu,
                                   scale=pv[:, l, PV_CW + c:PV_CW + c + 1], bias=pv[:, l, PV_CBB + c:PV_CBB + c + 1]).then_inc(c_silu, 1)
                act.wait_ge(c_silu, CT * (l + 1))
                act.activation(t_hi[:, HEADS:, :], c_sq.rearrange("p (c t) -> p c t", c=CT), ACT.Copy).then_inc(c_hi, 1)
                act.wait_ge(o_done, l + 1)
                act.activation(o_sq, o_banks(0), ACT.Square).then_inc(o_squared, 1)
                preload(ACT.Sqrt)
                act.wait_ge(o_summed, l + 1)
                act.activation(o_ss[:], o_ss[:], ACT.Sqrt, scale=1.0 / DV, bias=eps[:]).then_inc(o_rooted, 1)
                hi(b + N_IN + 3)
                act.wait_ge(o_turned, l + 1)
                act.activation(t_hi[:, 0:HEADS, :].rearrange("p h t -> p (h t)"), o_banks(2), ACT.Copy,
                               scale=pv[:, l, PV_GN:PV_GN + 1]).then_inc(mix_hi, 1)
                hi(b + N_MIX)
                hi(b + N_MIX + 1)

            act.wait_ge(pool_step, 3)
            norm(0, x_ready, [16, 16])
            turned(0)
            hi(0)
            act.wait_ge(small_ready, 16 * (L + 2))
            for l in range(L):
                act.activation(gr_hi[:, l], gr_raw[:, l], ACT.Copy).then_inc(small_hi, 1)
            act.activation(rt_hi[:], rt_raw[:], ACT.Copy).then_inc(small_hi, 1)
            hi(1)
            hi(2)
            mixer(0)

            d0 = DENSE0
            norm(1, [added] * TT, [1, 2])
            turned(1)
            hi(d0 + 2)

            def dense_gate(c, n):
                after_unit(n)
                if c:
                    act.wait_ge(dact_ready, c)
                act.activation(dg[:], WB[c % 2][:], ACT.Silu).then_inc(dgate_ready, 1)

            def dense_turn(c, n_free):
                if n_free is not None:
                    after_unit(n_free)
                act.wait_ge(dact_ready, c + 1)
                act.activation(dT_hi[:].rearrange("p f t -> p (f t)"), dact[:], ACT.Copy).then_inc(dT_hi_ready, 1)

            gate_at = [d0] + [d0 + 3 * c - 1 for c in range(1, CHUNKS)]
            down_at = [d0 + 3 * c + 4 for c in range(CHUNKS - 1)] + [d0 + N_FF - 1]
            done = 3
            for c in range(CHUNKS):
                while done < min(gate_at[c] + 3 - d0, N_FF):
                    hi(d0 + done)
                    done += 1
                dense_gate(c, gate_at[c])
                if done < N_FF:
                    hi(d0 + done)
                    done += 1
                dense_turn(c, down_at[c - 1] if c else None)
            for n in range(BASE[1], BASE[1] + 2):
                hi(n)
            norm(2, [added] * TT, [3, 4])
            turned(2)
            hi(BASE[1] + 2)
            mixer(1)

            norm(3, [added] * TT, [5, 6])
            turned(3)
            preload(ACT.Exp)
            act.wait_ge(lead_ready, 1)
            act.activation(rout[:, 12, :, 1], rout[:, 12, :, 0], ACT.Exp).then_inc(lead_exp, 1)

            def stage_half(g, count):
                act.wait_ge(gathered, count)
                act.activation(stage[:, 4 * g:4 * g + 4, :], YB[:, 2, :].rearrange("p (k j) -> p k j", k=4), ACT.Copy).then_inc(staged, 1)

            for g in range(2):
                stage_half(g, g + 1)
            act.wait_ge(staged, 2)
            act.activation(xs_hi, stage[:], ACT.Copy).then_inc(xs_hi_ready, 1)
            act.wait_ge(meta_ready, 1)
            n_items = act.value_load(meta[0:1, 0:1], min_val=NE, max_val=ITEMS)

            def y_part():
                act.activation(y_hi, YB[:, 0:2, :].rearrange("p a c -> p (a c)"), ACT.Copy, scale=slot_gate[:]).then_inc(y_hi_ready, 1)

            act.wait_ge(y_zeroed, 1)
            with act.Fori(0, n_items) as i:
                preload(ACT.Silu)
                for u in range(N_FF):
                    if u >= 2:
                        hi(MOE0 + u, i)
                    if u == 2:
                        act.wait_ge(unit_used, i * N_FF + MOE0)
                        y_part()
                    for c in range(EC):
                        if TURN[c] + 2 == u:
                            act.wait_ge(eT_done, i * EC + (c + 1))
                            w = 4 if c < EC - 1 else 2
                            act.activation(eT_hi[:, 0:w, :], YB[:, 3, 0:P * w].rearrange("p (f t) -> p f t", f=w), ACT.Copy).then_inc(eT_hi_ready, 1)
                        if GATE_END[c] + 2 == u:
                            act.wait_ge(unit_used, i * N_FF + (MOE0 + GATE_END[c] + 1))
                            act.wait_ge(eact_ready, i * EC + (c + 1))
                            w = 512 if c < EC - 1 else 256
                            act.activation(eg[:, 0:w], WB[c % 2][:, 0:w], ACT.Silu).then_inc(egate_ready, 1)
                    for g in range(2):
                        if GATHER[g] + 2 == u:
                            act.wait_ge(xs_lo_ready, i + 1)
                            stage_half(g, i * 2 + (3 + g))
                    if LAST_UP + 2 == u:
                        act.wait_ge(unit_used, i * N_FF + (MOE0 + LAST_UP + 1))
                        act.wait_ge(staged, i * 2 + 4)
                        act.activation(xs_hi, stage[:], ACT.Copy).then_inc(xs_hi_ready, 1)
                with act.If(i < n_items - 1):
                    for u in range(2):
                        hi(MOE0 + N_FF + u, i)
            act.wait_ge(unit_used, n_items * N_FF + MOE0)
            y_part()
            norm(4, [quad_added] * TT, [n_items * 4 + 3, n_items * 4 + 5])

        @block.vector
        def _(dve):
            def lo(n, item=None):
                slot, _ = slot_use(n)
                if item is None:
                    dve.wait_ge(hi_ready, n + 1)
                    if n >= RING:
                        dve.wait_ge(unit_used, n - RING + 1)
                else:
                    dve.wait_ge(hi_ready, item * N_FF + (n + 1))
                    dve.wait_ge(unit_used, item * N_FF + (n - RING + 1))
                dve.tensor_tensor(w_lo[:, n % RING, :], raw[:, slot, :], w_hi[:, n % RING, :].bitcast(F32), ALU.subtract).then_inc(lo_ready, 1)

            def norm(j):
                for t in range(TT):
                    m = TT * j + t + 1
                    dve.wait_ge(rooted, m)
                    dve.reciprocal(rstd[:, t:t + 1], rstd[:, t:t + 1]).then_inc(inverted, 1)
                    dve.wait_ge(inverted, m)
                    if t == 0:
                        dve.wait_ge(lnw_ready, 16 * (j + 1))
                    dve.scalar_tensor_tensor(out=h[:, t, :], in0=X[:, t, :], scalar=rstd[:, t:t + 1], in1=lnw[:],
                                             op0=ALU.mult, op1=ALU.mult).then_inc(normed, 1)

            def turned(j):
                for q in range(4):
                    t, g = divmod(q, 2)
                    dst = (slice(None), slice(4 * g, 4 * g + 4), slice(P * t, P * (t + 1)))
                    dve.wait_ge(t_hi_ready, 4 * j + q + 1)
                    dve.tensor_tensor(t_lo[dst], WB[q][:].rearrange("p (k t) -> p k t", k=4), t_hi[dst].bitcast(F32),
                                      ALU.subtract).then_inc(t_lo_ready, 1)

            def after_unit(n):
                dve.wait_ge(unit_used, n + 1)

            def residual(j, n):
                for t in range(TT):
                    if t == 0:
                        dve.wait_ge(tile_done, j + 1)
                    else:
                        after_unit(n)
                    dve.tensor_tensor(X[:, t, :], X[:, t, :], YB[:, 2 * t:2 * t + 2, :].rearrange("p a c -> p (a c)"),
                                      ALU.add).then_inc(added, 1)

            def mixer(l):
                b = BASE[l]

                def conv_input(g):
                    dve.wait_ge(cgate_ready, 2 * l + g + 1)
                    dve.wait_ge(pads_ready, 2 * (l + 1))
                    dve.tensor_tensor(cu[:, 2 * g:2 * g + 2, PAD:], cgate, WB[2 * g][:].rearrange("p (c t) -> p c t", c=2),
                                      ALU.mult).then_inc(cu_ready, 1)

                done = [0]

                def conv(count):
                    for c, w in DVE_CONV[done[0]:done[0] + count]:
                        if w == 0:
                            dve.wait_ge(cu_ready, 2 * l + c // 2 + 1)
                            dve.tensor_scalar(acc[:, c, :], cu[:, c, 0:T], taps[:, l, 0, c:c + 1],
                                              pv[:, l, PV_CB + c:PV_CB + c + 1], ALU.mult, ALU.add).then_inc(conv_step[c], 1)
                        else:
                            dve.wait_ge(conv_step[c], STEPS[c] * l + w)
                            dve.scalar_tensor_tensor(out=acc[:, c, :], in0=cu[:, c, w:w + T], scalar=taps[:, l, w, c:c + 1],
                                                     in1=acc[:, c, :], op0=ALU.mult, op1=ALU.add).then_inc(conv_step[c], 1)
                    done[0] += count

                dve.wait_ge(gr_done, l + 1)
                dve.tensor_copy(gr_t, YB[0:RANK, 3, 0:T]).then_inc(gr_copied, 1)
                lo(b + 3)
                conv_input(0)
                conv(7)
                lo(b + 4)
                conv(8)
                lo(b + 5)
                conv_input(1)
                dve.wait_ge(logit_done, l + 1)
                dve.wait_ge(gate_abs, KT * (l + 1))
                for k in range(KT):
                    ins = dve.tensor_scalar(cum[:, k, :], YB[:, 2, T * k:T * (k + 1)], pv[:, l, PV_BG + k:PV_BG + k + 1], 0.0,
                                            ALU.add, ALU.min)
                ins.then_inc(gate_min, 1)
                conv(7)
                lo(b + 6)
                dve.wait_ge(gate_ln, l + 1)
                dve.wait_ge(gate_min, l + 1)
                dve.tensor_tensor(cum[:], cum[:], Difs[:, 0], ALU.subtract).then_inc(gate_sub, 1)
                dve.wait_ge(gate_sub, l + 1)
                for k in range(KT):
                    for t in range(TT):
                        c = cum[:, k, P * t:P * (t + 1)]
                        ins = dve.tensor_tensor_scan(c, ones[:], c, 0.0, ALU.mult, ALU.add)
                ins.then_inc(cum_ready, 1)
                conv(6)
                lo(b + 7)

                def differences(n):
                    s = LEVELS[n]
                    Dif = Difs[:, n % 2]
                    if n == 0:
                        dve.wait_ge(cum_ready, l + 1)
                    if n >= 2:
                        dve.wait_ge(kE_ready, 8 * l + n - 1)
                        dve.wait_ge(qE_ready, 8 * l + n - 1)
                    if s == P:
                        dve.tensor_tensor(Dif[:, :, 0:P], cum[:, :, P - 1:P].broadcast_to([P, KT, P]), cum[:, :, 0:P],
                                          ALU.subtract).then_inc(dif_ready, 1)
                        return
                    nb = KT * T // (2 * s)
                    blocks = cum[:].rearrange("p k (b s) -> p (k b) s", s=2 * s)
                    dst = Dif.rearrange("p k (b s) -> p (k b) s", s=2 * s)
                    ref = blocks[:, :, s - 1:s].broadcast_to([P, nb, s])
                    dve.tensor_tensor(dst[:, :, 0:s], ref, blocks[:, :, 0:s], ALU.subtract)
                    dve.tensor_tensor(dst[:, :, s:], blocks[:, :, s:], ref, ALU.subtract).then_inc(dif_ready, 1)

                def q_decayed(n):
                    dve.wait_ge(decay_ready, 8 * l + n + 1)
                    if n == 0:
                        dve.wait_ge(qk_ready, 2 * (l + 1))
                    if n >= 2:
                        dve.wait_ge(level_done, 9 * l + n - 1)
                    dve.tensor_tensor(qkE[n % 2][:, 0], qk[:, 0], Difs[:, n % 2], ALU.mult).then_inc(qE_ready, 1)

                def level_read_out(n):
                    dve.wait_ge(level_done, 9 * l + n + 1)
                    if n == 1:
                        dve.wait_ge(pads_ready, 2 * (l + 1))
                    if n > 1:
                        dve.wait_ge(level_read, 2 * (9 * l + n))
                    for r in range(2):
                        bank = YB[:, 2 * (n % 2) + r, :]
                        if n == 0:
                            ins = dve.tensor_copy(attx[:, r].rearrange("p a i -> p (a i)"), bank[:, 0:2 * P])
                        else:
                            ins = dve.copy_predicated(att[:, r], masks[:, n - 1:n, :].broadcast_to([P, 2 * TT, P]),
                                                      bank.rearrange("p (a i) -> p a i", i=P))
                        ins.then_inc(level_read, 1)

                differences(0)
                differences(1)
                conv(30)
                q_decayed(0)
                differences(2)
                lo(b + 8)
                q_decayed(1)
                level_read_out(0)
                differences(3)
                conv(6)
                q_decayed(2)
                level_read_out(1)
                differences(4)
                lo(b + 9)
                conv(4)
                q_decayed(3)
                level_read_out(2)
                differences(5)
                q_decayed(4)
                level_read_out(3)
                conv(len(DVE_CONV))
                differences(6)
                dve.wait_ge(diag_used, sum(PAIRS) * (l + 1))
                dve.wait_ge(conv_step[2], (BY_VECTOR + 1) * l + BY_VECTOR)
                dve.tensor_tensor(acc[:, 2, :], acc[:, 2, :], WB[2][:, T:2 * T], ALU.add).then_inc(conv_step[2], 1)
                q_decayed(5)
                level_read_out(4)
                differences(7)
                lo(b + 10)
                q_decayed(6)
                level_read_out(5)
                dve.wait_ge(c_summed, l + 1)
                dve.scalar_tensor_tensor(out=acc[:], in0=WB[2][:, 0:T].unsqueeze(1).broadcast_to([P, CT, T]), scalar=-1.0 / CH,
                                         in1=acc[:], op0=ALU.mult, op1=ALU.add).then_inc(c_centred, 1)
                q_decayed(7)
                level_read_out(6)
                lo(b + 11)
                dve.wait_ge(c_rooted, l + 1)
                dve.reciprocal(c_rms, c_rms).then_inc(c_inverted, 1)
                level_read_out(7)
                dve.wait_ge(c_inverted, l + 1)
                dve.tensor_tensor(acc[:], acc[:], c_rms.unsqueeze(1).broadcast_to([P, CT, T]), ALU.mult).then_inc(c_scaled, 1)
                level_read_out(8)
                lo(b + 12)
                dve.wait_ge(c_hi, l + 1)
                dve.tensor_tensor(t_lo[:, HEADS:, :], c_sq.rearrange("p (c t) -> p c t", c=CT), t_hi[:, HEADS:, :].bitcast(F32),
                                  ALU.subtract).then_inc(c_lo, 1)
                dve.wait_ge(o_squared, l + 1)
                dve.tensor_reduce(o_ss[:], o_sq.rearrange("p (a c) -> p a c", c=DV), AX, ALU.add).then_inc(o_summed, 1)
                dve.wait_ge(o_rooted, l + 1)
                dve.reciprocal(o_ss[:], o_ss[:]).then_inc(o_inverted, 1)
                dve.wait_ge(o_inverted, l + 1)
                dve.wait_ge(og_ready, 2 * (l + 1))
                for t in range(TT):
                    for hd in range(HEADS):
                        a = HEADS * t + hd
                        gate = og.rearrange("p (g t c) -> p g t c", g=2, t=TT)[:, hd // 2, t, DV * (hd % 2):DV * (hd % 2 + 1)]
                        ins = dve.scalar_tensor_tensor(out=o_sq[:, DV * a:DV * (a + 1)], in0=WB[t][:, DV * hd:DV * (hd + 1)],
                                                       scalar=o_ss[:, a:a + 1], in1=gate, op0=ALU.mult, op1=ALU.mult)
                ins.then_inc(o_gated, 1)
                lo(b + N_IN + 3)
                dve.wait_ge(mix_hi, l + 1)
                dve.scalar_tensor_tensor(out=t_lo[:, 0:HEADS, :].rearrange("p h t -> p (h t)"),
                                         in0=o_banks(2), scalar=pv[:, l, PV_GN:PV_GN + 1],
                                         in1=t_hi[:, 0:HEADS, :].rearrange("p h t -> p (h t)").bitcast(F32),
                                         op0=ALU.mult, op1=ALU.subtract).then_inc(mix_lo, 1)
                lo(b + N_MIX)
                lo(b + N_MIX + 1)
                residual(2 * l, b + N_MIX - 1)

            norm(0)
            turned(0)
            lo(0)
            dve.wait_ge(small_hi, 3)
            for l in range(L):
                dve.tensor_tensor(gr_lo[:, l], gr_raw[:, l], gr_hi[:, l].bitcast(F32), ALU.subtract).then_inc(small_lo, 1)
            dve.tensor_tensor(rt_lo[:], rt_raw[:], rt_hi[:].bitcast(F32), ALU.subtract).then_inc(small_lo, 1)
            lo(1)
            dve.wait_ge(turned_rows, L + 1)
            dve.tensor_copy(taps[:].rearrange("p l w c -> p (l w c)"), YB[:, 0, 0:L * TAPS * CT])
            dve.tensor_copy(pv[:].rearrange("p l c -> p (l c)"), YB[:, 0, L * TAPS * CT:L * (TAPS * CT + NPV)]).then_inc(params_ready, 1)
            lo(2)
            mixer(0)

            d0 = DENSE0
            norm(1)
            turned(1)
            lo(d0 + 2)

            def dense_act(c, n):
                after_unit(n)
                dve.wait_ge(dgate_ready, c + 1)
                if c:
                    dve.wait_ge(dT_lo_ready, c)
                dve.tensor_tensor(dact[:], dg[:], WB[2 + c % 2][:], ALU.mult).then_inc(dact_ready, 1)

            def dense_turn(c):
                dve.wait_ge(dT_hi_ready, c + 1)
                dve.tensor_tensor(dT_lo[:].rearrange("p f t -> p (f t)"), dact[:], dT_hi[:].rearrange("p f t -> p (f t)").bitcast(F32),
                                  ALU.subtract).then_inc(dT_lo_ready, 1)

            up_at = [d0 + 1] + [d0 + 3 * c for c in range(1, CHUNKS)]
            done = 3
            for c in range(CHUNKS):
                while done < min(up_at[c] + 3 - d0, N_FF):
                    lo(d0 + done)
                    done += 1
                dense_act(c, up_at[c])
                dense_turn(c)
            while done < N_FF:
                lo(d0 + done)
                done += 1
            lo(BASE[1])
            lo(BASE[1] + 1)
            residual(1, BASE[1] - 1)
            norm(2)
            turned(2)
            lo(BASE[1] + 2)
            mixer(1)

            norm(3)
            turned(3)
            steps = [0]

            def step(ins):
                steps[0] += 1
                ins.then_inc(route_step, 1)
                dve.wait_ge(route_step, steps[0])

            lg, eq, score, first, l2, second, comb, chosen, place, over, rank = (rout[:, k] for k in range(11))
            lead = rout[:, 12]
            top = rout[:, 13]
            prefer = rout[:, 14]
            wide = (P, TT, NE)

            def each(col):
                return col.broadcast_to(list(wide))

            dve.wait_ge(consts_ready, 4 + EXTRA)
            for e in range(NE):
                ins = dve.memset(prefer[:, :, e:e + 1], float(NE - e))
            step(ins)
            dve.wait_ge(logits_done, 1)
            dve.tensor_copy(lgT[:], YB[0:NE, 3, 0:T]).then_inc(lgT_copied, 1)
            dve.wait_ge(logits_turned, 1)
            step(dve.tensor_copy(lg, YB[:, 0, 0:TT * NE].rearrange("p (t e) -> p t e", t=TT)))

            def largest(values, k, onehot):
                step(dve.tensor_reduce(top[:, :, k], values, AX, ALU.max))
                step(dve.tensor_tensor(eq, values, each(top[:, :, k:k + 1]), ALU.is_equal))
                step(dve.tensor_tensor(score, eq, prefer, ALU.mult))
                step(dve.tensor_reduce(top[:, :, 2 + k], score, AX, ALU.max))
                step(dve.tensor_tensor(onehot, score, each(top[:, :, 2 + k:3 + k]), ALU.is_equal))

            largest(lg, 0, first)
            step(dve.scalar_tensor_tensor(out=l2, in0=first, scalar=NEG, in1=lg, op0=ALU.mult, op1=ALU.add))
            largest(l2, 1, second)
            dve.tensor_tensor(lead[:, :, 0], top[:, :, 1], top[:, :, 0], ALU.subtract).then_inc(lead_ready, 1)
            dve.tensor_tensor(chosen, first, second, ALU.add).then_inc(choice_ready, 1)
            dve.wait_ge(lead_exp, 1)
            step(dve.tensor_scalar(lead[:, :, 2], lead[:, :, 1], 1.0, None, ALU.add))
            step(dve.reciprocal(lead[:, :, 3], lead[:, :, 2]))
            step(dve.tensor_tensor(lead[:, :, 4], lead[:, :, 3], lead[:, :, 1], ALU.mult))
            step(dve.tensor_tensor(first, first, each(lead[:, :, 3:4]), ALU.mult))
            step(dve.tensor_tensor(second, second, each(lead[:, :, 4:5]), ALU.mult))
            step(dve.tensor_tensor(comb, first, second, ALU.add))
            dve.wait_ge(places_done, 1)
            step(dve.scalar_tensor_tensor(out=place, in0=YB[:, 1, 0:TT * NE].rearrange("p (t e) -> p t e", t=TT), scalar=1.0,
                                          in1=chosen, op0=ALU.add, op1=ALU.mult))
            step(dve.tensor_scalar(place, place, -1.0, None, ALU.add))
            def select(item, count):
                dve.tensor_copy(cur[:, 0, :], slot_of[:, bass.ds(item, 1), :].rearrange("p o t -> p (o t)"))
                dve.tensor_copy(cur[:, 1, :], gate_of[:, bass.ds(item, 1), :].rearrange("p o t -> p (o t)")).then_inc(cur_ready, 1)
                dve.wait_ge(cur_ready, count)
                for t in range(TT):
                    ins = dve.tensor_scalar(sel[:, t, :], slot_no[:], cur[:, 0, t:t + 1], None, ALU.is_equal)
                ins.then_inc(sel_ready, 1)

            for t in range(TT):
                ins = dve.tensor_scalar(sel[:, t, :], slot_no[:], place[:, t, 0:1], None, ALU.is_equal)
            ins.then_inc(sel_ready, 1)
            dve.tensor_copy(cur[:, 0, :], place[:, :, 0])
            dve.tensor_copy(cur[:, 1, :], comb[:, :, 0]).then_inc(cur_ready, 1)
            step(dve.tensor_copy(slot_of[:, 0:NE, :].rearrange("p e t -> p t e"), place))
            step(dve.tensor_copy(gate_of[:, 0:NE, :].rearrange("p e t -> p t e"), comb))
            dve.wait_ge(counts_done, 1)
            step(dve.tensor_scalar(over[:, 0, :], YB[:, 3, 0:NE], float(P), None, ALU.is_gt))
            step(dve.tensor_tensor_scan(rank[:, 0, :], ones[:, 0:NE], over[:, 0, :], 0.0, ALU.mult, ALU.add))
            shape3 = [P, EXTRA, NE]
            pick = rout[:, 15:17].rearrange("p a t e -> p (a t) e")[:, 0:EXTRA, :]
            prod = rout[:, 17:20].rearrange("p k t e -> p t k e")
            step(dve.tensor_tensor(pick, rank[:, 0:1, :].broadcast_to(shape3), number[:], ALU.is_equal))
            step(dve.tensor_tensor(pick, pick, over[:, 0:1, :].broadcast_to(shape3), ALU.mult))
            for table, values in ((slot_of, place), (gate_of, comb)):
                for t in range(TT):
                    ins = dve.tensor_tensor(prod[:, t], values[:, t:t + 1, :].broadcast_to(shape3), pick, ALU.mult)
                step(ins)
                step(dve.tensor_reduce(table[:, NE:NE + EXTRA, :].rearrange("p k t -> p t k"), prod, AX, ALU.add))
            step(dve.tensor_scalar(slot_of[:, NE:NE + EXTRA, :], slot_of[:, NE:NE + EXTRA, :], -float(P), None, ALU.add))
            step(dve.tensor_tensor(prod[:, 0], prefer[:, 0:1, :].broadcast_to(shape3), pick, ALU.mult))
            step(dve.tensor_reduce(top[:, 0, 4:4 + EXTRA], prod[:, 0], AX, ALU.add))
            step(dve.tensor_scalar(top[:, 0, 4:4 + EXTRA], top[:, 0, 4:4 + EXTRA], -1.0, float(NE), ALU.mult, ALU.add))
            step(dve.tensor_scalar(meta[:, 1:1 + EXTRA], top[:, 0, 4:4 + EXTRA], float(NE - 1), None, ALU.min))
            dve.tensor_scalar(meta[:, 0:1], rank[:, 0:1, NE - 1], float(NE), None, ALU.add).then_inc(meta_ready, 1)
            dve.wait_ge(meta_ready, 1)
            n_items = dve.value_load(meta[0:1, 0:1], min_val=NE, max_val=ITEMS)
            dve.memset(slot_gate[:], 0.0)
            dve.memset(selT[:].bitcast(F32), 0.0)
            dve.memset(YB[:, 0:2, :], 0.0).then_inc(y_zeroed, 1)

            def y_part(count):
                dve.wait_ge(y_hi_ready, count)
                dve.scalar_tensor_tensor(out=y_lo, in0=YB[:, 0:2, :].rearrange("p a c -> p (a c)"), scalar=slot_gate[:],
                                         in1=y_hi.bitcast(F32), op0=ALU.mult, op1=ALU.subtract).then_inc(y_lo_ready, 1)

            def xs_part(count):
                dve.wait_ge(xs_hi_ready, count)
                dve.tensor_tensor(xs_lo, stage[:], xs_hi.bitcast(F32), ALU.subtract).then_inc(xs_lo_ready, 1)

            def add_quad(r, count):
                t, half = divmod(r, 2)
                dve.wait_ge(scattered, count)
                dve.wait_ge(quad_added, count)
                dst = X[:, t, HALF * half:HALF * (half + 1)]
                dve.tensor_tensor(dst, dst, YB[:, 2, :], ALU.add).then_inc(quad_added, 1)

            xs_part(1)
            dve.memset(started[:, 0:1], 0.0).then_inc(eact_ready, 1)
            dve.memset(started[:, 1:2], 0.0).then_inc(quad_added, 1)
            dve.wait_ge(y_zeroed, 1)
            with dve.Fori(0, n_items) as i:
                for u in range(N_FF):
                    if u >= 2:
                        lo(MOE0 + u, i)
                    if u == 2:
                        y_part(i + 1)
                    for r in range(4):
                        if SCATTER[r] + 2 == u:
                            add_quad(r, i * 4 + (r + 1))
                    for c in range(EC):
                        if TURN[c] + 2 == u:
                            dve.wait_ge(eT_hi_ready, i * EC + (c + 1))
                            w = 4 if c < EC - 1 else 2
                            dve.tensor_tensor(eT_lo[:, 0:w, :], YB[:, 3, 0:P * w].rearrange("p (f t) -> p f t", f=w),
                                              eT_hi[:, 0:w, :].bitcast(F32), ALU.subtract).then_inc(eT_lo_ready, 1)
                        if UP_END[c] + 2 == u:
                            dve.wait_ge(egate_ready, i * EC + (c + 1))
                            dve.wait_ge(unit_used, i * N_FF + (MOE0 + UP_END[c] + 1))
                            w = 512 if c < EC - 1 else 256
                            dve.tensor_tensor(eact[:, 0:w], eg[:, 0:w], WB[2 + c % 2][:, 0:w], ALU.mult).then_inc(eact_ready, 1)
                    if TURN_SEL + 2 == u:
                        dve.wait_ge(selT_done, i + 1)
                        dve.tensor_copy(selT[:].rearrange("p t j -> p (t j)"), YB[:, 2, 0:TT * P])
                        dve.tensor_copy(slot_gate[:], YB[:, 2, TT * P:TT * P + 1]).then_inc(selT_ready, 1)
                        select(i + 1, i + 2)
                    if LAST_UP + 2 == u:
                        xs_part(i + 2)
                with dve.If(i < n_items - 1):
                    for u in range(2):
                        lo(MOE0 + N_FF + u, i)
            y_part(n_items + 1)
            for r in range(4):
                add_quad(r, n_items * 4 + (r + 1))
            norm(4)

        @block.tensor
        def _(pe):
            def unit(n, item=None):
                if item is None:
                    pe.wait_ge(hi_ready, n + 1)
                    pe.wait_ge(lo_ready, n + 1)
                else:
                    pe.wait_ge(hi_ready, item * N_FF + (n + 1))
                    pe.wait_ge(lo_ready, item * N_FF + (n + 1))
                return w_hi[:, n % RING, :], w_lo[:, n % RING, :]

            def channels_unit(n, bank, a_hi, a_lo):
                hi, lo = (w.rearrange("p (k c) -> p k c", k=KD) for w in unit(n))
                for f in range(2):
                    dst = bank[:, T * f:T * (f + 1)]
                    for k in range(KD):
                        cols = slice(P * f, P * (f + 1))
                        pe.matmul(dst, lo[:, k, cols], a_hi[:, k, :], start=(k == 0), stop=False)
                        pe.matmul(dst, hi[:, k, cols], a_hi[:, k, :], start=False, stop=False)
                        ins = pe.matmul(dst, hi[:, k, cols], a_lo[:, k, :], start=False, stop=(k == KD - 1))
                ins.then_inc(unit_used, 1)

            def tokens_unit(n, bank, a_hi, a_lo):
                hi, lo = (w.rearrange("p (k c) -> p k c", k=KD) for w in unit(n))
                for t in range(TT):
                    dst = bank[:, 256 * t:256 * (t + 1)]
                    for k in range(KD):
                        tok = slice(P * t, P * (t + 1))
                        pe.matmul(dst, a_hi[:, k, tok], hi[:, k, :], start=(k == 0), stop=False)
                        pe.matmul(dst, a_hi[:, k, tok], lo[:, k, :], start=False, stop=False)
                        ins = pe.matmul(dst, a_lo[:, k, tok], hi[:, k, :], start=False, stop=(k == KD - 1))
                ins.then_inc(unit_used, 1)

            def narrow(dst, small_hi_part, small_lo_part):
                for k in range(KD):
                    pe.matmul(dst, small_lo_part[:, k, :], t_hi[:, k, :], start=(k == 0), stop=False)
                    pe.matmul(dst, small_hi_part[:, k, :], t_hi[:, k, :], start=False, stop=False)
                    ins = pe.matmul(dst, small_hi_part[:, k, :], t_lo[:, k, :], start=False, stop=(k == KD - 1))
                return ins

            def down_unit(n, a_hi, a_lo, k0, first, last):
                hi, lo = (w.rearrange("p (k c) -> p k c", k=2) for w in unit(n))
                for k, t in [(k, t) for t in range(TT) for k in range(2)] if last else [(k, t) for k in range(2) for t in range(TT)]:
                        tok = slice(P * t, P * (t + 1))
                        for a, w, s, e in ((a_hi, hi, True, False), (a_hi, lo, False, False), (a_lo, hi, False, True)):
                            for half in range(2):
                                ins = pe.matmul(YB[:, 2 * t + half, :], a[:, k0 + k, tok], w[:, k, HALF * half:HALF * (half + 1)],
                                                start=(first and k == 0 and s), stop=(last and k == 1 and e))
                        if last and k == 1 and t == 0:
                            ins.then_inc(tile_done, 1)
                ins.then_inc(unit_used, 1)

            def turn_h(j):
                for q in range(4):
                    t, g = divmod(q, 2)
                    if g == 0:
                        pe.wait_ge(normed, TT * j + t + 1)
                    for k in range(4):
                        ins = pe.transpose(WB[q][:, P * k:P * (k + 1)], h[:, t, P * (4 * g + k):P * (4 * g + k + 1)], ident[:])
                    ins.then_inc(h_turned, 1)
                pe.wait_ge(t_hi_ready, 4 * (j + 1))
                pe.wait_ge(t_lo_ready, 4 * (j + 1))

            def mixer(l):
                b = BASE[l]
                turn_h(2 * l)
                channels_unit(b + 0, WB[0], t_hi, t_lo)
                if l == 0:
                    pe.wait_ge(small_hi, 3)
                    pe.wait_ge(small_lo, 3)
                narrow(YB[0:RANK, 3, 0:T], gr_hi[:, l], gr_lo[:, l]).then_inc(gr_done, 1)
                if l == 0:
                    turn_params()
                channels_unit(b + 1, WB[1], t_hi, t_lo)
                pe.wait_ge(gr_copied, l + 1)
                for k in range(KT):
                    ins = pe.matmul(YB[:, 2, T * k:T * (k + 1)], wgu[:, l, P * k:P * (k + 1)], gr_t, start=True, stop=True)
                ins.then_inc(logit_done, 1)
                channels_unit(b + 2, WB[2], t_hi, t_lo)
                channels_unit(b + 3, WB[3], t_hi, t_lo)
                pe.wait_ge(cu_ready, 2 * l + 1)
                channels_unit(b + U_Q, WB[0], t_hi, t_lo)
                pe.wait_ge(cu_ready, 2 * l + 2)

                def conv(c, r):
                    bank = YB[:, 3, T:2 * T] if c == 3 else WB[2][:, T:2 * T]
                    w0 = 0 if c == 3 else BY_VECTOR
                    for w in range(w0 + PE_TAPS * r, min(w0 + PE_TAPS * (r + 1), TAPS)):
                        m, k = (3 - c) * PAIRS[0] + (w - w0) // 2, (w - w0) % 2
                        if k == 0:
                            pe.wait_ge(diag_ready, sum(PAIRS) * l + m + 1)
                        ins = pe.matmul(bank, diag[:, m % 2, k, :], cu[:, c, w:w + T], start=(w == w0), stop=(w == TAPS - 1))
                        if k or w == TAPS - 1:
                            ins.then_inc(diag_used, 1)

                conv(3, 0)
                channels_unit(b + U_K, WB[1], t_hi, t_lo)
                conv(3, 1)
                tokens_unit(b + U_V, WB[2], t_hi, t_lo)
                conv(3, 2)

                def level(n):
                    if n < 8:
                        pe.wait_ge(qE_ready, 8 * l + n + 1)
                        pe.wait_ge(kE_ready, 8 * l + n + 1)
                        src = qkE[n % 2]
                    else:
                        src = qk
                    if n == 0:
                        pe.wait_ge(gate_min, l + 1)
                    if n == 1:
                        pe.wait_ge(conv_step[3], l + 1)
                    if n >= 2:
                        pe.wait_ge(level_read, 2 * (9 * l + n - 1))
                    for r in range(2):
                        rows = slice(DK * r, DK * (r + 1))
                        bank = YB[:, 2 * (n % 2) + r, :]
                        if n == 0:
                            pairs = [(hp, hp, slice(0, P), slice(P, T)) for hp in range(2)]
                        else:
                            pairs = [(2 * t + hp, hp, slice(P * t, P * (t + 1)), slice(P * t, P * (t + 1))) for t in range(TT) for hp in range(2)]
                        for place, hp, js, is_ in pairs:
                            ins = pe.matmul(bank[:, P * place:P * (place + 1)], src[rows, 1, hp, js], src[rows, 0, hp, is_],
                                            start=True, stop=True)
                    ins.then_inc(level_done, 1)

                level(0)
                tokens_unit(b + U_V + 1, WB[3], t_hi, t_lo)
                level(1)
                level(2)
                pe.wait_ge(qk_ready, 2 * (l + 1))
                tokens_unit(b + U_G, WB[0], t_hi, t_lo)
                level(3)
                pe.wait_ge(v_ready, 2 * l + 1)
                conv(2, 0)
                level(4)
                tokens_unit(b + U_G + 1, WB[1], t_hi, t_lo)
                for n in range(5, 9):
                    level(n)
                    if n == 5:
                        pe.wait_ge(v_ready, 2 * (l + 1))
                        for c in range(CT):
                            pe.wait_ge(conv_step[c], STEPS[c] * (l + 1))
                        for c in range(CT):
                            ins = pe.matmul(WB[2][:, 0:T], ones[:], acc[:, c, :], start=(c == 0), stop=(c == CT - 1))
                        ins.then_inc(c_summed, 1)
                    if n == 6:
                        pe.wait_ge(c_squared, l + 1)
                        for c in range(CT):
                            ins = pe.matmul(WB[3][:, 0:T], ones[:], c_sq[:, T * c:T * (c + 1)], start=(c == 0), stop=(c == CT - 1))
                        ins.then_inc(c_varied, 1)
                pe.wait_ge(level_read, 2 * 9 * (l + 1))
                pe.wait_ge(og_ready, 2 * (l + 1))
                for hd in range(HEADS):
                    hp, r = divmod(hd, 2)
                    vs = slice(DV * hd, DV * (hd + 1))
                    pe.matmul(WB[0][:, vs], att[:, r, hp, :], v[:, 0, vs], start=True, stop=True)
                    pe.matmul(WB[1][:, vs], attx[:, r, hp, :], v[:, 0, vs], start=True, stop=False)
                    ins = pe.matmul(WB[1][:, vs], att[:, r, 2 + hp, :], v[:, 1, vs], start=False, stop=True)
                ins.then_inc(o_done, 1)
                pe.wait_ge(c_hi, l + 1)
                pe.wait_ge(c_lo, l + 1)
                down_unit(b + N_IN, t_hi, t_lo, HEADS, True, False)
                pe.wait_ge(o_gated, l + 1)
                for hd in range(HEADS):
                    for t in range(TT):
                        a = HEADS * t + hd
                        c0 = T * (hd % 2) + P * t
                        ins = pe.transpose(WB[2 + hd // 2][:, c0:c0 + P], o_sq[:, DV * a:DV * (a + 1)], ident[:])
                ins.then_inc(o_turned, 1)
                down_unit(b + N_IN + 1, t_hi, t_lo, HEADS + 2, False, False)
                pe.wait_ge(mix_hi, l + 1)
                pe.wait_ge(mix_lo, l + 1)
                for j in range(HEADS // 2):
                    down_unit(b + N_IN + CT // 2 + j, t_hi, t_lo, 2 * j, False, j == HEADS // 2 - 1)

            def turn_params():
                pe.wait_ge(rows_ready, 16 * 6 * L)
                for l in range(L):
                    n = TAPS * CT
                    pe.transpose(YB[:, 0, n * l:n * (l + 1)], tap_rows[0:n, l, :], ident[0:n, 0:n]).then_inc(turned_rows, 1)
                pe.transpose(YB[:, 0, L * n:L * (n + NPV)], pv_rows[0:L * NPV, :], ident[0:L * NPV, 0:L * NPV]).then_inc(turned_rows, 1)

            pe.wait_ge(pool_step, 2)
            mixer(0)

            turn_h(1)
            n = DENSE0
            for c in range(CHUNKS + 1):
                if c < CHUNKS:
                    if c >= 2:
                        pe.wait_ge(dact_ready, c - 1)
                    channels_unit(n, WB[c % 2], t_hi, t_lo)
                    channels_unit(n + 1, WB[2 + c % 2], t_hi, t_lo)
                    n += 2
                if c:
                    if c == 1:
                        pe.wait_ge(added, TT)
                    pe.wait_ge(dT_hi_ready, c)
                    pe.wait_ge(dT_lo_ready, c)
                    down_unit(n, dT_hi, dT_lo, 0, c == 1, c == CHUNKS)
                    n += 1
            mixer(1)

            turn_h(3)
            narrow(YB[0:NE, 3, 0:T], rt_hi, rt_lo).then_inc(logits_done, 1)
            pe.wait_ge(lgT_copied, 1)
            for t in range(TT):
                ins = pe.transpose(YB[:, 0, NE * t:NE * (t + 1)], lgT[:, P * t:P * (t + 1)], ident[0:NE, 0:NE])
            ins.then_inc(logits_turned, 1)
            pe.wait_ge(choice_ready, 1)
            ch = rout[:, 7]
            pe.matmul(YB[:, 1, 0:NE], before[:], ch[:, 0, :], start=True, stop=True)
            pe.matmul(YB[:, 1, NE:2 * NE], ones[:], ch[:, 0, :], start=True, stop=False)
            pe.matmul(YB[:, 1, NE:2 * NE], before[:], ch[:, 1, :], start=False, stop=True).then_inc(places_done, 1)
            pe.matmul(YB[:, 3, 0:NE], ones[:], ch[:, 0, :], start=True, stop=False)
            pe.matmul(YB[:, 3, 0:NE], ones[:], ch[:, 1, :], start=False, stop=True).then_inc(counts_done, 1)

            def gather(g):
                for k in range(4):
                    cs = slice(P * (4 * g + k), P * (4 * g + k + 1))
                    for t in range(TT):
                        ins = pe.matmul(YB[:, 2, P * k:P * (k + 1)], h[:, t, cs], sel[:, t, :], start=(t == 0), stop=(t == TT - 1))
                ins.then_inc(gathered, 1)

            def scatter(r):
                t, half = divmod(r, 2)
                cs = slice(HALF * half, HALF * (half + 1))
                pe.matmul(YB[:, 2, :], selT[:, t, :], y_hi[:, cs], start=True, stop=False)
                pe.matmul(YB[:, 2, :], selT[:, t, :], y_lo[:, cs], start=False, stop=True).then_inc(scattered, 1)

            pe.wait_ge(sel_ready, 1)
            gather(0)
            pe.wait_ge(staged, 1)
            gather(1)
            pe.wait_ge(meta_ready, 1)
            n_items = pe.value_load(meta[0:1, 0:1], min_val=NE, max_val=ITEMS)
            with pe.Fori(0, n_items) as i:
                pe.wait_ge(xs_hi_ready, i + 1)
                pe.wait_ge(xs_lo_ready, i + 1)
                for u, (what, c, part) in enumerate(plan):
                    hi, lo = unit(MOE0 + u, i)
                    if what != "down":
                        width, nk = (512, 4) if c < EC - 1 else (256, 8)
                        k0 = 4 * part
                        hi, lo = (w.rearrange("p (k c) -> p k c", k=nk) for w in (hi, lo))
                        bank = WB[(0 if what == "gate" else 2) + c % 2][:, 0:width]
                        for k in range(nk):
                            start, stop = k0 + k == 0, k0 + k == KD - 1
                            pe.matmul(bank, xs_hi[:, k0 + k, :], hi[:, k, :], start=start, stop=False)
                            pe.matmul(bank, xs_hi[:, k0 + k, :], lo[:, k, :], start=False, stop=False)
                            ins = pe.matmul(bank, xs_lo[:, k0 + k, :], hi[:, k, :], start=False, stop=stop)
                    else:
                        if part == 0:
                            pe.wait_ge(eT_hi_ready, i * EC + (c + 1))
                            pe.wait_ge(eT_lo_ready, i * EC + (c + 1))
                        hi, lo = (w.rearrange("p (k c) -> p k c", k=2) for w in (hi, lo))
                        for k in range(2):
                            f = 2 * part + k
                            first, last = c == 0 and f == 0, c == EC - 1 and k == 1
                            for a, w, s, e in ((eT_hi, hi, True, False), (eT_hi, lo, False, False), (eT_lo, hi, False, True)):
                                for half in range(2):
                                    ins = pe.matmul(YB[:, half, :], a[:, f, :], w[:, k, HALF * half:HALF * (half + 1)],
                                                    start=(first and s), stop=(last and e))
                    ins.then_inc(unit_used, 1)
                    if u in SCATTER:
                        r = SCATTER.index(u)
                        if r == 0:
                            pe.wait_ge(y_hi_ready, i + 1)
                            pe.wait_ge(y_lo_ready, i + 1)
                            pe.wait_ge(staged, i * 2 + 2)
                        else:
                            pe.wait_ge(quad_added, i * 4 + (r + 1))
                        scatter(r)
                    if u in TURN:
                        tc = TURN.index(u)
                        pe.wait_ge(eact_ready, i * EC + (tc + 2))
                        for f in range(4 if tc < EC - 1 else 2):
                            ins = pe.transpose(YB[:, 3, P * f:P * (f + 1)], eact[:, P * f:P * (f + 1)], ident[:])
                        ins.then_inc(eT_done, 1)
                    if u == TURN_SEL:
                        pe.wait_ge(quad_added, i * 4 + 5)
                        for t in range(TT):
                            pe.transpose(YB[:, 2, P * t:P * (t + 1)], sel[:, t, :], ident[:])
                        for t in range(TT):
                            ins = pe.matmul(YB[:, 2, TT * P:TT * P + 1], sel[:, t, :], cur[:, 1, t:t + 1],
                                            start=(t == 0), stop=(t == TT - 1))
                        ins.then_inc(selT_done, 1)
                    if u in GATHER:
                        g = GATHER.index(u)
                        if g == 0:
                            pe.wait_ge(selT_ready, i + 1)
                            pe.wait_ge(sel_ready, i + 2)
                        else:
                            pe.wait_ge(staged, i * 2 + 3)
                        gather(g)
            pe.wait_ge(y_hi_ready, n_items + 1)
            pe.wait_ge(y_lo_ready, n_items + 1)
            pe.wait_ge(staged, n_items * 2 + 2)
            for r in range(4):
                if r:
                    pe.wait_ge(quad_added, n_items * 4 + (r + 1))
                scatter(r)


_INS = ['x', 'ln1_w', 'w_in', 'w_gate_up', 'b_gate', 'gla_norm_w', 'conv_w', 'conv_b', 'cn_w', 'cn_b', 'w_out',
        'ln2_w', 'wd_gate', 'wd_up', 'wd_down', 'w_router', 'we_gate', 'we_up', 'we_down', 'final_norm_w']


def kernel(**inputs):
    import numpy as np
    import concourse.bacc as bacc
    from concourse.bass_utils import run_bass_kernel_spmd

    nc = bacc.Bacc("TRN2", target_bir_lowering=False, num_devices=1)
    arrays, args = {}, []
    for name in _INS:
        a = np.ascontiguousarray(inputs[name])
        arrays[f"in_{name}"] = a
        args.append(nc.dram_tensor(f"in_{name}", a.shape, mybir.dt.from_np(a.dtype), kind="ExternalInput").ap())
    out = nc.dram_tensor("out", inputs["x"].shape, F32, kind="ExternalOutput").ap()
    trunk(nc, *args, out)
    r = run_bass_kernel_spmd(nc, [arrays], core_ids=[0])
    return r.results[0]["out"]
```
